# Optimizing a Trainium2 kernel written in Bass

```python
import jax
import jax.numpy as jnp
from jax import lax
import numpy as np
import math

D_MODEL = 1024
BATCH = 1
SEQ = 256
DEPTH = 1

GRID_W = 64
CTX_LEN = 256
D_MIX = D_MODEL
HEAD_DIM = 64
RW_W = D_MIX // 4
RW_H = RW_W // HEAD_DIM
RW_DH = HEAD_DIM
RW_LW = 64
RW_LA = 64
RW_LG = 128
NA_W = D_MIX // 2
NA_H = NA_W // HEAD_DIM
NA_KR = 8
NA_KC = 16
SC_W = D_MIX - RW_W - NA_W
SC_K = 3
PEER_H = 8
PEER_NKEYS = 128
PEER_N = PEER_NKEYS * PEER_NKEYS
PEER_DQ = 256
PEER_TOPK = 16
PEER_CHUNK = 128

NORM_EPS = 1e-6
GN_EPS = 64e-5
NEG_INF = -1e30
IN_SPLITS = (RW_W, RW_W, RW_W, 2 * RW_LW, 2 * RW_LA, RW_LG, NA_W, NA_W, NA_W, SC_W, SC_W, SC_W)
D_IN = sum(IN_SPLITS)


def rmsnorm(x, g):
    xf = x.astype(jnp.float32)
    y = xf * lax.rsqrt(jnp.mean(xf * xf, axis=-1, keepdims=True) + NORM_EPS)
    return (y * g.astype(jnp.float32)).astype(x.dtype)

def split_columns(z):
    offsets = [int(o) for o in np.cumsum(IN_SPLITS)[:-1]]
    return jnp.split(z, offsets, axis=-1)

def short_conv3(u, w):
    up = jnp.pad(u, ((0, 0), (1, 1), (0, 0)))
    return up[:, :-2] * w[0] + up[:, 1:-1] * w[1] + up[:, 2:] * w[2]

def gated_short_conv(z_b, z_c, z_x, w):
    return z_b * short_conv3(z_c * z_x, w)

def rwkv_prepare(z_r, z_k, z_v, z_w, z_a, w0, w_up, a0, a_up, k_k, k_a):
    f32 = jnp.float32
    B, T, _ = z_r.shape
    r, k, v = z_r.astype(f32), z_k.astype(f32), z_v.astype(f32)
    lw = jnp.tanh(z_w.astype(f32).reshape(B, T, 2, RW_LW))
    la = z_a.astype(f32).reshape(B, T, 2, RW_LA)
    w_raw = w0 + jnp.einsum('btdr,drc->btdc', lw, w_up)
    decay = jnp.exp(-jnp.exp(-jax.nn.softplus(-w_raw) - 0.5))
    a = jax.nn.sigmoid(a0 + jnp.einsum('btdr,drc->btdc', la, a_up))
    kk = (k * k_k).reshape(B, T, RW_H, RW_DH)
    kk = (kk * lax.rsqrt(jnp.sum(kk * kk, axis=-1, keepdims=True) + 1e-12)).reshape(B, T, RW_W)
    k_dir = k[:, :, None, :] * (1.0 + (a - 1.0) * k_a)
    b_dir = kk[:, :, None, :] * a
    tm = lambda t: jnp.moveaxis(t.reshape(B, T, RW_H, RW_DH), 1, 0)
    common = (tm(r), tm(kk), tm(v))
    per_dir = tuple((tm(decay[:, :, d]), tm(b_dir[:, :, d]), tm(k_dir[:, :, d])) for d in range(2))
    return common, per_dir

def wkv_scan(state0, r, kk, v, decay, b, k, reverse):
    def step(S, inp):
        r_t, kk_t, v_t, w_t, b_t, k_t = inp
        sa = jnp.einsum('bhij,bhj->bhi', S, kk_t)
        S = S * w_t[:, :, None, :] - sa[..., None] * b_t[:, :, None, :] + v_t[..., None] * k_t[:, :, None, :]
        return S, jnp.einsum('bhij,bhj->bhi', S, r_t)
    return lax.scan(step, state0, (r, kk, v, decay, b, k), reverse=reverse)

def rwkv_output(y_tm, z_r, z_k, z_v, z_g, g_up, r_k, lnx_g):
    f32 = jnp.float32
    B, T, _ = z_r.shape
    y = jnp.moveaxis(y_tm, 0, 1)
    mu = jnp.mean(y, axis=-1, keepdims=True)
    var = jnp.mean(jnp.square(y - mu), axis=-1, keepdims=True)
    y = (y - mu) * lax.rsqrt(var + GN_EPS) * lnx_g.astype(f32).reshape(RW_H, RW_DH)
    hd = lambda t: t.astype(f32).reshape(B, T, RW_H, RW_DH)
    r, k, v = hd(z_r), hd(z_k), hd(z_v)
    y = y + jnp.sum(r * k * r_k, axis=-1, keepdims=True) * v
    gate = jax.nn.sigmoid(z_g.astype(f32)) @ g_up.astype(f32)
    return (y.reshape(B, T, RW_W) * gate).astype(z_r.dtype)

def rwkv_mixer(pc, pl, w0, w_up, a0, a_up, g_up, k_k, k_a, r_k, lnx_g, need_ctx):
    c_common, c_dirs = rwkv_prepare(*pc[:5], w0, w_up, a0, a_up, k_k, k_a)
    l_common, l_dirs = rwkv_prepare(*pl[:5], w0, w_up, a0, a_up, k_k, k_a)
    state0 = jnp.zeros((pl[0].shape[0], RW_H, RW_DH, RW_DH), jnp.float32)
    ys_c, ys_l = [], []
    for d, reverse in enumerate((False, True)):
        ctx_state, y_c = wkv_scan(state0, *c_common, *c_dirs[d], reverse=reverse)
        _, y_l = wkv_scan(ctx_state, *l_common, *l_dirs[d], reverse=reverse)
        ys_c.append(y_c)
        ys_l.append(y_l)
    out_l = rwkv_output(ys_l[0] + ys_l[1], pl[0], pl[1], pl[2], pl[5], g_up, r_k, lnx_g)
    out_c = rwkv_output(ys_c[0] + ys_c[1], pc[0], pc[1], pc[2], pc[5], g_up, r_k, lnx_g) if need_ctx else None
    return out_c, out_l

def neighbourhood_attention(ql, kl, vl, kc, vc, rpb):
    f32 = jnp.float32
    B, S = ql.shape[:2]
    rows = S // GRID_W
    kr = min(NA_KR, rows)
    scale = HEAD_DIM ** -0.5
    grid = lambda t: t.reshape(B, rows, GRID_W, NA_H, HEAD_DIM)
    qg = grid(ql).astype(f32) * scale
    kg, vg = grid(kl).astype(f32), grid(vl)
    ri = jnp.arange(rows)
    row_idx = jnp.clip(ri - kr // 2, 0, rows - kr)[:, None] + jnp.arange(kr)[None, :]
    ci = jnp.arange(GRID_W)
    c0 = jnp.clip(ci - NA_KC // 2, 0, GRID_W - NA_KC)
    col_ok = (ci[None, :] >= c0[:, None]) & (ci[None, :] < c0[:, None] + NA_KC)
    dr = row_idx - ri[:, None] + (NA_KR - 1)
    dc = jnp.clip(ci[None, :] - ci[:, None] + (NA_KC - 1), 0, 2 * NA_KC - 2)
    bias = rpb[:, dr[:, None, :, None], dc[None, :, None, :]].astype(f32)
    k_band = kg[:, row_idx]
    v_band = vg[:, row_idx]
    s_win = jnp.einsum('brqhd,brkwhd->bhrqkw', qg, k_band) + bias[None]
    s_win = jnp.where(col_ok[:, None, :], s_win, NEG_INF)
    s_ctx = jnp.einsum('brqhd,bnhd->bhrqn', qg, kc.astype(f32))
    n_win = kr * GRID_W
    s = jnp.concatenate([s_win.reshape(B, NA_H, rows, GRID_W, n_win), s_ctx], axis=-1)
    p = jax.nn.softmax(s, axis=-1)
    p_win = p[..., :n_win].reshape(B, NA_H, rows, GRID_W, kr, GRID_W).astype(vl.dtype)
    p_ctx = p[..., n_win:].astype(vl.dtype)
    out = jnp.einsum('bhrqkw,brkwhd->brqhd', p_win, v_band) + jnp.einsum('bhrqn,bnhd->brqhd', p_ctx, vc)
    return out.reshape(B, S, NA_W)

def context_attention(qc, kc, vc):
    f32 = jnp.float32
    B, C = qc.shape[:2]
    s = jnp.einsum('bqhd,bkhd->bhqk', qc.astype(f32), kc.astype(f32)) * (HEAD_DIM ** -0.5)
    p = jax.nn.softmax(s, axis=-1).astype(vc.dtype)
    return jnp.einsum('bhqk,bkhd->bqhd', p, vc).reshape(B, C, NA_W)

def token_mixing(hc, hl, w_in, w_out, rw_w0, rw_w_up, rw_a0, rw_a_up, rw_g_up, rw_k_k, rw_k_a,
                 rw_r_k, rw_lnx_g, na_rpb, sc_conv_w, need_ctx):
    B, S = hl.shape[:2]
    C = hc.shape[1]
    pc = split_columns(hc @ w_in)
    pl = split_columns(hl @ w_in)
    y_rw_c, y_rw_l = rwkv_mixer(pc, pl, rw_w0, rw_w_up, rw_a0, rw_a_up, rw_g_up, rw_k_k, rw_k_a,
                                rw_r_k, rw_lnx_g, need_ctx)
    qc, kc, vc = (t.reshape(B, C, NA_H, HEAD_DIM) for t in pc[6:9])
    ql, kl, vl = (t.reshape(B, S, NA_H, HEAD_DIM) for t in pl[6:9])
    y_na_l = neighbourhood_attention(ql, kl, vl, kc, vc, na_rpb)
    y_sc_l = gated_short_conv(*pl[9:12], sc_conv_w)
    yl = jnp.concatenate([y_rw_l, y_na_l, y_sc_l], axis=-1) @ w_out
    if not need_ctx:
        return None, yl
    y_na_c = context_attention(qc, kc, vc)
    y_sc_c = gated_short_conv(*pc[9:12], sc_conv_w)
    yc = jnp.concatenate([y_rw_c, y_na_c, y_sc_c], axis=-1) @ w_out
    return yc, yl

def peer_ffn(h, q_w, sub_keys, u_tab, v_tab):
    f32 = jnp.float32
    lead = h.shape[:-1]
    t = h.reshape(-1, D_MODEL)
    n = t.shape[0]
    q = (t @ q_w).reshape(n, PEER_H, 2, PEER_DQ // 2)
    s = jnp.einsum('thpd,hpnd->thpn', q.astype(f32), sub_keys.astype(f32))
    s1, i1 = lax.top_k(s[:, :, 0], PEER_TOPK)
    s2, i2 = lax.top_k(s[:, :, 1], PEER_TOPK)
    cand_s = (s1[..., :, None] + s2[..., None, :]).reshape(n, PEER_H, PEER_TOPK * PEER_TOPK)
    cand_i = (i1[..., :, None] * PEER_NKEYS + i2[..., None, :]).reshape(n, PEER_H, PEER_TOPK * PEER_TOPK)
    top_s, pos = lax.top_k(cand_s, PEER_TOPK)
    idx = jnp.take_along_axis(cand_i, pos, axis=-1)
    gates = jax.nn.softmax(top_s, axis=-1).astype(h.dtype)

    def chunk(args):
        x_c, i_c, g_c = args
        act = jax.nn.gelu(jnp.einsum('chkd,cd->chk', u_tab[i_c], x_c))
        return jnp.einsum('chk,chkd->cd', g_c * act, v_tab[i_c])

    nc = n // PEER_CHUNK
    out = lax.map(chunk, (t.reshape(nc, PEER_CHUNK, D_MODEL),
                          idx.reshape(nc, PEER_CHUNK, PEER_H, PEER_TOPK),
                          gates.reshape(nc, PEER_CHUNK, PEER_H, PEER_TOPK)))
    return out.reshape(lead + (D_MODEL,))

def first_inputs(seed: int = 0) -> dict:
    key = jax.random.key(seed)
    keys = iter(jax.random.split(key, 32))
    nrm = lambda shape, std: std * jax.random.normal(next(keys), shape, jnp.float32)
    L, D = DEPTH, D_MODEL
    return {
        'x': nrm((BATCH, SEQ, D), 1.0),
        'c': nrm((BATCH, D), 1.0),
        'ctx': nrm((BATCH, CTX_LEN, D), 1.0),
        'c_ctx': nrm((D,), 1.0),
        'ada_w': nrm((L, D, 6 * D), 0.5 * D ** -0.5),
        'ada_b': nrm((L, 6 * D), 0.02),
        'norm1_g': 1.0 + nrm((L, D), 0.02),
        'norm2_g': 1.0 + nrm((L, D), 0.02),
        'w_in': nrm((L, D, D_IN), D ** -0.5),
        'rw_w0': jnp.linspace(-5.0, 1.0, RW_W, dtype=jnp.float32) + nrm((L, 2, RW_W), 0.1),
        'rw_w_up': nrm((L, 2, RW_LW, RW_W), 0.5 * RW_LW ** -0.5),
        'rw_a0': nrm((L, 2, RW_W), 0.1),
        'rw_a_up': nrm((L, 2, RW_LA, RW_W), 0.5 * RW_LA ** -0.5),
        'rw_g_up': nrm((L, RW_LG, RW_W), RW_LG ** -0.5),
        'rw_k_k': 0.85 + nrm((L, RW_W), 0.05),
        'rw_k_a': 1.0 + nrm((L, RW_W), 0.05),
        'rw_r_k': nrm((L, RW_H, RW_DH), 0.1),
        'rw_lnx_g': 1.0 + nrm((L, RW_W), 0.02),
        'na_rpb': nrm((L, NA_H, 2 * NA_KR - 1, 2 * NA_KC - 1), 0.1),
        'sc_conv_w': nrm((L, SC_K, SC_W), SC_K ** -0.5),
        'w_out': nrm((L, D_MIX, D), D_MIX ** -0.5),
        'peer_q_w': nrm((L, D, PEER_H * PEER_DQ), D ** -0.5),
        'peer_sub_keys': nrm((L, PEER_H, 2, PEER_NKEYS, PEER_DQ // 2), (PEER_DQ // 2) ** -0.5),
        'peer_u': nrm((L, PEER_N, D), D ** -0.5),
        'peer_v': nrm((L, PEER_N, D), PEER_TOPK ** -0.5),
        'final_g': 1.0 + nrm((D,), 0.02),
    }

def first_block(x, c, ctx, c_ctx, ada_w, ada_b, norm1_g, norm2_g, w_in, rw_w0, rw_w_up, rw_a0,
              rw_a_up, rw_g_up, rw_k_k, rw_k_a, rw_r_k, rw_lnx_g, na_rpb, sc_conv_w, w_out,
              peer_q_w, peer_sub_keys, peer_u, peer_v, final_g):
    xl, xc = x, ctx
    for i in range(DEPTH):
        need_ctx = i < DEPTH - 1
        mod_l = jax.nn.silu(c) @ ada_w[i] + ada_b[i]
        mod_c = jax.nn.silu(c_ctx) @ ada_w[i] + ada_b[i]
        sh1, sc1, g1, sh2, sc2, g2 = jnp.split(mod_l[:, None, :], 6, axis=-1)
        csh1, csc1, cg1, csh2, csc2, cg2 = jnp.split(mod_c, 6, axis=-1)
        hl = rmsnorm(xl, norm1_g[i]) * (1.0 + sc1) + sh1
        hc = rmsnorm(xc, norm1_g[i]) * (1.0 + csc1) + csh1
        yc, yl = token_mixing(hc, hl, w_in[i], w_out[i], rw_w0[i], rw_w_up[i], rw_a0[i], rw_a_up[i],
                              rw_g_up[i], rw_k_k[i], rw_k_a[i], rw_r_k[i], rw_lnx_g[i], na_rpb[i],
                              sc_conv_w[i], need_ctx)
        xl = xl + g1 * yl
        hl2 = rmsnorm(xl, norm2_g[i]) * (1.0 + sc2) + sh2
        xl = xl + g2 * peer_ffn(hl2, peer_q_w[i], peer_sub_keys[i], peer_u[i], peer_v[i])
        if need_ctx:
            xc = xc + cg1 * yc
            hc2 = rmsnorm(xc, norm2_g[i]) * (1.0 + csc2) + csh2
            xc = xc + cg2 * peer_ffn(hc2, peer_q_w[i], peer_sub_keys[i], peer_u[i], peer_v[i])
    return rmsnorm(xl, final_g)


DEPTH_2 = 4

N_MIXERS = 3
Q_BLK = 128
EPS = 1e-6
NEG = -1e30
FORCE = 1e4
NSA_HEADS = 16
NSA_DK = 64
NSA_KV = 4
NSA_REP = NSA_HEADS // NSA_KV
CMP_LEN = 32
CMP_STRIDE = 16
CMP_HID = 256
SEL_LEN = 64
SEL_TOPK = 16
WIN = 512
NSA_QW = NSA_HEADS * NSA_DK
NSA_KVW = NSA_KV * NSA_DK
NSA_IN = NSA_QW + 6 * NSA_KVW + 3 * NSA_HEADS
SB_HEADS = 16
SB_DH = D_MODEL // SB_HEADS
DIFF_HEADS = 8
DIFF_DH = D_MODEL // (2 * DIFF_HEADS)
D_FF = 2816
N_A = (DEPTH_2 + 2) // 3
N_B = (DEPTH_2 + 1) // 3
N_C = DEPTH_2 // 3


def rms_norm(x, g):
    xf = x.astype(jnp.float32)
    y = xf * lax.rsqrt(jnp.mean(xf * xf, axis=-1, keepdims=True) + EPS)
    return (y * g.astype(jnp.float32)).astype(x.dtype)

def alibi_slopes(n):
    return jnp.exp2(-8.0 * jnp.arange(1, n + 1, dtype=jnp.float32) / n)

def swiglu(h, w1, w2):
    gate, up = jnp.split(h @ w1, 2, axis=-1)
    return (jax.nn.silu(gate) * up) @ w2

def sweep_blocks(fn, seq):
    out = lax.map(fn, jnp.arange(seq // Q_BLK, dtype=jnp.int32) * Q_BLK)
    out = jnp.moveaxis(out, 0, 1)
    return out.reshape(out.shape[0], seq, *out.shape[3:])

def nsa_mixer(h, w_in, cmp_pe, cmp_w1, cmp_w2, w_out):
    B, T, _ = h.shape
    f32 = jnp.float32
    bounds = [int(b) for b in np.cumsum([NSA_QW] + [NSA_KVW] * 6)]
    parts = jnp.split(h @ w_in, bounds, axis=-1)
    q = parts[0].reshape(B, T, NSA_KV, NSA_REP, NSA_DK)
    kc, vc, ks, vs, kw, vw = [p.reshape(B, T, NSA_KV, NSA_DK) for p in parts[1:7]]
    gates = jax.nn.sigmoid(parts[7].astype(f32)).reshape(B, T, NSA_KV, NSA_REP, 3)
    scale = NSA_DK ** -0.5
    slopes = alibi_slopes(NSA_HEADS).reshape(NSA_KV, NSA_REP)

    n_cmp = (T - CMP_LEN) // CMP_STRIDE + 1
    cmp_start = jnp.arange(n_cmp) * CMP_STRIDE
    tok_idx = cmp_start[:, None] + jnp.arange(CMP_LEN)[None, :]

    def compress(a, j):
        blk = a[:, tok_idx] + cmp_pe[j][None, None, :, None, :]
        blk = jnp.moveaxis(blk, 3, 2).reshape(B, n_cmp, NSA_KV, CMP_LEN * NSA_DK)
        return jax.nn.gelu(blk @ cmp_w1[j]) @ cmp_w2[j]

    k_cmp = compress(kc, 0)
    v_cmp = compress(vc, 1)
    cmp_end = cmp_start + CMP_LEN - 1

    n_sel = T // SEL_LEN
    topk = min(SEL_TOPK, n_sel)
    sel_start = jnp.arange(n_sel) * SEL_LEN
    overlap = ((cmp_start[:, None] < sel_start[None, :] + SEL_LEN)
               & (cmp_start[:, None] + CMP_LEN > sel_start[None, :])).astype(f32)
    ks_blk = jnp.moveaxis(ks.reshape(B, n_sel, SEL_LEN, NSA_KV, NSA_DK), 3, 1)
    vs_blk = jnp.moveaxis(vs.reshape(B, n_sel, SEL_LEN, NSA_KV, NSA_DK), 3, 1)
    b_i = jnp.arange(B)[:, None, None, None]
    g_i = jnp.arange(NSA_KV)[None, :, None, None]
    sel_ids = jnp.arange(n_sel)

    kw_pad = jnp.pad(kw, ((0, 0), (WIN, 0), (0, 0), (0, 0)))
    vw_pad = jnp.pad(vw, ((0, 0), (WIN, 0), (0, 0), (0, 0)))

    def block(q0):
        t = q0 + jnp.arange(Q_BLK)
        qb = lax.dynamic_slice_in_dim(q, q0, Q_BLK, axis=1)
        s = jnp.einsum('bqgrd,bngd->bgrqn', qb, k_cmp).astype(f32) * scale
        dist = (t[:, None] - cmp_end[None, :]).astype(f32)
        valid = dist >= 0
        s = jnp.where(valid, s - slopes[None, :, :, None, None] * dist, NEG)
        p_cmp = jax.nn.softmax(s, axis=-1) * valid
        o_cmp = jnp.einsum('bgrqn,bngd->bqgrd', p_cmp.astype(v_cmp.dtype), v_cmp)
        imp = jnp.einsum('bgrqn,ns->bgqs', p_cmp, overlap)
        cur = t // SEL_LEN
        forced = ((sel_ids[None, :] == 0) | (sel_ids[None, :] == cur[:, None])
                  | (sel_ids[None, :] == cur[:, None] - 1))
        imp = jnp.where(forced, imp + FORCE, imp)
        imp = jnp.where(sel_ids[None, :] <= cur[:, None], imp, NEG)
        _, idx = lax.top_k(imp, topk)
        k_g = ks_blk[b_i, g_i, idx]
        v_g = vs_blk[b_i, g_i, idx]
        pos = idx[..., None] * SEL_LEN + jnp.arange(SEL_LEN)
        dist = (t[None, None, :, None, None] - pos).astype(f32)[:, :, None]
        s = jnp.einsum('bqgrd,bgqkld->bgrqkl', qb, k_g).astype(f32) * scale
        s = jnp.where(dist >= 0, s - slopes[None, :, :, None, None, None] * dist, NEG)
        p_sel = jax.nn.softmax(s, axis=(-2, -1))
        o_sel = jnp.einsum('bgrqkl,bgqkld->bqgrd', p_sel.astype(v_g.dtype), v_g)
        kwb = lax.dynamic_slice_in_dim(kw_pad, q0, WIN + Q_BLK, axis=1)
        vwb = lax.dynamic_slice_in_dim(vw_pad, q0, WIN + Q_BLK, axis=1)
        src = q0 - WIN + jnp.arange(WIN + Q_BLK)
        d_int = t[:, None] - src[None, :]
        valid = (d_int >= 0) & (d_int < WIN) & (src[None, :] >= 0)
        s = jnp.einsum('bqgrd,bsgd->bgrqs', qb, kwb).astype(f32) * scale
        s = jnp.where(valid, s - slopes[None, :, :, None, None] * d_int.astype(f32), NEG)
        p_win = jax.nn.softmax(s, axis=-1)
        o_win = jnp.einsum('bgrqs,bsgd->bqgrd', p_win.astype(vwb.dtype), vwb)
        g = lax.dynamic_slice_in_dim(gates, q0, Q_BLK, axis=1)
        o = g[..., 0:1] * o_cmp + g[..., 1:2] * o_sel + g[..., 2:3] * o_win
        return o.reshape(B, Q_BLK, NSA_QW)

    return sweep_blocks(block, T) @ w_out

def stick_breaking_mixer(h, w_in, w_out):
    B, T, _ = h.shape
    f32 = jnp.float32
    q, k, v = [a.reshape(B, T, SB_HEADS, SB_DH) for a in jnp.split(h @ w_in, 3, axis=-1)]
    scale = SB_DH ** -0.5
    src = jnp.arange(T)

    def block(q0):
        t = q0 + jnp.arange(Q_BLK)
        qb = lax.dynamic_slice_in_dim(q, q0, Q_BLK, axis=1)
        z = jnp.einsum('bqhd,bkhd->bhqk', qb, k).astype(f32) * scale
        before = src[None, :] < t[:, None]
        log_1m = jnp.where(before, jax.nn.log_sigmoid(-z), 0.0)
        log_rem = lax.cumsum(log_1m, axis=3, reverse=True) - log_1m
        a = jnp.where(before, jnp.exp(jax.nn.log_sigmoid(z) + log_rem), 0.0)
        o = jnp.einsum('bhqk,bkhd->bqhd', a.astype(v.dtype), v)
        return o.reshape(B, Q_BLK, D_MODEL)

    return sweep_blocks(block, T) @ w_out

def diff_attention_mixer(h, w_in, lam, subln_g, w_out, layer_idx):
    B, T, _ = h.shape
    f32 = jnp.float32
    lam_init = 0.8 - 0.6 * math.exp(-0.3 * layer_idx)
    lam_f = lam.astype(f32)
    lam_full = jnp.exp(jnp.sum(lam_f[0] * lam_f[1])) - jnp.exp(jnp.sum(lam_f[2] * lam_f[3])) + lam_init
    qa, ka, va = jnp.split(h @ w_in, 3, axis=-1)
    q = qa.reshape(B, T, DIFF_HEADS, 2, DIFF_DH)
    k = ka.reshape(B, T, DIFF_HEADS, 2, DIFF_DH)
    v = va.reshape(B, T, DIFF_HEADS, 2 * DIFF_DH)
    scale = DIFF_DH ** -0.5
    slopes = alibi_slopes(DIFF_HEADS)
    src = jnp.arange(T)

    def block(q0):
        t = q0 + jnp.arange(Q_BLK)
        qb = lax.dynamic_slice_in_dim(q, q0, Q_BLK, axis=1)
        dist = (t[:, None] - src[None, :]).astype(f32)
        s = jnp.einsum('bqhmd,bkhmd->bhmqk', qb, k).astype(f32) * scale
        s = jnp.where(dist >= 0, s - slopes[None, :, None, None, None] * dist, NEG)
        p = jax.nn.softmax(s, axis=-1)
        a = p[:, :, 0] - lam_full * p[:, :, 1]
        o = jnp.einsum('bhqk,bkhe->bqhe', a.astype(v.dtype), v)
        o = rms_norm(o, subln_g) * (1.0 - lam_init)
        return o.reshape(B, Q_BLK, D_MODEL)

    return sweep_blocks(block, T) @ w_out

def second_inputs(seed: int = 0) -> dict:
    key = jax.random.key(seed)
    ks = jax.random.split(key, 18)

    def nrm(k, shape, s):
        return s * jax.random.normal(k, shape, jnp.float32)

    return {
        'x': nrm(ks[0], (BATCH, SEQ, D_MODEL), 1.0),
        'c': nrm(ks[1], (BATCH, D_MODEL), 1.0),
        'ada_w': nrm(ks[2], (DEPTH_2, D_MODEL, 9 * D_MODEL), 0.5 * D_MODEL ** -0.5),
        'ada_b': nrm(ks[3], (DEPTH_2, 9 * D_MODEL), 0.02),
        'norm_g': 1.0 + nrm(ks[4], (DEPTH_2, 6, D_MODEL), 0.05),
        'ffn_w1': nrm(ks[5], (DEPTH_2, 2, D_MODEL, 2 * D_FF), D_MODEL ** -0.5),
        'ffn_w2': nrm(ks[6], (DEPTH_2, 2, D_FF, D_MODEL), D_FF ** -0.5),
        'nsa_w_in': nrm(ks[7], (N_A, D_MODEL, NSA_IN), D_MODEL ** -0.5),
        'nsa_cmp_pe': nrm(ks[8], (N_A, 2, CMP_LEN, NSA_DK), 0.1),
        'nsa_cmp_w1': nrm(ks[9], (N_A, 2, CMP_LEN * NSA_DK, CMP_HID), (CMP_LEN * NSA_DK) ** -0.5),
        'nsa_cmp_w2': nrm(ks[10], (N_A, 2, CMP_HID, NSA_DK), CMP_HID ** -0.5),
        'nsa_w_out': nrm(ks[11], (N_A, NSA_QW, D_MODEL), NSA_QW ** -0.5),
        'sb_w_in': nrm(ks[12], (N_B, D_MODEL, 3 * D_MODEL), D_MODEL ** -0.5),
        'sb_w_out': nrm(ks[13], (N_B, D_MODEL, D_MODEL), D_MODEL ** -0.5),
        'diff_w_in': nrm(ks[14], (N_C, D_MODEL, 3 * D_MODEL), D_MODEL ** -0.5),
        'diff_lam': nrm(ks[15], (N_C, 4, DIFF_DH), 0.1),
        'diff_subln_g': 1.0 + nrm(ks[16], (N_C, 2 * DIFF_DH), 0.05),
        'diff_w_out': nrm(ks[17], (N_C, D_MODEL, D_MODEL), D_MODEL ** -0.5),
    }

def second_block(x, c, ada_w, ada_b, norm_g, ffn_w1, ffn_w2, nsa_w_in, nsa_cmp_pe, nsa_cmp_w1, nsa_cmp_w2,
              nsa_w_out, sb_w_in, sb_w_out, diff_w_in, diff_lam, diff_subln_g, diff_w_out):
    B, T, D = x.shape
    cond = jax.nn.silu(c)
    for i in range(DEPTH_2):
        mod = (cond @ ada_w[i] + ada_b[i]).reshape(B, 3, 3, D)

        def sublayer(x, sidx, fn, res_w):
            shift = mod[:, sidx, 0][:, None, :]
            scl = mod[:, sidx, 1][:, None, :]
            gate = mod[:, sidx, 2][:, None, :]
            hh = rms_norm(x, norm_g[i, 2 * sidx]) * (1.0 + scl) + shift
            return x + res_w * gate * rms_norm(fn(hh), norm_g[i, 2 * sidx + 1])

        x = sublayer(x, 0, lambda hh: swiglu(hh, ffn_w1[i, 0], ffn_w2[i, 0]), 0.5)
        kind, j = i % N_MIXERS, i // N_MIXERS
        if kind == 0:
            mixer = lambda hh: nsa_mixer(hh, nsa_w_in[j], nsa_cmp_pe[j], nsa_cmp_w1[j], nsa_cmp_w2[j], nsa_w_out[j])
        elif kind == 1:
            mixer = lambda hh: stick_breaking_mixer(hh, sb_w_in[j], sb_w_out[j])
        else:
            mixer = lambda hh: diff_attention_mixer(hh, diff_w_in[j], diff_lam[j], diff_subln_g[j], diff_w_out[j], i)
        x = sublayer(x, 1, mixer, 1.0)
        x = sublayer(x, 2, lambda hh: swiglu(hh, ffn_w1[i, 1], ffn_w2[i, 1]), 0.5)
    return x


def setup_inputs(seed=0):
    out = dict(first_inputs(seed))
    for name, value in second_inputs(seed + 1).items():
        if name != "x":
            out[name + "_2"] = value
    return out


def reference(
    x, c, ctx, c_ctx, ada_w, ada_b, norm1_g, norm2_g, w_in, rw_w0, rw_w_up, rw_a0, rw_a_up,
    rw_g_up, rw_k_k, rw_k_a, rw_r_k, rw_lnx_g, na_rpb, sc_conv_w, w_out, peer_q_w,
    peer_sub_keys, peer_u, peer_v, final_g, c_2, ada_w_2, ada_b_2, norm_g_2, ffn_w1_2, ffn_w2_2,
    nsa_w_in_2, nsa_cmp_pe_2, nsa_cmp_w1_2, nsa_cmp_w2_2, nsa_w_out_2, sb_w_in_2, sb_w_out_2,
    diff_w_in_2, diff_lam_2, diff_subln_g_2, diff_w_out_2,
):
    x = first_block(
        x, c, ctx, c_ctx, ada_w, ada_b, norm1_g, norm2_g, w_in, rw_w0, rw_w_up, rw_a0, rw_a_up,
        rw_g_up, rw_k_k, rw_k_a, rw_r_k, rw_lnx_g, na_rpb, sc_conv_w, w_out, peer_q_w,
        peer_sub_keys, peer_u, peer_v, final_g,
    )
    return second_block(
        x, c_2, ada_w_2, ada_b_2, norm_g_2, ffn_w1_2, ffn_w2_2, nsa_w_in_2, nsa_cmp_pe_2,
        nsa_cmp_w1_2, nsa_cmp_w2_2, nsa_w_out_2, sb_w_in_2, sb_w_out_2, diff_w_in_2, diff_lam_2,
        diff_subln_g_2, diff_w_out_2,
    )


_drawn_inputs = setup_inputs


def setup_inputs(seed=0):
    import zlib

    import numpy as np

    out = dict(_drawn_inputs(seed))
    spreads = {}
    factors = {'norm1_g': 5.956,
     'norm2_g': 62.832,
     'rw_w_up': 61.401,
     'rw_a0': 64.0,
     'rw_k_k': 200.0,
     'rw_k_a': 64.0,
     'rw_lnx_g': 200.0,
     'na_rpb': 64.0,
     'diff_subln_g_2': 46.849,
     'rw_w0': 7.281,
     'rw_a_up': 3.614}
    for name, (base, spread) in spreads.items():
        noise = np.random.default_rng([zlib.crc32(name.encode()), seed]).standard_normal(out[name].shape)
        drawn = base * np.exp(spread * noise) if base else spread * noise
        out[name] = jnp.asarray(drawn.astype(out[name].dtype))
    for name, factor in factors.items():
        out[name] = (out[name] * factor).astype(out[name].dtype)
    return out
```

```python
from contextlib import ExitStack, contextmanager

import numpy as np

import concourse.bass as bass
from concourse import mybir

F32 = mybir.dt.float32
U32 = mybir.dt.uint32
ALU = mybir.AluOpType
ACT = mybir.ActivationFunctionType
AX = mybir.AxisListType

P = 128
D = 1024
KD = D // P
T = 256
TT = T // P
DH = 64
WN = 256
ITEM = KD * WN
W_SLOTS = 6
A_ITEM = (KD + 1) * WN
A_SLOTS = 3
BANK = 512
BANKS = 8
EPS = 1e-6
GN_EPS = 64e-5
NEG = -1e30

DEPTH = 4
D_FF = 2816
FF_STEPS = D_FF // WN
FF_ITEMS = 3 * FF_STEPS
MOD_COLS = 9 * D
MOD_ITEMS = MOD_COLS // WN
MIXERS = ("nsa", "stick", "diff", "nsa")
NSA_HEADS, NSA_KV = 16, 4
NSA_REP = NSA_HEADS // NSA_KV
CMP_LEN, CMP_STRIDE, CMP_HID = 32, 16, 256
N_CMP = (T - CMP_LEN) // CMP_STRIDE + 1
DIFF_HEADS = 8
SLOPES = [2.0 ** (-8.0 * (h + 1) / NSA_HEADS) for h in range(NSA_HEADS)]


class Signal:

    def __init__(self, sem):
        self.sem = sem
        self.base = 0

    def at(self, n):
        return self.base + n

    def passed(self, n):
        self.base += n


class Steps:

    def __init__(self, sem):
        self.sem = sem
        self.n = 0
        self.turns = 0

    def done(self, eng, ins):
        ins.then_inc(self.sem, 1)
        self.n += 1
        eng.wait_ge(self.sem, self.n + self.turns)

    @contextmanager
    def loop(self, eng, trips, steps):
        start = self.n
        with eng.Fori(0, trips, 1) as i:
            self.turns = i * steps
            yield i
        assert self.n - start == steps, (self.n - start, steps)
        self.turns = 0
        self.n += steps * (trips - 1)


class Core:

    def __init__(self, nc, ctx):
        self.nc = nc
        self.ctx = ctx
        self.signals = {}
        self.serial = 0
        self.pe_steps = Steps(ctx.enter_context(nc.semaphore("pe_steps")))
        self.act_steps = Steps(ctx.enter_context(nc.semaphore("act_steps")))
        self.dve_steps = Steps(ctx.enter_context(nc.semaphore("dve_steps")))
        self.pool_steps = Steps(ctx.enter_context(nc.semaphore("pool_steps")))
        self.w_loaded = [ctx.enter_context(nc.semaphore(f"w_loaded{s}")) for s in range(W_SLOTS)]
        self.w_used = ctx.enter_context(nc.semaphore("w_used"))
        self.a_loaded = [ctx.enter_context(nc.semaphore(f"a_loaded{s}")) for s in range(A_SLOTS)]
        self.a_used = ctx.enter_context(nc.semaphore("a_used"))
        self.w_issued = self.w_taken = 0
        self.a_issued = self.a_taken = 0
        self.a_limit = MOD1_ITEMS + MOD_ITEMS

    def semaphore_of(self, name):
        if name not in self.signals:
            self.signals[name] = Signal(self.ctx.enter_context(self.nc.semaphore(name)))
        return self.signals[name]

    def sb(self, ctx, name, shape, dtype=F32):
        self.serial += 1
        return ctx.enter_context(self.nc.sbuf_tensor(f"{name}_{self.serial}", shape, dtype))

    def w_item(self, n):
        return self.ring[:, n % W_SLOTS, :].rearrange("p (k n) -> p k n", k=KD)

    def w_wait(self, pe, n, turn=0):
        pe.wait_ge(self.w_loaded[n % W_SLOTS], (turn + (n // W_SLOTS + 1)) * 16)

    def issue_w(self, sp, take):
        total = self.w_stream.shape[0]
        upto = min(self.w_taken + take + W_SLOTS, total)
        n = self.w_issued
        if n < W_SLOTS:
            for n in range(0, W_SLOTS):
                sp.dma_start(self.ring[:, n, :], self.w_stream[n]).then_inc(self.w_loaded[n], 16)
            n = W_SLOTS
        turns = (upto - n) // W_SLOTS
        if turns > 1:
            with sp.Fori(0, turns, 1) as i:
                for s in range(W_SLOTS):
                    sp.wait_ge(self.w_used, i * W_SLOTS + (n + s - W_SLOTS + 1))
                    src = self.w_stream[bass.ds(i * W_SLOTS + (n + s), 1), :, :]
                    sp.dma_start(self.ring[:, (n + s) % W_SLOTS, :],
                                 src.rearrange("a p n -> p (a n)")).then_inc(
                                     self.w_loaded[(n + s) % W_SLOTS], 16)
            n += turns * W_SLOTS
        while n < upto:
            sp.wait_ge(self.w_used, n - W_SLOTS + 1)
            sp.dma_start(self.ring[:, n % W_SLOTS, :], self.w_stream[n]).then_inc(
                self.w_loaded[n % W_SLOTS], 16)
            n += 1
        self.w_issued = n
        self.w_taken += take

    def issue_a(self, sp, take, ahead):
        upto = min(self.a_taken + take + (A_SLOTS if ahead else 0), self.a_limit)
        n = self.a_issued
        while n < upto and n < self.a_first + A_SLOTS:
            sp.dma_start(self.a_ring[:, n % A_SLOTS, :], self.a_stream[n]).then_inc(
                self.a_loaded[n % A_SLOTS], 16)
            n += 1
        turns = (upto - n) // A_SLOTS
        if turns > 0:
            with sp.Fori(0, turns, 1) as i:
                for s in range(A_SLOTS):
                    sp.wait_ge(self.a_used, i * A_SLOTS + (n + s - A_SLOTS + 1))
                    src = self.a_stream[bass.ds(i * A_SLOTS + (n + s), 1), :, :]
                    sp.dma_start(self.a_ring[:, (n + s) % A_SLOTS, :],
                                 src.rearrange("a p n -> p (a n)")).then_inc(
                                     self.a_loaded[(n + s) % A_SLOTS], 16)
            n += turns * A_SLOTS
        while n < upto:
            sp.wait_ge(self.a_used, n - A_SLOTS + 1)
            sp.dma_start(self.a_ring[:, n % A_SLOTS, :], self.a_stream[n]).then_inc(
                self.a_loaded[n % A_SLOTS], 16)
            n += 1
        self.a_issued = n
        self.a_taken += take

    def issue_both(self, sp, w_take, a_take):
        w_to = min(self.w_taken + w_take + W_SLOTS, self.w_stream.shape[0])
        a_to = min(self.a_taken + a_take + A_SLOTS, self.a_limit)
        turns = min((w_to - self.w_issued) // W_SLOTS, (a_to - self.a_issued) // (2 * A_SLOTS))
        if a_take and turns > 1:
            w, a = self.w_issued, self.a_issued
            with sp.Fori(0, turns, 1) as i:
                for s in range(W_SLOTS):
                    sp.wait_ge(self.w_used, i * W_SLOTS + (w + s - W_SLOTS + 1))
                    src = self.w_stream[bass.ds(i * W_SLOTS + (w + s), 1), :, :]
                    sp.dma_start(self.ring[:, (w + s) % W_SLOTS, :],
                                 src.rearrange("a p n -> p (a n)")).then_inc(
                                     self.w_loaded[(w + s) % W_SLOTS], 16)
                    sp.wait_ge(self.a_used, i * (2 * A_SLOTS) + (a + s - A_SLOTS + 1))
                    src = self.a_stream[bass.ds(i * (2 * A_SLOTS) + (a + s), 1), :, :]
                    sp.dma_start(self.a_ring[:, (a + s) % A_SLOTS, :],
                                 src.rearrange("a p n -> p (a n)")).then_inc(
                                     self.a_loaded[(a + s) % A_SLOTS], 16)
            self.w_issued += turns * W_SLOTS
            self.a_issued += turns * 2 * A_SLOTS
        self.issue_w(sp, w_take)
        if a_take:
            self.issue_a(sp, a_take, 1)

    def mod_unit(self, dve, n, outs, turn=0):
        dve.wait_ge(self.a_loaded[n % A_SLOTS], (turn + (n // A_SLOTS + 1)) * 16)
        item = self.a_ring[:, n % A_SLOTS, :].rearrange("p (k n) -> p k n", k=KD + 1)
        for cond, acc in outs:
            for k in range(KD):
                last = dve.scalar_tensor_tensor(
                    out=acc, in0=item[:, k, :], scalar=cond[:, k:k + 1],
                    in1=item[:, KD, :] if k == 0 else acc, op0=ALU.mult, op1=ALU.add)
                self.dve_steps.done(dve, last)
        dve.sem_inc(self.a_used, 1)


def put(eng, is_act, out, in_, scale=1.0):
    if is_act:
        return eng.activation(out, in_, ACT.Copy, scale=scale)
    return eng.tensor_scalar(out, in_, scale, None, ALU.mult)


def wide(ap, n):
    return bass.AP(ap.tensor, ap.offset, [list(x) for x in ap.ap] + [[0, n]])


def columns(core, k, c0, n):
    return slice(c0, c0 + n)


def norm_stage(core, post, pre, of=None):
    nc = core.nc
    squares, roots = core.semaphore_of("squares_ready"), core.semaphore_of("roots_ready")
    means, rows = core.semaphore_of("means_ready"), core.semaphore_of("rows_ready")
    turned, x_new = core.semaphore_of("turned_ready"), core.semaphore_of("x_new")
    x, hT, gain, shift = of or (core.x, core.hT, core.gain, core.shift)
    y = core.y
    n_post = 1 if post is not None else 0
    n_pre = 1 if pre is not None else 0
    with ExitStack() as ctx:
        junk = core.sb(ctx, "junk", [P, 2, D])
        ss = core.sb(ctx, "ss", [P, 2, 2 * TT])
        stat = core.sb(ctx, "stat", [P, 4, TT])
        xn = core.sb(ctx, "xn", [P, TT, D])
        block = ctx.enter_context(nc.Block())

        @block.sync
        def _(sp):
            core.issue_w(sp, 0)

        @block.scalar
        def _(act):
            if n_post:
                for i in range(2 * TT):
                    act.activation(junk[:, i // 2, (i % 2) * BANK:(i % 2 + 1) * BANK], y[:, i, :], ACT.Square,
                                   accum_out=ss[:, 0, i:i + 1]).then_inc(squares.sem, 1)
                act.wait_ge(means.sem, means.at(1))
                act.activation(stat[:, 0, :], stat[:, 0, :], ACT.Sqrt).then_inc(roots.sem, 1)
                act.wait_ge(x_new.sem, x_new.at(1))
            if n_pre:
                for t in range(TT):
                    act.activation(junk[:, t, :], x[:, t, :], ACT.Square,
                                   accum_out=ss[:, 1, t:t + 1]).then_inc(squares.sem, 1)
                act.wait_ge(means.sem, means.at(n_post + 1))
                act.activation(stat[:, 2, :], stat[:, 2, :], ACT.Sqrt).then_inc(roots.sem, 1)
                for k in range(KD):
                    act.wait_ge(turned.sem, turned.at(k // 2 + 1))
                    act.activation(hT[:, k, :], core.ps[:, k // 2, (k % 2) * T:(k % 2 + 1) * T],
                                   ACT.Identity, scale=gain[:, pre, k:k + 1],
                                   bias=shift[:, pre, k:k + 1])

        @block.vector
        def _(dve):
            if n_post:
                dve.wait_ge(squares.sem, squares.at(2 * TT))
                for t in range(TT):
                    core.dve_steps.done(dve, dve.tensor_tensor(
                        stat[:, 1, t:t + 1], ss[:, 0, 2 * t:2 * t + 1], ss[:, 0, 2 * t + 1:2 * t + 2],
                        ALU.add))
                dve.tensor_scalar(stat[:, 0, :], stat[:, 1, :], 1.0 / D, EPS, ALU.mult,
                                  ALU.add).then_inc(means.sem, 1)
                dve.wait_ge(roots.sem, roots.at(1))
                core.dve_steps.done(dve, dve.reciprocal(stat[:, 1, :], stat[:, 0, :]))
                for i in range(2 * TT):
                    t, half = i // 2, i % 2
                    part = slice(half * BANK, (half + 1) * BANK)
                    core.dve_steps.done(dve, dve.scalar_tensor_tensor(
                        out=xn[:, t, part], in0=y[:, i, :], scalar=stat[:, 1, t:t + 1],
                        in1=core.gates[:, post, part], op0=ALU.mult, op1=ALU.mult))
                last = dve.tensor_tensor(x[:], x[:], xn[:], ALU.add)
                last.then_inc(x_new.sem, 1)
                dve.wait_ge(x_new.sem, x_new.at(1))
            if n_pre:
                dve.wait_ge(squares.sem, squares.at(2 * TT * n_post + TT))
                dve.tensor_scalar(stat[:, 2, :], ss[:, 1, 0:TT], 1.0 / D, EPS, ALU.mult,
                                  ALU.add).then_inc(means.sem, 1)
                dve.wait_ge(roots.sem, roots.at(n_post + 1))
                core.dve_steps.done(dve, dve.reciprocal(stat[:, 3, :], stat[:, 2, :]))
                for t in range(TT):
                    dve.tensor_scalar(xn[:, t, :], x[:, t, :], stat[:, 3, t:t + 1], None,
                                      ALU.mult).then_inc(rows.sem, 1)

        @block.tensor
        def _(pe):
            if n_pre:
                pe.wait_ge(rows.sem, rows.at(TT))
                for k in range(KD):
                    for t in range(TT):
                        last = pe.transpose(core.ps[:, k // 2, (k % 2) * T + t * P:(k % 2) * T + (t + 1) * P],
                                            xn[:, t, k * P:(k + 1) * P], core.ident[:])
                    if k % 2:
                        last.then_inc(turned.sem, 1)

    squares.passed(2 * TT * n_post + TT * n_pre)
    roots.passed(n_post + n_pre)
    means.passed(n_post + n_pre)
    rows.passed(TT * n_pre)
    turned.passed(KD // 2 * n_pre)
    x_new.passed(n_post)


def mod_columns(core, pe, acc, vectors, col, bank):
    for v in vectors:
        for k in range(KD):
            last = pe.matmul(core.ps[:, bank, col:col + 1], acc[:, v * D + k * P:v * D + (k + 1) * P],
                             core.ones[:, 0:1], start=True, stop=True)
            col += 1
    return last


def shape_columns(core, dve, layer, bank):
    cols = core.ps[:, bank, 0:9 * KD].rearrange("p (s a k) -> p s a k", s=3, a=3)
    dve.tensor_copy(core.shift[:], cols[:, :, 0, :])
    dve.scalar_tensor_tensor(out=core.gain[:], in0=cols[:, :, 1, :], scalar=1.0, in1=core.norm_pre[:, layer],
                             op0=ALU.add, op1=ALU.mult)
    for s in range(3):
        weight = 0.5 if s != 1 else 1.0
        last = dve.scalar_tensor_tensor(out=core.gate_cols[:, s, :], in0=cols[:, s, 2, :], scalar=weight,
                                        in1=core.norm_post[:, layer, s, :], op0=ALU.mult, op1=ALU.mult)
    return last


def mod_stage(core, layer, acc):
    nc = core.nc
    summed, shaped, wide_out = (core.semaphore_of(n) for n in ("mod_summed", "mod_shaped", "mod_wide"))
    with nc.Block() as block:
        @block.sync
        def _(sp):
            core.issue_w(sp, 0)
            core.issue_a(sp, 0, 1)

        @block.tensor
        def _(pe):
            if acc is not None:
                mod_columns(core, pe, acc, range(9), 0, 0).then_inc(summed.sem, 1)
                pe.wait_ge(shaped.sem, shaped.at(1))
            for s in range(3):
                for half in range(2):
                    for j in range(4):
                        k = 4 * half + j
                        col = core.gate_cols[:, s, k:k + 1]
                        last = pe.matmul(core.ps[:, 1 + 2 * s + half, j * P:(j + 1) * P],
                                         bass.AP(col.tensor, col.offset, [list(col.ap[0]), [0, P]]),
                                         core.ident[:], start=True, stop=True)
                    last.then_inc(wide_out.sem, 1)

        def copies(eng, is_act):
            for i in range(0 if is_act else 1, 6, 2):
                eng.wait_ge(wide_out.sem, wide_out.at(i + 1))
                put(eng, is_act, core.gates[:, i // 2, (i % 2) * BANK:(i % 2 + 1) * BANK], core.ps[:, 1 + i, :])

        @block.scalar
        def _(act):
            copies(act, True)

        @block.vector
        def _(dve):
            if acc is not None:
                dve.wait_ge(summed.sem, summed.at(1))
                shape_columns(core, dve, layer, 0).then_inc(shaped.sem, 1)
            copies(dve, False)

    if acc is not None:
        summed.passed(1)
        shaped.passed(1)
    wide_out.passed(6)


FF_TURNS = (FF_STEPS - 3) // 2


def ffn_stage(core, with_mod):
    nc = core.nc
    silus, hidden = core.semaphore_of("silu_ready"), core.semaphore_of("hidden_ready")
    w_used = core.w_used
    first, a0 = core.w_taken, core.a_taken
    n_mod = MOD_ITEMS if with_mod else 0
    per_turn = 2 * 3

    def gate_item(s):
        return first + (3 * s - 1 if s else 0)

    def up_item(s):
        return first + (3 * s if s else 1)

    def down_item(s):
        return first + (3 * s + 4 if s < FF_STEPS - 1 else FF_ITEMS - 1)

    with ExitStack() as ctx:
        act_g = core.sb(ctx, "act_g", [P, 2, 2 * T])
        hid = core.sb(ctx, "hid", [P, 2, 2, T])
        block = ctx.enter_context(nc.Block())

        @block.sync
        def _(sp):
            core.issue_both(sp, FF_ITEMS, n_mod)

        @block.tensor
        def _(pe):
            def up(s, i=0):
                if s >= 2:
                    pe.wait_ge(hidden.sem, i * 2 + hidden.at(s - 1))
                for part, n in enumerate((gate_item(s), up_item(s))):
                    core.w_wait(pe, n, i)
                    w = core.w_item(n)
                    for m in range(2):
                        for k in range(KD):
                            last = pe.matmul(core.ps[:, 2 * (s % 2) + part, m * T:(m + 1) * T],
                                             w[:, k, m * P:(m + 1) * P], core.hT[:, k, :],
                                             start=(k == 0), stop=(k == KD - 1))
                    last.then_inc(w_used, 1)

            def down(s, i=0):
                pe.wait_ge(hidden.sem, i * 2 + hidden.at(s + 1))
                core.w_wait(pe, down_item(s), i)
                w = core.w_item(down_item(s)).rearrange("p k n -> p (k n)").rearrange("p (m n) -> p m n", m=2)
                for t in range(TT):
                    for half in range(2):
                        for m in range(2):
                            last = pe.matmul(core.y[:, 2 * t + half, :], hid[:, s % 2, m, t * P:(t + 1) * P],
                                             w[:, m, half * BANK:(half + 1) * BANK],
                                             start=(s == 0 and m == 0), stop=(s == FF_STEPS - 1 and m == 1))
                last.then_inc(w_used, 1)

            up(0)
            up(1)
            down(0)
            up(2)
            down(1)
            with pe.Fori(0, FF_TURNS, 1) as i:
                up(3, i)
                down(2, i)
                up(4, i)
                down(3, i)
            down(FF_STEPS - 1)

        @block.scalar
        def _(act):
            def silu(s, i=0):
                if s >= 2:
                    act.wait_ge(hidden.sem, i * 2 + hidden.at(s - 1))
                act.wait_ge(w_used, i * per_turn + gate_item(s) + 1)
                act.activation(act_g[:, s % 2, :], core.ps[:, 2 * (s % 2), :], ACT.Silu).then_inc(silus.sem, 1)

            silu(0)
            silu(1)
            with act.Fori(0, FF_TURNS, 1) as i:
                silu(2, i)
                silu(3, i)
            silu(FF_STEPS - 1)

        @block.vector
        def _(dve):
            def hide(s, i=0):
                dve.wait_ge(silus.sem, i * 2 + silus.at(s + 1))
                dve.wait_ge(w_used, i * per_turn + up_item(s) + 1)
                if s >= 2:
                    dve.wait_ge(w_used, i * per_turn + down_item(s - 2) + 1)
                dve.tensor_tensor(hid[:, s % 2, :, :].rearrange("p m n -> p (m n)"), act_g[:, s % 2, :],
                                  core.ps[:, 2 * (s % 2) + 1, :], ALU.mult).then_inc(hidden.sem, 1)

            def mods(i, n):
                for j in range(A_SLOTS) if n_mod else ():
                    acc = core.acc[:, bass.ds(i * (2 * A_SLOTS * WN) + (n + j) * WN, WN)]
                    core.mod_unit(dve, a0 + n + j, [(core.cond, acc)], i * 2)

            hide(0)
            mods(0, 0)
            hide(1)
            mods(0, A_SLOTS)
            with core.dve_steps.loop(dve, FF_TURNS, 2 * A_SLOTS * KD if n_mod else 0) as i:
                hide(2, i)
                mods(i, 2 * A_SLOTS)
                hide(3, i)
                mods(i, 3 * A_SLOTS)
            hide(FF_STEPS - 1)
            for n in range(2 * (FF_TURNS + 1) * A_SLOTS, n_mod, A_SLOTS):
                mods(0, n)

    silus.passed(FF_STEPS)
    hidden.passed(FF_STEPS)


def ada_stage(core, take, also=None):
    nc = core.nc
    a0 = core.a_taken
    both = also[2] if also else 0
    with nc.Block() as block:
        @block.sync
        def _(sp):
            core.issue_a(sp, take, 0 if core.a_ends else 1)

        @block.vector
        def _(dve):
            for first, last, two in ((0, both, True), (both, take, False)):
                turns, rest = (last - first) // A_SLOTS, (last - first) % A_SLOTS

                def unit(j, i=0):
                    outs = [(core.cond, core.acc[:, bass.ds(i * (A_SLOTS * WN) + j * WN, WN)])]
                    if two:
                        outs.append((also[0], core.acc[:, bass.ds(i * (A_SLOTS * WN) + j * WN + also[1], WN)]))
                    core.mod_unit(dve, a0 + j, outs, i)

                if turns:
                    with core.dve_steps.loop(dve, turns, A_SLOTS * KD * (2 if two else 1)) as i:
                        for j in range(A_SLOTS):
                            unit(first + j, i)
                for j in range(last - rest, last):
                    unit(j)


def projections(core, items, units, side=None):
    nc = core.nc
    ready = core.semaphore_of("proj_ready")
    copied = [core.semaphore_of("proj_copied_act"), core.semaphore_of("proj_copied_dve")]
    first = core.w_taken
    by = 1 if side else 2
    last_of = {item: u for u, (item, _, _) in enumerate(units)}
    inner = [u for u, (item, _, _) in enumerate(units) if last_of[item] != u]
    with nc.Block() as block:
        @block.sync
        def _(sp):
            if side:
                side[0](sp, items)
            else:
                core.issue_w(sp, items)

        @block.tensor
        def _(pe):
            for u, (item, halves, _) in enumerate(units):
                if u >= BANKS:
                    pe.wait_ge(copied[u % by].sem, copied[u % by].at((u - BANKS) // by + 1))
                core.w_wait(pe, first + item)
                w = core.w_item(first + item)
                for m, (rows, stationary, moving) in enumerate(halves):
                    for k in range(KD):
                        last = pe.matmul(core.ps[0:rows, u % BANKS, m * T:(m + 1) * T], stationary(w, k),
                                         moving(w, k), start=(k == 0), stop=(k == KD - 1))
                last.then_inc(ready.sem if u in inner else core.w_used, 1)

        def copy(eng, parity):
            for u, (item, _, out) in enumerate(units):
                if u % by == parity:
                    if u in inner:
                        eng.wait_ge(ready.sem, ready.at(inner.index(u) + 1))
                    else:
                        eng.wait_ge(core.w_used, first + item + 1)
                    out(eng, parity == 0, core.ps[:, u % BANKS, :]).then_inc(copied[parity].sem, 1)

        @block.scalar
        def _(act):
            copy(act, 0)

        @block.vector
        def _(dve):
            if side:
                side[1](dve)
            else:
                copy(dve, 1)

    ready.passed(len(inner))
    for parity in range(by):
        copied[parity].passed(len(range(parity, len(units), by)))


def across(core, src, item, out, scale=1.0):
    def half(m):
        return (P, lambda w, k: w[:, k, m * P:(m + 1) * P], lambda w, k: src[:, k, :])
    return (item, [half(0), half(1)],
            lambda eng, is_act, bank: put(eng, is_act, out, bank.rearrange("p (m n) -> p m n", m=2), scale))


def along(core, src, item, out, cols=WN):
    def half(t):
        return (P, lambda w, k: src[:, k, t * P:(t + 1) * P], lambda w, k: w[:, k, :])
    return (item, [half(0), half(1)],
            lambda eng, is_act, bank: put(eng, is_act, out,
                                          bank.rearrange("p (t n) -> p t n", t=TT)[:, :, 0:cols]))


def across_twice(core, src, item, out):
    item, halves, _ = across(core, src, item, None)

    def copies(eng, is_act, bank):
        pairs = bank.rearrange("p (m n) -> p m n", m=2)
        for odd in range(2):
            for half in range(2):
                last = put(eng, is_act, out[half * DH:(half + 1) * DH, odd::2, :],
                           pairs[odd * DH:(odd + 1) * DH, :, :])
        return last

    return (item, halves, copies)


def out_projection(core, src):
    nc = core.nc
    first = core.w_taken
    items = D // WN
    with nc.Block() as block:
        @block.sync
        def _(sp):
            core.issue_w(sp, items)

        @block.tensor
        def _(pe):
            for n in range(items):
                core.w_wait(pe, first + n)
                w = core.w_item(first + n)
                for t in range(TT):
                    for k in range(KD):
                        last = pe.matmul(core.y[:, 2 * t + n // 2, (n % 2) * WN:(n % 2 + 1) * WN],
                                         src[:, k, t * P:(t + 1) * P], w[:, k, :],
                                         start=(k == 0), stop=(k == KD - 1))
                last.then_inc(core.w_used, 1)


LOGITS = 2 * BANK
LBUF = 528
L_BUFS = 3


def attention(core, ctx, mixer, n_units):
    nc = core.nc
    scored, logits = core.semaphore_of("at_scored"), core.semaphore_of("at_logits")
    raised, weighed = core.semaphore_of("at_raised"), core.semaphore_of("at_weighed")
    turned, copied = core.semaphore_of("at_turned"), core.semaphore_of("at_copied")
    valued, out = core.semaphore_of("at_valued"), core.semaphore_of("at_out")
    primed = core.semaphore_of("at_primed")
    with ExitStack() as inner:
        L = core.sb(inner, "logits", [P, L_BUFS, LBUF])
        pT = core.sb(inner, "probs_T", [P, 2, 5 * P])
        mx = core.sb(inner, "maxima", [P, L_BUFS, 4])
        sums = core.sb(inner, "sums", [P, L_BUFS, 4])
        block = inner.enter_context(nc.Block())

        def S(u):
            return core.ps[:, 2 * (u % 2):2 * (u % 2) + 2, :].rearrange("p b n -> p (b n)")

        turn_out = core.ps[:, 4:6, :].rearrange("p b n -> p (b n)")

        def O(u):
            return core.ps[:, 6 + u % 2, :]

        @block.sync
        def _(sp):
            core.issue_w(sp, 0)

        @block.tensor
        def _(pe):
            def score(u):
                if u >= 2:
                    pe.wait_ge(logits.sem, logits.at(u - 1))
                for c, n, stationary, moving in mixer.scores(u):
                    last = pe.matmul(S(u)[:, c:c + n], stationary, moving, start=True, stop=True)
                last.then_inc(scored.sem, 1)

            def turn(u):
                pe.wait_ge(weighed.sem, weighed.at(u + 1))
                if u >= 1:
                    pe.wait_ge(copied.sem, copied.at(u))
                for i, (c, n) in enumerate(mixer.tiles(u)):
                    last = pe.transpose(turn_out[0:n, i * P:(i + 1) * P], L[:, u % L_BUFS, c:c + n], core.ident[:])
                last.then_inc(turned.sem, 1)

            def value(u):
                pe.wait_ge(copied.sem, copied.at(u + 1))
                if u >= 2:
                    pe.wait_ge(out.sem, out.at(u - 1))
                mixer.values(pe, u, pT[:, u % 2, :], O(u)).then_inc(valued.sem, 1)

            score(0)
            score(1)
            for u in range(n_units):
                if u + 2 < n_units:
                    score(u + 2)
                turn(u)
                if u >= 1:
                    value(u - 1)
            value(n_units - 1)

        @block.scalar
        def _(act):
            def prime(u):
                act.wait_ge(scored.sem, scored.at(u + 1))
                mixer.first(act, u, S(u)).then_inc(primed.sem, 1)

            def exps(u):
                act.wait_ge(logits.sem, logits.at(u + 1))
                for g, (c, n) in enumerate(mixer.groups(u)):
                    part = L[:, u % L_BUFS, c:c + n]
                    if mixer.first is not None:
                        last = act.activation(part, part, ACT.Exp)
                    else:
                        last = act.activation(part, part, ACT.Exp, bias=mx[:, u % L_BUFS, g:g + 1],
                                              accum_out=sums[:, u % L_BUFS, g:g + 1])
                last.then_inc(raised.sem, 1)

            def copy(u):
                act.wait_ge(turned.sem, turned.at(u + 1))
                if u >= 2:
                    act.wait_ge(valued.sem, valued.at(u - 1))
                tiles = mixer.tiles(u)
                full = sum(n == P for _, n in tiles)
                last = act.activation(pT[:, u % 2, 0:full * P], turn_out[:, 0:full * P], ACT.Copy)
                if full < len(tiles):
                    n = tiles[-1][1]
                    last = act.activation(pT[0:n, u % 2, full * P:(full + 1) * P],
                                          turn_out[0:n, full * P:(full + 1) * P], ACT.Copy)
                last.then_inc(copied.sem, 1)

            def copy_out(u):
                act.wait_ge(valued.sem, valued.at(u + 1))
                mixer.out(act, u, O(u)).then_inc(out.sem, 1)

            if mixer.first is not None:
                prime(0)
            for u in range(n_units + 2):
                if mixer.first is not None and u + 1 < n_units:
                    if u >= 1:
                        act.wait_ge(logits.sem, logits.at(u))
                    prime(u + 1)
                if u < n_units:
                    exps(u)
                if 1 <= u <= n_units:
                    copy(u - 1)
                if u >= 2:
                    copy_out(u - 2)

        @block.vector
        def _(dve):
            def logit(u):
                dve.wait_ge(scored.sem, scored.at(u + 1))
                if u >= L_BUFS:
                    dve.wait_ge(turned.sem, turned.at(u - L_BUFS + 1))
                if mixer.first is not None:
                    dve.wait_ge(primed.sem, primed.at(u + 1))
                mixer.logits(dve, u, S(u), L[:, u % L_BUFS, :], mx[:, u % L_BUFS, :]).then_inc(logits.sem, 1)

            def weigh(u):
                dve.wait_ge(raised.sem, raised.at(u + 1))
                mixer.weigh(dve, u, L[:, u % L_BUFS, :], sums[:, u % L_BUFS, :]).then_inc(weighed.sem, 1)

            logit(0)
            for u in range(n_units):
                if u + 1 < n_units:
                    logit(u + 1)
                weigh(u)

    for s in (scored, logits, raised, weighed, turned, copied, valued, out):
        s.passed(n_units)
    if mixer.first is not None:
        primed.passed(n_units)


def causal(t):
    return (t + 1) * P


def alibi(core, h, t):
    return core.alibi[:, h, t * P:t * P + causal(t)]


class Softmax:

    first = None

    def finish_maxima(self, dve, mx, n):
        return dve.tensor_scalar(mx[:, 0:n], mx[:, 0:n], -1.0, None, ALU.mult)


class NSA(Softmax):

    def __init__(self, core, ctx):
        self.core = core
        self.qT = core.sb(ctx, "qT", [P, KD, T])
        self.ksT = core.sb(ctx, "ksT", [P, NSA_KV, T])
        self.kwT = core.sb(ctx, "kwT", [P, NSA_KV, T])
        self.vs = core.sb(ctx, "vs", [P, TT, NSA_KV * DH])
        self.vw = core.sb(ctx, "vw", [P, TT, NSA_KV * DH])
        self.gate = core.sb(ctx, "gate", [P, TT, 3 * NSA_HEADS])
        self.kcmpT = core.sb(ctx, "kcmpT", [P, NSA_KV, N_CMP])
        self.vcmp = core.sb(ctx, "vcmp", [N_CMP, NSA_KV, DH])
        self.oT = core.sb(ctx, "oT", [P, KD, T])

    def at(self, u):
        h, t = u // TT, u % TT
        return h, t, slice((h % 2) * DH, (h % 2) * DH + DH), h // NSA_REP

    def scores(self, u):
        h, t, part, g = self.at(u)
        q = self.qT[part, h // 2, t * P:(t + 1) * P]
        n = causal(t)
        return [(0, n, q, self.ksT[part, g, 0:n]), (T, n, q, self.kwT[part, g, 0:n]),
                (2 * T, N_CMP, q, self.kcmpT[part, g, :])]

    def groups(self, u):
        n = causal(u % TT)
        return [(0, n), (T, n), (2 * T, N_CMP)]

    def tiles(self, u):
        n = u % TT + 1
        return [(j * P, P) for j in range(n)] + [(T + j * P, P) for j in range(n)] + [(2 * T, N_CMP)]

    def logits(self, dve, u, S, L, mx):
        core = self.core
        h, t, _, _ = self.at(u)
        for g, (c, n) in enumerate(self.groups(u)):
            bias = alibi(core, h, t) if g < 2 else core.cmp_bias[:, h, t, :]
            last = dve.tensor_tensor_reduce(L[:, c:c + n], S[:, c:c + n], bias, 1.0, -3e38, ALU.add, ALU.max,
                                            mx[:, g:g + 1])
        core.dve_steps.done(dve, last)
        return self.finish_maxima(dve, mx, 3)

    def weigh(self, dve, u, L, sums):
        core = self.core
        h, t, _, _ = self.at(u)
        core.dve_steps.done(dve, dve.reciprocal(sums[:, 0:3], sums[:, 0:3]))
        core.dve_steps.done(dve, dve.tensor_tensor(sums[:, 0:3], sums[:, 0:3],
                                                   self.gate[:, t, 3 * h:3 * h + 3], ALU.mult))
        for g, (c, n) in enumerate(self.groups(u)):
            if g < 2:
                dve.tensor_scalar(L[:, c:c + n], L[:, c:c + n], sums[:, g:g + 1], None, ALU.mult)
            else:
                last = dve.scalar_tensor_tensor(out=L[:, c:c + n], in0=L[:, c:c + n], scalar=sums[:, g:g + 1],
                                                in1=core.cmp_valid[:, t, :], op0=ALU.mult, op1=ALU.mult)
        return last

    def values(self, pe, u, pT, O):
        h, t, part, g = self.at(u)
        vals = [(self.vs, j) for j in range(t + 1)] + [(self.vw, j) for j in range(t + 1)]
        for i, (v, j) in enumerate(vals):
            pe.matmul(O[part, 0:P], v[:, j, g * DH:(g + 1) * DH], pT[:, i * P:(i + 1) * P],
                      start=(i == 0), stop=False)
        i = len(vals)
        return pe.matmul(O[part, 0:P], self.vcmp[:, g, :], pT[0:N_CMP, i * P:(i + 1) * P], start=False, stop=True)

    def out(self, act, u, O):
        h, t, part, _ = self.at(u)
        return act.activation(self.oT[part, h // 2, t * P:(t + 1) * P], O[part, 0:P], ACT.Copy)


class Diff(Softmax):

    def __init__(self, core, ctx, lam_init):
        self.core = core
        self.keep = 1.0 - lam_init
        self.qT = core.sb(ctx, "qT", [P, DIFF_HEADS, T])
        self.kT = core.sb(ctx, "kT", [P, DIFF_HEADS, T])
        self.v = core.sb(ctx, "v", [P, TT, D])
        self.lam = core.sb(ctx, "lam", [P, 1])
        self.o = core.sb(ctx, "o", [P, TT, D])

    def scores(self, u):
        h, t = u // TT, u % TT
        n = causal(t)
        return [(m * BANK, n, self.qT[m * DH:(m + 1) * DH, h, t * P:(t + 1) * P],
                 self.kT[m * DH:(m + 1) * DH, h, 0:n]) for m in range(2)]

    def groups(self, u):
        n = causal(u % TT)
        return [(0, n), (T, n)]

    def tiles(self, u):
        return [(j * P, P) for j in range(u % TT + 1)]

    def logits(self, dve, u, S, L, mx):
        core = self.core
        h, t = u // TT, u % TT
        for g, (c, n) in enumerate(self.groups(u)):
            last = dve.tensor_tensor_reduce(L[:, c:c + n], S[:, g * BANK:g * BANK + n], alibi(core, 2 * h + 1, t), 1.0, -3e38,
                                            ALU.add, ALU.max, mx[:, g:g + 1])
        core.dve_steps.done(dve, last)
        return self.finish_maxima(dve, mx, 2)

    def weigh(self, dve, u, L, sums):
        core = self.core
        n = causal(u % TT)
        core.dve_steps.done(dve, dve.reciprocal(sums[:, 0:2], sums[:, 0:2]))
        core.dve_steps.done(dve, dve.tensor_tensor(sums[:, 1:2], sums[:, 1:2], self.lam[:], ALU.mult))
        core.dve_steps.done(dve, dve.tensor_scalar(L[:, T:T + n], L[:, T:T + n], sums[:, 1:2], None, ALU.mult))
        return dve.scalar_tensor_tensor(out=L[:, 0:n], in0=L[:, 0:n], scalar=sums[:, 0:1], in1=L[:, T:T + n],
                                        op0=ALU.mult, op1=ALU.subtract)

    def values(self, pe, u, pT, O):
        h, t = u // TT, u % TT
        for j in range(t + 1):
            last = pe.matmul(O[:, 0:P], pT[:, j * P:(j + 1) * P], self.v[:, j, h * P:(h + 1) * P],
                             start=(j == 0), stop=(j == t))
        return last

    def out(self, act, u, O):
        h, t = u // TT, u % TT
        return act.activation(self.o[:, t, h * P:(h + 1) * P], O[:, 0:P], ACT.Copy)


class Stick:

    def __init__(self, core, ctx):
        self.core = core
        self.qT = core.sb(ctx, "qT", [P, KD, T])
        self.kT = core.sb(ctx, "kT", [P, KD, T])
        self.v = core.sb(ctx, "v", [P, TT, D])
        self.oT = core.sb(ctx, "oT", [P, KD, T])
        self.soft = core.sb(ctx, "soft", [P, 2, T])
        self.scan = core.sb(ctx, "scan", [P, 2, T])

    def at(self, u):
        h, t = u // TT, u % TT
        return h, t, slice((h % 2) * DH, (h % 2) * DH + DH)

    def scores(self, u):
        h, t, part = self.at(u)
        n = causal(t)
        return [(0, n, self.qT[part, h // 2, t * P:(t + 1) * P], self.kT[part, h // 2, 0:n])]

    def groups(self, u):
        return [(0, causal(u % TT))]

    def tiles(self, u):
        return [(j * P, P) for j in range(u % TT + 1)]

    def first(self, act, u, S):
        n = causal(u % TT)
        soft = self.soft[:, u % 2, 0:n]
        steps = self.core.act_steps
        steps.done(act, act.activation(soft, S[:, 0:n], ACT.Abs))
        steps.done(act, act.activation(soft, soft, ACT.Exp, scale=-1.0))
        return act.activation(soft, soft, ACT.Ln, bias=1.0)

    def logits(self, dve, u, S, L, mx):
        core = self.core
        t = u % TT
        n = causal(t)
        soft, scan = self.soft[:, u % 2, 0:n], self.scan[:, u % 2, 0:n]
        steps = core.dve_steps
        steps.done(dve, dve.scalar_tensor_tensor(out=soft, in0=S[:, 0:n], scalar=0.0, in1=soft,
                                                 op0=ALU.max, op1=ALU.add))
        steps.done(dve, dve.tensor_tensor(soft[:, t * P:n], soft[:, t * P:n], core.before[:], ALU.mult))
        steps.done(dve, dve.tensor_tensor_scan(scan, soft, soft, 0.0, ALU.add, ALU.bypass))
        steps.done(dve, dve.tensor_tensor(L[:, 0:n], S[:, 0:n], soft, ALU.subtract))
        steps.done(dve, dve.tensor_tensor(L[:, 0:n], L[:, 0:n], scan, ALU.add))
        return dve.tensor_scalar(L[:, 0:n], L[:, 0:n], scan[:, n - 1:n], 0.0, ALU.subtract, ALU.min)

    def weigh(self, dve, u, L, sums):
        t = u % TT
        part = L[:, t * P:causal(t)]
        return dve.tensor_tensor(part, part, self.core.before[:], ALU.mult)

    def values(self, pe, u, pT, O):
        h, t, part = self.at(u)
        for j in range(t + 1):
            last = pe.matmul(O[part, 0:P], self.v[:, j, h * DH:(h + 1) * DH], pT[:, j * P:(j + 1) * P],
                             start=(j == 0), stop=(j == t))
        return last

    def out(self, act, u, O):
        h, t, part = self.at(u)
        return act.activation(self.oT[part, h // 2, t * P:(t + 1) * P], O[part, 0:P], ACT.Copy)


NSA_PROJ = 11


def nsa_stage(core, j):
    nc = core.nc
    hT = core.hT
    consts, done = core.semaphore_of("nsa_consts"), core.semaphore_of("nsa_gates")
    with ExitStack() as ctx:
        n = NSA(core, ctx)
        with ExitStack() as early:
            srcT = [core.sb(early, f"cmp_src{i}", [P, NSA_KV, T]) for i in range(2)]
            units = [across(core, hT, i, n.qT[:, 2 * i:2 * i + 2, :], DH ** -0.5) for i in range(4)]
            for i in range(2):
                units += [across_twice(core, hT, 4 + i, srcT[i][:])]
            for i, dst in enumerate((n.ksT, n.kwT)):
                units += [across_twice(core, hT, 6 + i, dst[:])]
            units += [along(core, hT, 8, n.vs[:]), along(core, hT, 9, n.vw[:]),
                      along(core, hT, 10, n.gate[:], 3 * NSA_HEADS)]
            projections(core, NSA_PROJ, units)
            compress(core, n, j, srcT)
        attention(core, ctx, n, NSA_HEADS * TT)
        out_projection(core, n.oT)


def compress(core, n, j, srcT):
    nc = core.nc
    consts, blocks = core.semaphore_of("cmp_consts"), core.semaphore_of("cmp_blocks")
    hid, act_h, outs = core.semaphore_of("cmp_hid"), core.semaphore_of("cmp_act"), core.semaphore_of("cmp_outs")
    first = core.w_taken
    nb = NSA_KV * N_CMP
    chunks = CMP_LEN // 2
    with ExitStack() as ctx:
        pe_col = core.sb(ctx, "cmp_pe", [P, 2, chunks])
        w2 = core.sb(ctx, "cmp_w2", [P, 2, 2, DH])
        blk = core.sb(ctx, "cmp_blk", [P, 2, chunks, nb])
        hT = core.sb(ctx, "cmp_hT", [P, 2, 2, nb])
        block = ctx.enter_context(nc.Block())

        @block.sync
        def _(sp):
            sp.dma_start(pe_col[:], core.io["cmp_pe"][j]).then_inc(consts.sem, 16)
            sp.dma_start(w2[:], core.io["cmp_w2"][j]).then_inc(consts.sem, 16)
            core.issue_w(sp, 4)

        @block.vector
        def _(dve):
            dve.wait_ge(consts.sem, consts.at(32))
            for i in range(2):
                for c in range(chunks):
                    for up in range(2):
                        part = slice(up * DH, (up + 1) * DH)
                        t0 = 2 * c + up
                        src = srcT[i][part, :, t0:t0 + (N_CMP - 1) * CMP_STRIDE + 1:CMP_STRIDE]
                        dst = blk[part, i, c, :].rearrange("p (g n) -> p g n", g=NSA_KV)
                        last = dve.tensor_scalar(dst, src, pe_col[part, i, c:c + 1], None, ALU.add)
                last.then_inc(blocks.sem, 1)
            for i in range(2):
                dve.wait_ge(outs.sem, outs.at(i + 1))
                if i == 0:
                    dve.tensor_copy(n.kcmpT[:].rearrange("p g n -> p (g n)"), core.ps[:, 4, 0:nb])
                else:
                    for g in range(NSA_KV):
                        dve.tensor_copy(n.vcmp[:, g, :], core.ps[0:N_CMP, 5, g * DH:(g + 1) * DH])

        @block.scalar
        def _(act):
            gate = n.gate[:]
            core.act_steps.done(act, act.activation(gate, gate, ACT.Sigmoid))
            for i in range(2):
                act.wait_ge(hid.sem, hid.at(i + 1))
                for m in range(2):
                    last = act.activation(hT[:, i, m, :], core.ps[:, 2 * i + m, 0:nb], ACT.Gelu_apprx_tanh)
                last.then_inc(act_h.sem, 1)

        @block.tensor
        def _(pe):
            for i in range(2):
                pe.wait_ge(blocks.sem, blocks.at(i + 1))
                for part in range(2):
                    item = first + 2 * i + part
                    core.w_wait(pe, item)
                    w = core.w_item(item)
                    for k in range(KD):
                        for m in range(2):
                            last = pe.matmul(core.ps[:, 2 * i + m, 0:nb], w[:, k, m * P:(m + 1) * P],
                                             blk[:, i, part * KD + k, :],
                                             start=(part == 0 and k == 0), stop=(part == 1 and k == KD - 1))
                    last.then_inc(core.w_used, 1)
                pe.wait_ge(core.w_used, item + 1)
                pe.sem_inc(hid.sem, 1)
            for i in range(2):
                pe.wait_ge(act_h.sem, act_h.at(i + 1))
                if i == 0:
                    for half in range(2):
                        for m in range(2):
                            last = pe.matmul(core.ps[half * DH:(half + 1) * DH, 4, 0:nb], w2[:, 0, m, :],
                                             hT[:, 0, m, :], start=(m == 0), stop=(m == 1))
                else:
                    for g in range(NSA_KV):
                        for m in range(2):
                            last = pe.matmul(core.ps[0:N_CMP, 5, g * DH:(g + 1) * DH],
                                             hT[:, 1, m, g * N_CMP:(g + 1) * N_CMP], w2[:, 1, m, :],
                                             start=(m == 0), stop=(m == 1))
                last.then_inc(outs.sem, 1)

    consts.passed(32)
    for s in (blocks, hid, act_h, outs):
        s.passed(2)


def stick_stage(core):
    with ExitStack() as ctx:
        n = Stick(core, ctx)
        units = [across(core, core.hT, i, n.qT[:, 2 * i:2 * i + 2, :], DH ** -0.5) for i in range(4)]
        units += [across(core, core.hT, 4 + i, n.kT[:, 2 * i:2 * i + 2, :]) for i in range(4)]
        units += [along(core, core.hT, 8 + i, n.v[:, :, i * WN:(i + 1) * WN]) for i in range(4)]
        projections(core, 12, units)
        attention(core, ctx, n, (D // DH) * TT)
        out_projection(core, n.oT)


def diff_stage(core, layer):
    nc = core.nc
    lam_init = 0.8 - 0.6 * float(np.exp(-0.3 * layer))
    consts, lam_sums, lam_exps = core.semaphore_of("diff_consts"), core.semaphore_of("diff_sums"), core.semaphore_of("diff_exps")
    ss, roots = core.semaphore_of("diff_squares"), core.semaphore_of("diff_roots")
    normed, turned = core.semaphore_of("diff_normed"), core.semaphore_of("diff_turned")
    with ExitStack() as ctx:
        n = Diff(core, ctx, lam_init)
        lam_in = core.sb(ctx, "lam_in", [P, 4, DH])
        lam_s = core.sb(ctx, "lam_s", [P, 2])
        junk = core.sb(ctx, "lam_junk", [P, 2, DH])
        g = core.sb(ctx, "subln_g", [P, P])
        units = [across(core, core.hT, i, n.qT[:, 2 * i:2 * i + 2, :], DH ** -0.5) for i in range(4)]
        units += [across(core, core.hT, 4 + i, n.kT[:, 2 * i:2 * i + 2, :]) for i in range(4)]
        units += [along(core, core.hT, 8 + i, n.v[:, :, i * WN:(i + 1) * WN]) for i in range(4)]
        projections(core, 12, units)
        with nc.Block() as block:
            @block.sync
            def _(sp):
                lam_dram = core.io["diff_lam"].rearrange("a n d -> a (n d)")
                sp.dma_start(lam_in[:].rearrange("p n d -> p (n d)"),
                             lam_dram.partition_broadcast(P)).then_inc(consts.sem, 16)
                sp.dma_start(g[:], core.io["subln_g"].partition_broadcast(P)).then_inc(consts.sem, 16)

            @block.vector
            def _(dve):
                dve.wait_ge(consts.sem, consts.at(32))
                for i in range(2):
                    last = dve.tensor_tensor_reduce(junk[:, i, :], lam_in[:, 2 * i, :], lam_in[:, 2 * i + 1, :],
                                                    1.0, 0.0, ALU.mult, ALU.add, lam_s[:, i:i + 1])
                last.then_inc(lam_sums.sem, 1)
                dve.wait_ge(lam_exps.sem, lam_exps.at(1))
                core.dve_steps.done(dve, dve.tensor_tensor(n.lam[:], lam_s[:, 0:1], lam_s[:, 1:2], ALU.subtract))
                dve.tensor_scalar(n.lam[:], n.lam[:], lam_init, None, ALU.add)

            @block.scalar
            def _(act):
                act.wait_ge(lam_sums.sem, lam_sums.at(1))
                act.activation(lam_s[:], lam_s[:], ACT.Exp).then_inc(lam_exps.sem, 1)
        attention(core, ctx, n, DIFF_HEADS * TT)
        oT = n.qT
        with ExitStack() as inner:
            sq = core.sb(inner, "sq", [P, TT, D])
            st = core.sb(inner, "st", [P, 2, TT, DIFF_HEADS])
            block = inner.enter_context(nc.Block())

            @block.vector
            def _(dve):
                o4 = n.o[:].rearrange("p t (h e) -> p t h e", h=DIFF_HEADS)
                sq4 = sq[:].rearrange("p t (h e) -> p t h e", h=DIFF_HEADS)
                core.dve_steps.done(dve, dve.tensor_tensor(sq[:], n.o[:], n.o[:], ALU.mult))
                core.dve_steps.done(dve, dve.tensor_reduce(st[:, 0], sq4, AX.X, ALU.add))
                dve.tensor_scalar(st[:, 0], st[:, 0], 1.0 / P, EPS, ALU.mult, ALU.add).then_inc(ss.sem, 1)
                dve.wait_ge(roots.sem, roots.at(1))
                core.dve_steps.done(dve, dve.reciprocal(st[:, 1], st[:, 0]))
                for t in range(TT):
                    core.dve_steps.done(dve, dve.tensor_tensor(sq4[:, t], o4[:, t], wide(st[:, 1, t, :], P), ALU.mult))
                    gb = bass.AP(g[:].tensor, g[:].offset, [list(g[:].ap[0]), [0, DIFF_HEADS], list(g[:].ap[1])])
                    core.dve_steps.done(dve, dve.scalar_tensor_tensor(
                        out=sq4[:, t], in0=sq4[:, t], scalar=n.keep, in1=gb, op0=ALU.mult, op1=ALU.mult))
                    dve.sem_inc(normed.sem, 1)

            @block.scalar
            def _(act):
                act.wait_ge(ss.sem, ss.at(1))
                act.activation(st[:, 0], st[:, 0], ACT.Sqrt).then_inc(roots.sem, 1)
                for k in range(0, KD, 2):
                    act.wait_ge(turned.sem, turned.at(k // 2 + 1))
                    act.activation(oT[:, k:k + 2, :], core.ps[:, k // 2, :].rearrange("p (k n) -> p k n", k=2),
                                   ACT.Copy)

            @block.tensor
            def _(pe):
                pe.wait_ge(normed.sem, normed.at(TT))
                for k in range(KD):
                    for t in range(TT):
                        last = pe.transpose(core.ps[:, k // 2, (k % 2) * T + t * P:(k % 2) * T + (t + 1) * P],
                                            sq[:, t, k * P:(k + 1) * P], core.ident[:])
                    if k % 2:
                        last.then_inc(turned.sem, 1)
        out_projection(core, oT)
    consts.passed(32)
    for s in (lam_sums, lam_exps, ss, roots):
        s.passed(1)
    normed.passed(TT)
    turned.passed(KD // 2)


def second_block(core):
    taken = {"nsa": 0}
    with ExitStack() as ctx:
        core.alibi = core.sb(ctx, "alibi", [P, NSA_HEADS, P + T])
        core.cmp_bias = core.sb(ctx, "cmp_bias", [P, NSA_HEADS, TT, N_CMP])
        core.cmp_valid = core.sb(ctx, "cmp_valid", [P, TT, N_CMP])
        core.before = core.sb(ctx, "before", [P, P])
        tables = core.semaphore_of("attention_tables")
        with core.nc.Block() as block:
            @block.scalar
            def _(act):
                act.dma_start(core.alibi[:], core.io["alibi"]).then_inc(tables.sem, 16)
                act.dma_start(core.cmp_bias[:], core.io["cmp_bias"]).then_inc(tables.sem, 16)
                act.dma_start(core.cmp_valid[:], core.io["cmp_valid"]).then_inc(tables.sem, 16)
                act.dma_start(core.before[:], core.io["before"]).then_inc(tables.sem, 16)
                act.wait_ge(tables.sem, tables.at(64))
        tables.passed(64)
        norm_stage(core, None, 0)
        for layer, kind in enumerate(MIXERS):
            last = layer == DEPTH - 1
            ffn_stage(core, False)
            norm_stage(core, 0, 1)
            if kind == "nsa":
                nsa_stage(core, taken["nsa"])
                taken["nsa"] += 1
            elif kind == "stick":
                stick_stage(core)
            else:
                diff_stage(core, layer)
            norm_stage(core, 1, 2)
            with ExitStack() as mod:
                if not last:
                    core.acc = core.sb(mod, "mod_acc", [P, MOD_COLS])
                ffn_stage(core, not last)
                norm_stage(core, 2, None)
                if not last:
                    mod_stage(core, layer + 1, core.acc)
            if not last:
                norm_stage(core, None, 0)


def w_items(w):
    n = w.shape[1] // WN
    return w.reshape(KD, P, n, WN).transpose(2, 1, 0, 3).reshape(n, P, ITEM)


def padded(w):
    n = -w.shape[1] % WN
    return np.concatenate([w, np.zeros((w.shape[0], n), w.dtype)], 1) if n else w


def ffn_items(w1, w2):
    gate, up = w_items(w1[:, :D_FF]), w_items(w1[:, D_FF:])
    down = w2.reshape(FF_STEPS, 2, P, D).transpose(0, 2, 1, 3).reshape(FF_STEPS, P, ITEM)
    order = [gate[:1], up[:1]]
    for s in range(FF_STEPS - 1):
        order += [gate[s + 1:s + 2], up[s + 1:s + 2], down[s:s + 1]]
    return order + [down[FF_STEPS - 1:]]


def mod_items(w, b):
    n = w.shape[1] // WN
    out = np.zeros((n, P, KD + 1, WN), w.dtype)
    out[:, :, :KD] = w.reshape(KD, P, n, WN).transpose(2, 1, 0, 3)
    out[:, 0, KD] = b.reshape(n, WN)
    return out.reshape(n, P, A_ITEM)


def columns_of(v):
    return np.ascontiguousarray(np.swapaxes(v.reshape(*v.shape[:-1], v.shape[-1] // P, P), -1, -2))


def attention_tables():
    q = np.arange(P)[:, None]
    alibi = np.zeros((P, NSA_HEADS, P + T), np.float32)
    cmp_bias = np.zeros((P, NSA_HEADS, TT, N_CMP), np.float32)
    cmp_valid = np.zeros((P, TT, N_CMP), np.float32)
    ends = np.arange(N_CMP)[None, :] * CMP_STRIDE + CMP_LEN - 1
    for t in range(TT):
        dist = (q + t * P - np.arange(causal(t))[None, :]).astype(np.float32)
        near = (q + t * P - ends).astype(np.float32)
        cmp_valid[:, t] = near >= 0
        for h in range(NSA_HEADS):
            slope = np.float32(SLOPES[h])
            alibi[:, h, t * P:t * P + causal(t)] = np.where(dist >= 0, -slope * dist, np.float32(NEG))
            cmp_bias[:, h, t] = np.where(near >= 0, -slope * near, np.float32(NEG))
    before = (np.arange(P)[None, :] < q).astype(np.float32)
    return {"alibi": alibi, "cmp_bias": cmp_bias, "cmp_valid": cmp_valid, "before": before,
            "ident": np.eye(P, dtype=np.float32)}


def second_layout(a):
    w = []
    nsa = 0
    for layer, kind in enumerate(MIXERS):
        w += ffn_items(a["ffn_w1_2"][layer, 0], a["ffn_w2_2"][layer, 0])
        if kind == "nsa":
            cols = a["nsa_w_in_2"][nsa]
            main = NSA_HEADS * DH + 6 * NSA_KV * DH
            q, kc, vc, ks, vs, kw, vw = np.split(cols[:, :main], [1024 + 256 * i for i in range(6)], 1)
            gates = cols[:, main:].reshape(D, NSA_HEADS, 3)[:, :, [1, 2, 0]].reshape(D, 3 * NSA_HEADS)
            w += [w_items(x) for x in (q, kc, vc, ks, kw, vs, vw, padded(gates))]
            w += [a["nsa_cmp_w1_2"][nsa].reshape(2, 2, KD, P, CMP_HID).transpose(0, 1, 3, 2, 4).reshape(4, P, ITEM)]
            w += [w_items(a["nsa_w_out_2"][nsa])]
            nsa += 1
        else:
            name = "sb" if kind == "stick" else "diff"
            w += [w_items(a[name + "_w_in_2"][0]), w_items(a[name + "_w_out_2"][0])]
        w += ffn_items(a["ffn_w1_2"][layer, 1], a["ffn_w2_2"][layer, 1])
    norm = a["norm_g_2"]
    mods = np.concatenate([mod_items(a["ada_w_2"][i], a["ada_b_2"][i]) for i in range(DEPTH)])
    small = {
        "norm_pre": np.ascontiguousarray(columns_of(norm[:, 0::2]).transpose(2, 0, 1, 3)),
        "norm_post": np.ascontiguousarray(columns_of(norm[:, 1::2]).transpose(2, 0, 1, 3)),
        "cond2_in": columns_of(a["c_2"][0]),
        "cmp_pe": np.ascontiguousarray(
            a["nsa_cmp_pe_2"].reshape(-1, 2, CMP_LEN // 2, 2, DH).transpose(0, 3, 4, 1, 2).reshape(-1, P, 2, CMP_LEN // 2)),
        "cmp_w2": np.ascontiguousarray(a["nsa_cmp_w2_2"].reshape(-1, 2, 2, P, DH).transpose(0, 3, 1, 2, 4)),
        "diff_lam": np.ascontiguousarray(a["diff_lam_2"]),
        "subln_g": np.ascontiguousarray(a["diff_subln_g_2"]),
    }
    return w, mods, small


RW_W = 256
RW_H = RW_W // DH
CHUNK = 64
NCH = 2 * T // CHUNK
LEVELS = 6
LOG_DECAY = -float(np.exp(-0.5))
ROOT_EPS = 1e-12


def heads(ap):
    return ap.rearrange("p (h n) -> p h n", h=RW_H)


def spread(ap, n):
    return bass.AP(ap.tensor, ap.offset, [list(ap.ap[0]), [0, n]] + [list(x) for x in ap.ap[1:]])


def place_of(t, c, d):
    n = 2 * (t % TT) + c
    return NCH // 2 * (t // TT) + (NCH // 2 - 1 - n if d else n)


class Recurrence:

    def __init__(self, core, ctx):
        sb = lambda name, shape: core.sb(ctx, name, shape)
        self.psi = sb("psi", [P, NCH, RW_H, DH])
        self.gamma = sb("gamma", [P, NCH, RW_H, DH])
        self.p_end = sb("p_end", [P, NCH, RW_H])
        self.state = sb("state", [P, NCH + 1, RW_H, DH])
        self.qT = sb("rw_qT", [P, TT, RW_H, P])
        self.y = sb("rw_y", [P, TT, RW_W])
        self.masks = sb("rw_masks", [P, 2, 4 + LEVELS, P])
        self.chunk_sum = sb("chunk_sum", [P, 2])
        self.w0a0 = sb("w0a0", [P, 2, 2 * RW_W])
        self.rows = sb("rw_rows", [P, 4, RW_W])
        self.up = sb("rw_up", [P, 2, RW_W])


def rw_tile_stage(core, rw, a, t):
    nc = core.nc
    is_x = t >= TT
    names = ("kk_root", "kk_done", "wa_up", "wa_in", "wa_out", "cums", "p_ready", "ends", "nats", "turn1", "turn1_out",
             "tri", "tri_out", "lvl_in", "lvl_z", "lvl_z_out", "lvl_x", "lvl_x_out", "cv", "cv_out",
             "mg", "mg_out", "maps", "maps_out", "kk_sum")
    s = {n: core.semaphore_of("rw_" + n) for n in names}
    with ExitStack() as ctx:
        early = core.sb(ctx, "early", [P, 2, 6 * RW_W])
        late = early
        kk = core.sb(ctx, "kk", [P, 2, RW_W])
        st = core.sb(ctx, "kk_st", [P, RW_H])
        bx = core.sb(ctx, "bx", [P, 2, 2, RW_W])
        kc = core.sb(ctx, "kc", [P, 2, RW_H, P])
        mg = core.sb(ctx, "mg", [P, 2, RW_H, P])
        chT = core.sb(ctx, "chT", [P, 4, RW_H, P])
        tri = core.sb(ctx, "tri", [P, 2, 4, RW_H, P])
        block = ctx.enter_context(nc.Block())
        n_ch = 4 if is_x else 3

        def wa(d):
            return early[:, d, 0:2 * RW_W]

        def decay(d, which):
            return early[:, d, (2 + which) * RW_W:(3 + which) * RW_W]

        def tmp(d):
            return early[:, d, 5 * RW_W:6 * RW_W]

        def lvl(d, which):
            return late[:, d, which * BANK:(which + 1) * BANK].rearrange("p (h n) -> p h n", h=RW_H)

        def bank(i):
            return core.ps[:, i, :].rearrange("p (h n) -> p h n", h=RW_H)

        def part(d):
            return slice(d * DH, (d + 1) * DH)

        tok = slice(t * P, (t + 1) * P)

        @block.sync
        def _(sp):
            core.issue_w(sp, 0)

        @block.scalar
        def _(act):
            act.wait_ge(s["kk_sum"].sem, s["kk_sum"].at(1))
            act.activation(st[:], st[:], ACT.Sqrt).then_inc(s["kk_root"].sem, 1)
            for d in range(2):
                act.wait_ge(s["wa_in"].sem, s["wa_in"].at(d + 1))
                act.activation(wa(d), wa(d), ACT.Sigmoid).then_inc(s["wa_out"].sem, 1)
            for d in range(2):
                act.wait_ge(s["cums"].sem, s["cums"].at(d + 1))
                act.activation(early[:, d, 2 * RW_W:4 * RW_W], core.ps[:, 2 + d, :], ACT.Exp)
                act.activation(decay(d, 2), core.ps[:, 2 + d, 0:RW_W], ACT.Exp, scale=-1.0)
                for c in range(2):
                    last = act.activation(rw.p_end[part(d), place_of(t, c, d), :],
                                          core.ps[part(d), 4 + d, c:c + 2 * RW_H - 1:2], ACT.Exp)
                last.then_inc(s["p_ready"].sem, 1)
            for d in range(2):
                for i in range(n_ch):
                    n = n_ch * d + i
                    act.wait_ge(s["turn1"].sem, s["turn1"].at(n + 1))
                    act.activation(chT[part(d), i, :, :], bank(4 + i)[0:DH], ACT.Copy).then_inc(
                        s["turn1_out"].sem, 1)
            for level in range(LEVELS):
                for d in range(2):
                    n = 2 * level + d
                    act.wait_ge(s["lvl_z"].sem, s["lvl_z"].at(n + 1))
                    act.activation(lvl(d, 2), bank(4 * d), ACT.Copy).then_inc(s["lvl_z_out"].sem, 1)
            for d in range(2):
                act.wait_ge(s["cv"].sem, s["cv"].at(d + 1))
                act.activation(kc[:, d, :, DH:P], heads(core.ps[:, 4 * d, 0:RW_W]), ACT.Copy).then_inc(
                    s["cv_out"].sem, 1)
            for d in range(2):
                act.wait_ge(s["mg"].sem, s["mg"].at(d + 1))
                act.activation(mg[:, d, :, :], bank(4 * d + 1), ACT.Copy, scale=-1.0).then_inc(
                    s["mg_out"].sem, 1)

        @block.vector
        def _(dve):
            steps = core.dve_steps
            k, v = a.k[:, t, :], a.v[:, t, :]
            kk_raw, kk_n = kk[:, 0, :], kk[:, 1, :]
            steps.done(dve, dve.tensor_tensor(kk_raw, k, rw.rows[:, 0, :], ALU.mult))
            steps.done(dve, dve.tensor_tensor(kk_n, kk_raw, kk_raw, ALU.mult))
            steps.done(dve, dve.tensor_reduce(st[:], heads(kk_n), AX.X, ALU.add))
            dve.tensor_scalar(st[:], st[:], ROOT_EPS, None, ALU.add).then_inc(s["kk_sum"].sem, 1)
            for d in range(2):
                dve.wait_ge(s["wa_up"].sem, s["wa_up"].at(d + 1))
                dve.tensor_tensor(wa(d), core.ps[:, d, :], rw.w0a0[:, d, :], ALU.add).then_inc(s["wa_in"].sem, 1)
            dve.wait_ge(s["kk_root"].sem, s["kk_root"].at(1))
            steps.done(dve, dve.reciprocal(st[:], st[:]))
            steps.done(dve, dve.tensor_tensor(heads(kk_n), heads(kk_raw), wide(st[:], DH), ALU.mult))
            for d in range(2):
                dve.wait_ge(s["p_ready"].sem, s["p_ready"].at(d + 1))
                a_in = wa(d)[:, RW_W:]
                dve.tensor_tensor(kc[:, d, :, 0:DH], heads(decay(d, 1)), heads(kk_n), ALU.mult)
                steps.done(dve, dve.tensor_tensor(tmp(d), kk_n, a_in, ALU.mult))
                steps.done(dve, dve.tensor_tensor(bx[:, d, 0, :], tmp(d), decay(d, 2), ALU.mult))
                steps.done(dve, dve.scalar_tensor_tensor(out=tmp(d), in0=a_in, scalar=-1.0, in1=rw.rows[:, 1, :],
                                                         op0=ALU.add, op1=ALU.mult))
                steps.done(dve, dve.scalar_tensor_tensor(out=tmp(d), in0=tmp(d), scalar=1.0, in1=k,
                                                         op0=ALU.add, op1=ALU.mult))
                last = dve.tensor_tensor(bx[:, d, 1, :], tmp(d), decay(d, 2), ALU.mult)
                if is_x:
                    steps.done(dve, last)
                    last = dve.tensor_tensor(decay(d, 0), decay(d, 0), a.r[:, t - TT, :], ALU.mult)
                last.then_inc(s["nats"].sem, 1)
            for d in range(2):
                for i in range(4 if is_x else 2):
                    n = (4 if is_x else 2) * d + i
                    dve.wait_ge(s["tri"].sem, s["tri"].at(n + 1))
                    dve.tensor_tensor(tri[:, d, i, :, :], bank(4 * d + i), spread(rw.masks[:, d, i // 2, :], RW_H),
                                      ALU.mult).then_inc(s["tri_out"].sem, 1)
            dve.wait_ge(s["turn1"].sem, s["turn1"].at(2 * n_ch))
            for d in range(2):
                for i in range(2):
                    last = dve.tensor_copy(lvl(d, i), spread(core.ident[:], RW_H))
            steps.done(dve, last)
            for level in range(LEVELS):
                for d in range(2):
                    n = 2 * level + d
                    if level == 0:
                        dve.wait_ge(s["tri_out"].sem, s["tri_out"].at((4 if is_x else 2) * d + 1))
                    else:
                        dve.wait_ge(s["lvl_x"].sem, s["lvl_x"].at(n - 1))
                        for i in range(2):
                            dve.tensor_tensor(lvl(d, i), lvl(d, i), bank(4 * d + 1 + i), ALU.subtract)
                    dve.tensor_tensor(lvl(d, 2), tri[:, d, 0, :, :], spread(rw.masks[:, d, 4 + level, :], RW_H),
                                      ALU.mult).then_inc(s["lvl_in"].sem, 1)
            for d in range(2):
                dve.wait_ge(s["lvl_x"].sem, s["lvl_x"].at(2 * LEVELS - 1 + d))
                dve.tensor_tensor(lvl(d, 1), lvl(d, 1), bank(4 * d + 2), ALU.subtract).then_inc(
                    s["lvl_x_out"].sem, 1)
            for d in range(2):
                dve.wait_ge(s["maps"].sem, s["maps"].at(d + 1))
                for c in range(2):
                    n = place_of(t, c, d)
                    eye = core.ident[part(d), d * DH:(d + 1) * DH]
                    src = core.ps[part(d), 4 * d + c, :]
                    dve.tensor_tensor(rw.psi[part(d), n, :, :], heads(src[:, 0:RW_W]), spread(eye, RW_H), ALU.add)
                    last = dve.tensor_copy(rw.gamma[part(d), n, :, :], heads(src[:, RW_W:]))
                if is_x:
                    x = t - TT
                    dve.tensor_tensor(rw.qT[part(d), x, :, :], bank(4 * d + 2)[part(d)], chT[part(d), 3, :, :], ALU.add)
                    y = core.ps[:, 4 * d + 3, 0:RW_W]
                    if d == 0:
                        last = dve.tensor_copy(rw.y[:, x, :], y)
                        steps.done(dve, last)
                    else:
                        dve.tensor_tensor(rw.y[:, x, :], rw.y[:, x, :], y, ALU.add)

        @block.tensor
        def _(pe):
            for d in range(2):
                for i in range(2):
                    last = pe.matmul(core.ps[:, d, i * RW_W:(i + 1) * RW_W], a.waT[part(d), i, tok],
                                     rw.up[part(d), i, :], start=True, stop=True)
                last.then_inc(s["wa_up"].sem, 1)
            for d in range(2):
                pe.wait_ge(s["wa_out"].sem, s["wa_out"].at(d + 1))
                for h in range(RW_H):
                    pe.matmul(core.ps[part(d), 4 + d, 2 * h:2 * h + 2], early[:, d, h * DH:(h + 1) * DH],
                              rw.chunk_sum[:], start=True, stop=True)
                for i in range(2):
                    last = pe.matmul(core.ps[:, 2 + d, i * RW_W:(i + 1) * RW_W], rw.masks[:, d, 2 + i, :],
                                     early[:, d, 0:RW_W], start=True, stop=True)
                last.then_inc(s["cums"].sem, 1)
            pe.wait_ge(s["p_ready"].sem, s["p_ready"].at(2))
            for d in range(2):
                pe.wait_ge(s["nats"].sem, s["nats"].at(d + 1))
                for i in range(n_ch):
                    if d:
                        pe.wait_ge(s["turn1_out"].sem, s["turn1_out"].at(i + 1))
                    for h in range(RW_H):
                        src = (kc[:, d, h, 0:DH], bx[:, d, 0, h * DH:(h + 1) * DH],
                               bx[:, d, 1, h * DH:(h + 1) * DH], decay(d, 0)[:, h * DH:(h + 1) * DH])[i]
                        last = pe.transpose(core.ps[0:DH, 4 + i, h * P:(h + 1) * P], src, core.ident[:])
                    last.then_inc(s["turn1"].sem, 1)
            for d in range(2):
                pe.wait_ge(s["turn1_out"].sem, s["turn1_out"].at(n_ch * (d + 1)))
                for i in range(4 if is_x else 2):
                    src, dst = ((1, 0), (2, 0), (1, 3), (2, 3))[i]
                    for h in range(RW_H):
                        last = pe.matmul(core.ps[:, 4 * d + i, h * P:(h + 1) * P], chT[part(d), src, h, :],
                                         chT[part(d), dst, h, :], start=True, stop=True)
                    last.then_inc(s["tri"].sem, 1)
            for level in range(LEVELS):
                for d in range(2):
                    n = 2 * level + d
                    if level == 0:
                        pe.wait_ge(s["tri_out"].sem, s["tri_out"].at((4 if is_x else 2) * (d + 1)))
                    pe.wait_ge(s["lvl_in"].sem, s["lvl_in"].at(n + 1))
                    for h in range(RW_H):
                        last = pe.matmul(bank(4 * d)[:, h, :], lvl(d, 2)[:, h, :], lvl(d, 0)[:, h, :],
                                         start=True, stop=True)
                    last.then_inc(s["lvl_z"].sem, 1)
                for d in range(2):
                    n = 2 * level + d
                    pe.wait_ge(s["lvl_z_out"].sem, s["lvl_z_out"].at(n + 1))
                    for h in range(RW_H):
                        pe.matmul(bank(4 * d + 1)[:, h, :], lvl(d, 1)[:, h, :], lvl(d, 2)[:, h, :],
                                  start=True, stop=True)
                        last = pe.matmul(bank(4 * d + 2)[:, h, :], lvl(d, 2)[:, h, :], lvl(d, 1)[:, h, :],
                                         start=True, stop=True)
                    last.then_inc(s["lvl_x"].sem, 1)
            for d in range(2):
                for h in range(RW_H):
                    last = pe.matmul(core.ps[:, 4 * d, h * DH:(h + 1) * DH], tri[:, d, 1, h, :],
                                     a.v[:, t, h * DH:(h + 1) * DH], start=True, stop=True)
                last.then_inc(s["cv"].sem, 1)
            for d in range(2):
                pe.wait_ge(s["cv_out"].sem, s["cv_out"].at(d + 1))
                pe.wait_ge(s["lvl_x_out"].sem, s["lvl_x_out"].at(d + 1))
                for h in range(RW_H):
                    last = pe.matmul(bank(4 * d + 1)[:, h, :], lvl(d, 1)[:, h, :], kc[:, d, h, :],
                                     start=True, stop=True)
                last.then_inc(s["mg"].sem, 1)
            for d in range(2):
                pe.wait_ge(s["mg_out"].sem, s["mg_out"].at(d + 1))
                if is_x:
                    for h in range(RW_H):
                        pe.matmul(core.ps[part(d), 4 * d + 2, h * P:(h + 1) * P], mg[:, d, h, 0:DH],
                                  tri[:, d, 2, h, :], start=True, stop=True)
                    for h in range(RW_H):
                        y = core.ps[:, 4 * d + 3, h * DH:(h + 1) * DH]
                        pe.matmul(y, tri[:, d, 3, h, :], a.v[:, t, h * DH:(h + 1) * DH], start=True, stop=False)
                        pe.matmul(y, tri[:, d, 2, h, :], mg[:, d, h, DH:P], start=False, stop=True)
                for c in range(2):
                    ch = slice(c * CHUNK, (c + 1) * CHUNK)
                    for h in range(RW_H):
                        hd = slice(h * DH, (h + 1) * DH)
                        pe.matmul(core.ps[part(d), 4 * d + c, hd], mg[ch, d, h, 0:DH], bx[ch, d, 0, hd],
                                  start=True, stop=True)
                    for h in range(RW_H):
                        hd = slice(h * DH, (h + 1) * DH)
                        dst = core.ps[part(d), 4 * d + c, RW_W + h * DH:RW_W + (h + 1) * DH]
                        pe.matmul(dst, bx[ch, d, 1, hd], a.v[ch, t, hd], start=True, stop=False)
                        last = pe.matmul(dst, bx[ch, d, 0, hd], mg[ch, d, h, DH:P], start=False, stop=True)
                    core.pe_steps.done(pe, last)
                pe.sem_inc(s["maps"].sem, 1)

    for n in ("kk_root", "kk_sum"):
        s[n].passed(1)
    for n in ("wa_up", "wa_in", "wa_out", "cums", "p_ready", "nats", "cv", "cv_out", "mg", "mg_out", "maps",
              "lvl_x_out"):
        s[n].passed(2)
    for n in ("turn1", "turn1_out"):
        s[n].passed(2 * n_ch)
    for n in ("tri", "tri_out"):
        s[n].passed(8 if is_x else 4)
    for n in ("lvl_in", "lvl_z", "lvl_z_out", "lvl_x"):
        s[n].passed(2 * LEVELS)


def rw_chain_stage(core, rw):
    nc = core.nc
    moved = [core.semaphore_of(f"state_moved{d}") for d in range(2)]
    kept = [core.semaphore_of(f"state_kept{d}") for d in range(2)]
    y_done = core.semaphore_of("rw_y_done")

    def part(d):
        return slice(d * DH, (d + 1) * DH)

    with nc.Block() as block:
        @block.sync
        def _(sp):
            core.issue_w(sp, 0)

        @block.tensor
        def _(pe):
            for n in range(1, NCH):
                for d in range(2):
                    pe.wait_ge(kept[d].sem, kept[d].at(n))
                    for h in range(RW_H):
                        last = pe.matmul(core.ps[part(d), d, h * DH:(h + 1) * DH], rw.psi[part(d), n, h, :],
                                         rw.state[part(d), n, h, :], start=True, stop=True)
                    last.then_inc(moved[d].sem, 1)
            for d in range(2):
                for x in range(TT):
                    for c in range(2):
                        n = place_of(TT + x, c, d)
                        for h in range(RW_H):
                            last = pe.matmul(
                                core.ps[c * CHUNK:(c + 1) * CHUNK, 2 + d, x * RW_W + h * DH:x * RW_W + (h + 1) * DH],
                                rw.qT[part(d), x, h, c * CHUNK:(c + 1) * CHUNK], rw.state[part(d), n, h, :],
                                start=True, stop=True)
                last.then_inc(y_done.sem, 1)

        @block.vector
        def _(dve):
            for n in range(NCH):
                for d in range(2):
                    new = rw.state[part(d), n + 1, :, :]
                    end = wide(rw.p_end[part(d), n, :], DH)
                    src = rw.gamma[part(d), n, :, :]
                    if n:
                        dve.wait_ge(moved[d].sem, moved[d].at(n))
                        core.dve_steps.done(dve, dve.tensor_tensor(
                            new, heads(core.ps[part(d), d, 0:RW_W]), src, ALU.add))
                        src = new
                    dve.tensor_tensor(new, src, end, ALU.mult).then_inc(kept[d].sem, 1)
            for d in range(2):
                dve.wait_ge(y_done.sem, y_done.at(d + 1))
                core.dve_steps.done(dve, dve.tensor_tensor(
                    rw.y[:], rw.y[:], core.ps[:, 2 + d, :].rearrange("p (t n) -> p t n", t=TT), ALU.add))

    for d in range(2):
        moved[d].passed(NCH - 1)
        kept[d].passed(NCH)
    y_done.passed(2)


def rw_output_stage(core, rw, a, outT):
    nc = core.nc
    gate, gates = core.semaphore_of("rw_gate"), core.semaphore_of("rw_gates")
    var, root = core.semaphore_of("rw_var"), core.semaphore_of("rw_root")
    done, turned = core.semaphore_of("rw_done"), core.semaphore_of("rw_turned")
    consts = core.semaphore_of("rw_g_up")
    with ExitStack() as ctx:
        g_up = core.sb(ctx, "g_up", [P, RW_W])
        sq = core.sb(ctx, "rw_sq", [P, TT, RW_W])
        bonus = core.sb(ctx, "rw_bonus", [P, TT, RW_W])
        st = core.sb(ctx, "rw_st", [P, 3, TT * RW_H])
        block = ctx.enter_context(nc.Block())

        def by_head(ap):
            return ap.rearrange("p t (h n) -> p (t h) n", h=RW_H)

        def rows(i):
            return spread(rw.rows[:, i, :], TT)

        @block.sync
        def _(sp):
            sp.dma_start(g_up[:], core.io["rw_g_up"]).then_inc(consts.sem, 16)

        @block.scalar
        def _(act):
            act.activation(a.gT[:], a.gT[:], ACT.Sigmoid).then_inc(gate.sem, 1)
            act.wait_ge(var.sem, var.at(1))
            act.activation(st[:, 1, :], st[:, 1, :], ACT.Sqrt).then_inc(root.sem, 1)
            act.wait_ge(turned.sem, turned.at(1))
            act.activation(outT[:, 0:2, :], core.ps[:, 1, :].rearrange("p (k n) -> p k n", k=2), ACT.Copy)

        @block.tensor
        def _(pe):
            pe.wait_ge(gate.sem, gate.at(1))
            pe.wait_ge(consts.sem, consts.at(16))
            for x in range(TT):
                last = pe.matmul(core.ps[:, 0, x * RW_W:(x + 1) * RW_W], a.gT[:, x * P:(x + 1) * P], g_up[:],
                                 start=True, stop=True)
            last.then_inc(gates.sem, 1)
            pe.wait_ge(done.sem, done.at(1))
            for k in range(2):
                for x in range(TT):
                    last = pe.transpose(core.ps[:, 1, k * T + x * P:k * T + (x + 1) * P],
                                        rw.y[:, x, k * P:(k + 1) * P], core.ident[:])
            last.then_inc(turned.sem, 1)

        @block.vector
        def _(dve):
            do = lambda ins: core.dve_steps.done(dve, ins)
            y = by_head(rw.y[:])
            do(dve.tensor_reduce(st[:, 0, :], y, AX.X, ALU.add))
            do(dve.tensor_scalar(st[:, 0, :], st[:, 0, :], 1.0 / DH, None, ALU.mult))
            do(dve.tensor_tensor(y, y, wide(st[:, 0, :], DH), ALU.subtract))
            do(dve.tensor_tensor(sq[:], rw.y[:], rw.y[:], ALU.mult))
            do(dve.tensor_reduce(st[:, 1, :], by_head(sq[:]), AX.X, ALU.add))
            dve.tensor_scalar(st[:, 1, :], st[:, 1, :], 1.0 / DH, GN_EPS, ALU.mult, ALU.add).then_inc(var.sem, 1)
            do(dve.tensor_tensor(bonus[:], a.r[:], a.k[:, TT:2 * TT, :], ALU.mult))
            do(dve.tensor_tensor(bonus[:], bonus[:], rows(2), ALU.mult))
            do(dve.tensor_reduce(st[:, 2, :], by_head(bonus[:]), AX.X, ALU.add))
            do(dve.tensor_tensor(by_head(bonus[:]), by_head(a.v[:, TT:2 * TT, :]), wide(st[:, 2, :], DH), ALU.mult))
            dve.wait_ge(root.sem, root.at(1))
            do(dve.reciprocal(st[:, 1, :], st[:, 1, :]))
            do(dve.tensor_tensor(y, y, wide(st[:, 1, :], DH), ALU.mult))
            do(dve.tensor_tensor(rw.y[:], rw.y[:], rows(3), ALU.mult))
            do(dve.tensor_tensor(rw.y[:], rw.y[:], bonus[:], ALU.add))
            dve.wait_ge(gates.sem, gates.at(1))
            dve.tensor_tensor(rw.y[:], rw.y[:], core.ps[:, 0, :].rearrange("p (t n) -> p t n", t=TT),
                              ALU.mult).then_inc(done.sem, 1)
    consts.passed(16)
    for x in (gate, gates, var, root, done, turned):
        x.passed(1)


MOD1_ITEMS = 6 * D // WN
NA_HEADS = 8
NA_W = NA_HEADS * DH
GRID = 64
NA_KC = 16
PROJ1 = 14
MOD1_FIRST = 2 * D // WN
CTX_COL = 2 * D


class Mod1:

    def __init__(self, core, ctx):
        self.gain = core.sb(ctx, "gain1", [P, 2, KD])
        self.shift = core.sb(ctx, "shift1", [P, 2, KD])
        self.cols = core.sb(ctx, "cols1", [P, 4, KD])


def mod1_columns_stage(core, m):
    nc = core.nc
    consts, summed = core.semaphore_of("mod1_consts"), core.semaphore_of("mod1_summed")
    with ExitStack() as ctx:
        g = core.sb(ctx, "norm1_g", [P, KD])
        block = ctx.enter_context(nc.Block())

        @block.sync
        def _(sp):
            sp.dma_start(g[:], core.io["norm1_g"]).then_inc(consts.sem, 16)

        @block.tensor
        def _(pe):
            mod_columns(core, pe, core.acc, range(4), 0, 0).then_inc(summed.sem, 1)

        @block.vector
        def _(dve):
            dve.wait_ge(consts.sem, consts.at(16))
            dve.wait_ge(summed.sem, summed.at(1))
            cols = core.ps[:, 0, 0:4 * KD].rearrange("p (w j k) -> p w j k", w=2, j=2)
            dve.tensor_copy(m.shift[:], cols[:, :, 0])
            dve.scalar_tensor_tensor(out=m.gain[:], in0=cols[:, :, 1], scalar=1.0, in1=spread(g[:], 2),
                                     op0=ALU.add, op1=ALU.mult)
    consts.passed(16)
    summed.passed(1)


def mod1_rest_stage(core, m, rest_acc, layer_acc):
    nc = core.nc
    consts, summed = core.semaphore_of("mod1_consts"), core.semaphore_of("mod1_summed")
    with ExitStack() as ctx:
        g = core.sb(ctx, "norm2_g", [P, KD])
        block = ctx.enter_context(nc.Block())

        @block.sync
        def _(sp):
            sp.dma_start(g[:], core.io["norm2_g"]).then_inc(consts.sem, 16)

        @block.tensor
        def _(pe):
            mod_columns(core, pe, layer_acc, range(9), 0, 0).then_inc(summed.sem, 1)
            mod_columns(core, pe, rest_acc, range(4), 0, 1).then_inc(summed.sem, 1)

        @block.vector
        def _(dve):
            dve.wait_ge(summed.sem, summed.at(1))
            shape_columns(core, dve, 0, 0)
            dve.wait_ge(consts.sem, consts.at(16))
            dve.wait_ge(summed.sem, summed.at(2))
            cols = core.ps[:, 1, 0:4 * KD].rearrange("p (v k) -> p v k", v=4)
            core.dve_steps.done(dve, dve.tensor_copy(m.cols[:], cols))
            dve.scalar_tensor_tensor(out=m.cols[:, 2, :], in0=cols[:, 2, :], scalar=1.0, in1=g[:],
                                     op0=ALU.add, op1=ALU.mult)
    consts.passed(16)
    summed.passed(2)


def rows1_stage(core, m):
    wide_out = core.semaphore_of("mod_wide")
    with core.nc.Block() as block:
        @block.sync
        def _(sp):
            core.issue_w(sp, 0)

        @block.tensor
        def _(pe):
            for i in range(8):
                for j in range(4):
                    col = m.cols[:, i // 2, 4 * (i % 2) + j:4 * (i % 2) + j + 1]
                    last = pe.matmul(core.ps[:, i, j * P:(j + 1) * P],
                                     bass.AP(col.tensor, col.offset, [list(col.ap[0]), [0, P]]),
                                     core.ident[:], start=True, stop=True)
                last.then_inc(wide_out.sem, 1)

        def copies(eng, is_act):
            for i in range(0 if is_act else 1, 8, 2):
                eng.wait_ge(wide_out.sem, wide_out.at(i + 1))
                put(eng, is_act, m.rows[:, i // 2, (i % 2) * BANK:(i % 2 + 1) * BANK], core.ps[:, i, :])

        @block.scalar
        def _(act):
            copies(act, True)

        @block.vector
        def _(dve):
            copies(dve, False)
    wide_out.passed(8)


class Projected:

    def __init__(self, core, ctx):
        self.r = core.sb(ctx, "r", [P, TT, RW_W])
        self.k = core.sb(ctx, "k", [P, 2 * TT, RW_W])
        self.v = core.sb(ctx, "v", [P, 2 * TT, RW_W])
        self.waT = core.sb(ctx, "waT", [P, 2, 2 * T])
        self.gT = core.sb(ctx, "gT", [P, T])

    def allocate_short(self, core, short):
        self.qT = core.sb(short, "na_qT", [P, NA_W // P, T])
        self.kT = core.sb(short, "na_kT", [P, NA_W // P, 2 * T])
        self.nv = core.sb(short, "na_v", [P, 2 * TT, NA_W])
        self.sc = core.sb(short, "sc", [P, 3, 2, T])


def first_projections(core, a, hT, hcT, side):
    def unit_g(item):
        return (item, [(P, lambda w, k: w[:, k, 0:P], lambda w, k: hT[:, k, :])],
                lambda eng, is_act, bank: put(eng, is_act, a.gT[:], bank[:, 0:T]))

    units = [along(core, hT, 0, a.r[:])]
    for i, dst in ((1, a.k), (2, a.v)):
        units += [along(core, hcT, i, dst[:, 0:TT, :]), along(core, hT, i, dst[:, TT:2 * TT, :])]
    units += [across(core, hcT, 3, a.waT[:, :, 0:T]), across(core, hT, 3, a.waT[:, :, T:2 * T])]
    units += [unit_g(4)]
    units += [across(core, hT, 5 + i, a.qT[:, 2 * i:2 * i + 2, :], DH ** -0.5) for i in range(2)]
    for i in range(2):
        units += [across(core, hT, 7 + i, a.kT[:, 2 * i:2 * i + 2, 0:T]),
                  across(core, hcT, 7 + i, a.kT[:, 2 * i:2 * i + 2, T:2 * T])]
    for i in range(2):
        units += [along(core, hT, 9 + i, a.nv[:, 0:TT, i * WN:(i + 1) * WN]),
                  along(core, hcT, 9 + i, a.nv[:, TT:2 * TT, i * WN:(i + 1) * WN])]
    units += [across(core, hT, 11 + i, a.sc[:, i, :, :]) for i in range(3)]
    projections(core, PROJ1, units, side)


class Neighbours(Softmax):

    def __init__(self, core, ctx, a, outT):
        self.core, self.a, self.outT = core, a, outT
        self.bias = core.sb(ctx, "na_bias", [P, NA_HEADS, TT, T])

    def at(self, u):
        h, t = u // TT, u % TT
        return h, t, slice((h % 2) * DH, (h % 2) * DH + DH)

    def scores(self, u):
        h, t, part = self.at(u)
        return [(0, 2 * T, self.a.qT[part, h // 2, t * P:(t + 1) * P], self.a.kT[part, h // 2, :])]

    def groups(self, u):
        return [(0, 2 * T)]

    def tiles(self, u):
        return [(j * P, P) for j in range(2 * TT)]

    def logits(self, dve, u, S, L, mx):
        core = self.core
        h, t, _ = self.at(u)
        dve.tensor_tensor_reduce(L[:, 0:T], S[:, 0:T], self.bias[:, h, t, :], 1.0, -3e38, ALU.add, ALU.max,
                                 mx[:, 0:1])
        core.dve_steps.done(dve, dve.tensor_scalar(L[:, T:2 * T], S[:, T:2 * T], 1.0, -3e38, ALU.mult, ALU.max,
                                                   accum_out=mx[:, 1:2]))
        core.dve_steps.done(dve, dve.tensor_tensor(mx[:, 0:1], mx[:, 0:1], mx[:, 1:2], ALU.max))
        return self.finish_maxima(dve, mx, 1)

    def weigh(self, dve, u, L, sums):
        self.core.dve_steps.done(dve, dve.reciprocal(sums[:, 0:1], sums[:, 0:1]))
        return dve.tensor_scalar(L[:, 0:2 * T], L[:, 0:2 * T], sums[:, 0:1], None, ALU.mult)

    def values(self, pe, u, pT, O):
        h, t, part = self.at(u)
        for j in range(2 * TT):
            last = pe.matmul(O[part, 0:P], self.a.nv[:, j, h * DH:(h + 1) * DH], pT[:, j * P:(j + 1) * P],
                             start=(j == 0), stop=(j == 2 * TT - 1))
        return last

    def out(self, act, u, O):
        h, t, part = self.at(u)
        return act.activation(self.outT[part, 2 + h // 2, t * P:(t + 1) * P], O[part, 0:P], ACT.Copy)


def neighbour_stage(core, a, outT):
    nc = core.nc
    loaded, ready = core.semaphore_of("na_loaded"), core.semaphore_of("na_ready")
    with ExitStack() as ctx:
        n = Neighbours(core, ctx, a, outT)
        with ExitStack() as inner:
            w = core.sb(inner, "sc_w", [P, 3, 2])
            u = core.sb(inner, "sc_u", [P, 2, T + 2])
            o = core.sb(inner, "sc_o", [P, 2, T])
            block = inner.enter_context(nc.Block())

            @block.sync
            def _(sp):
                sp.dma_start(n.bias[:], core.io["na_bias"]).then_inc(loaded.sem, 16)
                sp.dma_start(w[:], core.io["sc_w"]).then_inc(ready.sem, 16)
                core.issue_w(sp, 0)

            @block.gpsimd
            def _(pool):
                pool.wait_ge(loaded.sem, loaded.at(16))
                for half in range(P // GRID):
                    part = slice(half * GRID, (half + 1) * GRID)
                    view = n.bias[part].rearrange("p h t (r c) -> p (h t) r c", c=GRID)
                    low, high = view[:, :, :, 0:GRID - NA_KC], view[:, :, :, NA_KC:GRID]
                    groups = NA_HEADS * TT
                    core.pool_steps.done(pool, pool.affine_select(
                        out=low, in_=low, compare_op=ALU.is_ge, fill=NEG, base=NA_KC // 2,
                        pattern=[[0, groups], [0, T // GRID], [1, GRID - NA_KC]], channel_multiplier=-1))
                    core.pool_steps.done(pool, pool.affine_select(
                        out=high, in_=high, compare_op=ALU.is_gt, fill=NEG, base=NA_KC // 2 - NA_KC,
                        pattern=[[0, groups], [0, T // GRID], [-1, GRID - NA_KC]], channel_multiplier=1))

            @block.vector
            def _(dve):
                dve.wait_ge(ready.sem, ready.at(16))
                dve.memset(u[:], 0.0)
                core.dve_steps.done(dve, dve.memset(o[:], 0.0))
                core.dve_steps.done(dve, dve.tensor_tensor(u[:, :, 1:T + 1], a.sc[:, 1], a.sc[:, 2], ALU.mult))
                for tap in range(3):
                    for m in range(2):
                        last = dve.scalar_tensor_tensor(out=o[:, m, :], in0=u[:, m, tap:tap + T],
                                                        scalar=w[:, tap, m:m + 1], in1=o[:, m, :],
                                                        op0=ALU.mult, op1=ALU.add)
                    core.dve_steps.done(dve, last)
                dve.tensor_tensor(outT[:, 6:8, :], o[:], a.sc[:, 0], ALU.mult)
        attention(core, ctx, n, NA_HEADS * TT)
    loaded.passed(16)
    ready.passed(16)


def recurrent_mixer(core, a, outT):
    nc = core.nc
    consts = core.semaphore_of("rw_consts")
    with ExitStack() as ctx:
        rw = Recurrence(core, ctx)
        with nc.Block() as block:
            @block.sync
            def _(sp):
                io = core.io
                sp.dma_start(rw.masks[:], io["rw_masks"]).then_inc(consts.sem, 16)
                sp.dma_start(rw.chunk_sum[:], io["chunk_sum"]).then_inc(consts.sem, 16)
                sp.dma_start(rw.up[:], io["rw_up"]).then_inc(consts.sem, 16)
                sp.dma_start(rw.w0a0[:].rearrange("p d n -> p (d n)"),
                             io["w0a0"].partition_broadcast(P)).then_inc(consts.sem, 16)
                sp.dma_start(rw.rows[:].rearrange("p d n -> p (d n)"),
                             io["rw_rows"].partition_broadcast(P)).then_inc(consts.sem, 16)
                sp.wait_ge(consts.sem, consts.at(80))

            @block.scalar
            def _(act):
                act.activation(a.waT[:, 0, :], a.waT[:, 0, :], ACT.Tanh)

            @block.vector
            def _(dve):
                dve.memset(rw.state[:, 0, :, :], 0.0)
        consts.passed(80)
        for t in range(2 * TT):
            rw_tile_stage(core, rw, a, t)
        rw_chain_stage(core, rw)
        rw_output_stage(core, rw, a, outT)


def mixed_stage(core, m):
    nc = core.nc
    squares, mean = core.semaphore_of("mix_squares"), core.semaphore_of("mix_mean")
    root, rows, turned = core.semaphore_of("mix_root"), core.semaphore_of("mix_rows"), core.semaphore_of("mix_turned")
    with ExitStack() as ctx:
        t_sb = core.sb(ctx, "gated", [P, TT, D])
        ss = core.sb(ctx, "ss1", [P, TT])
        block = ctx.enter_context(nc.Block())
        x = core.x

        @block.vector
        def _(dve):
            do = lambda ins: core.dve_steps.done(dve, ins)
            for i in range(2 * TT):
                t, part = i // 2, slice((i % 2) * BANK, (i % 2 + 1) * BANK)
                do(dve.tensor_tensor(t_sb[:, t, part], core.y[:, i, :], m.rows[:, 0, part], ALU.mult))
            do(dve.tensor_tensor(x[:], x[:], t_sb[:], ALU.add))
            for t in range(TT):
                do(dve.tensor_tensor_reduce(t_sb[:, t, :], x[:, t, :], x[:, t, :], 1.0, 0.0, ALU.mult, ALU.add,
                                            ss[:, t:t + 1]))
            dve.tensor_scalar(ss[:], ss[:], 1.0 / D, EPS, ALU.mult, ALU.add).then_inc(mean.sem, 1)
            dve.wait_ge(root.sem, root.at(1))
            do(dve.reciprocal(ss[:], ss[:]))
            for t in range(TT):
                do(dve.scalar_tensor_tensor(out=core.h2[:, t, :], in0=x[:, t, :], scalar=ss[:, t:t + 1],
                                            in1=m.rows[:, 2, :], op0=ALU.mult, op1=ALU.mult))
                dve.tensor_tensor(core.h2[:, t, :], core.h2[:, t, :], m.rows[:, 1, :],
                                  ALU.add).then_inc(rows.sem, 1)

        @block.scalar
        def _(act):
            act.wait_ge(mean.sem, mean.at(1))
            act.activation(ss[:], ss[:], ACT.Sqrt).then_inc(root.sem, 1)
            for k in range(0, KD, 2):
                act.wait_ge(turned.sem, turned.at(k // 2 + 1))
                act.activation(core.hT[:, k:k + 2, :], core.ps[:, k // 2, :].rearrange("p (k n) -> p k n", k=2),
                               ACT.Copy)

        @block.tensor
        def _(pe):
            pe.wait_ge(rows.sem, rows.at(TT))
            for k in range(KD):
                for t in range(TT):
                    last = pe.transpose(core.ps[:, k // 2, (k % 2) * T + t * P:(k % 2) * T + (t + 1) * P],
                                        core.h2[:, t, k * P:(k + 1) * P], core.ident[:])
                if k % 2:
                    last.then_inc(turned.sem, 1)
    mean.passed(1)
    root.passed(1)
    rows.passed(TT)
    turned.passed(KD // 2)


PEER_H, PEER_KEYS, PEER_TOP = 8, 128, 16
PEER_PAIRS = PEER_H * PEER_TOP
PEER_N = PEER_KEYS * PEER_KEYS
PER_BATCH = 2
G_SLOTS = 8
G_BATCHES = G_SLOTS // PER_BATCH


def peer_topk_stage(core, ctx, idx, gates):
    nc = core.nc
    consts, scored = core.semaphore_of("peer_keys_in"), core.semaphore_of("peer_scored")
    copied = core.semaphore_of("peer_copied")
    shifted, raised = core.semaphore_of("peer_shifted"), core.semaphore_of("peer_raised")
    steps = core.dve_steps
    with ExitStack() as inner:
        qT = core.sb(inner, "peer_qT", [P, 2 * PEER_H, T])
        keys = core.sb(inner, "peer_keys", [P, 2 * PEER_H, PEER_KEYS])
        units = [across(core, core.hT, i, qT[:, 2 * i:2 * i + 2, :]) for i in range(PEER_H)]
        projections(core, PEER_H, units)
        sc = core.sb(inner, "peer_s", [P, 2 * PEER_H, PEER_KEYS])
        top = core.sb(inner, "peer_top", [P, 2 * PEER_H, PEER_TOP])
        top_i = core.sb(inner, "peer_top_i", [P, 2 * PEER_H, PEER_TOP], U32)
        top_f = core.sb(inner, "peer_top_f", [P, 2 * PEER_H, PEER_TOP])
        cand = core.sb(inner, "peer_cand", [P, PEER_H, PEER_TOP * PEER_TOP])
        best = core.sb(inner, "peer_best", [P, PEER_H, PEER_TOP])
        pos = core.sb(inner, "peer_pos", [P, PEER_H, PEER_TOP], U32)
        pos2 = core.sb(inner, "peer_pos2", [P, 2, PEER_PAIRS], U32)
        pos_f = core.sb(inner, "peer_pos_f", [P, 2, PEER_PAIRS])
        hit = core.sb(inner, "peer_hit", [P, PEER_H, PEER_TOP * PEER_TOP])
        count = core.sb(inner, "peer_count", [P, PEER_TOP])
        part_i = core.sb(inner, "peer_part", [P, 2, PEER_PAIRS])
        sums = core.sb(inner, "peer_sums", [P, PEER_H])
        block = inner.enter_context(nc.Block())

        @block.sync
        def _(sp):
            sp.dma_start(keys[:], core.io["peer_keys"]).then_inc(consts.sem, 16)
            sp.dma_start(count[:], core.io["count16"]).then_inc(consts.sem, 16)
            core.issue_w(sp, 0)

        @block.tensor
        def _(pe):
            pe.wait_ge(consts.sem, consts.at(32))
            for t in range(TT):
                for b in range(4):
                    if t:
                        pe.wait_ge(copied.sem, copied.at(b + 1))
                    for i in range(4):
                        last = pe.matmul(core.ps[:, b, i * P:(i + 1) * P], qT[:, 4 * b + i, t * P:(t + 1) * P],
                                         keys[:, 4 * b + i, :], start=True, stop=True)
                    last.then_inc(scored.sem, 1)

        @block.scalar
        def _(act):
            for t in range(TT):
                act.wait_ge(shifted.sem, shifted.at(t + 1))
                act.activation(gates[:, t, :], gates[:, t, :], ACT.Exp).then_inc(raised.sem, 1)

        @block.vector
        def _(dve):
            def do(ins):
                steps.done(dve, ins)

            def top16(values, out, out_i, n):
                for half in range(2):
                    cols = slice(8 * half, 8 * half + 8)
                    for r in range(n):
                        last = dve.max(out[:, r, cols], values[:, r, :])
                    do(last)
                    for r in range(n):
                        last = dve.max_index(out_i[:, r, cols], out[:, r, cols], values[:, r, :])
                    do(last)
                    if half == 0:
                        for r in range(n):
                            last = dve.match_replace(values[:, r, :], out[:, r, cols], values[:, r, :], -3e38)
                        do(last)

            for t in range(TT):
                for b in range(4):
                    dve.wait_ge(scored.sem, scored.at(4 * t + b + 1))
                    last = dve.tensor_copy(sc[:, 4 * b:4 * b + 4, :],
                                           core.ps[:, b, :].rearrange("p (i n) -> p i n", i=4))
                    last.then_inc(copied.sem, 1)
                dve.wait_ge(copied.sem, copied.at(4 * t + 4))
                top16(sc, top, top_i, 2 * PEER_H)
                do(dve.tensor_copy(top_f[:], top_i[:]))
                for h in range(PEER_H):
                    last = dve.tensor_tensor(cand[:, h, :].rearrange("p (a b) -> p a b", a=PEER_TOP),
                                             wide(top[:, 2 * h, :], PEER_TOP),
                                             spread(top[:, 2 * h + 1, :], PEER_TOP), ALU.add)
                do(last)
                top16(cand, best, pos, PEER_H)
                flat = pos[:].rearrange("p h k -> p (h k)")
                dve.tensor_scalar(pos2[:, 0, :], flat, 4, None, ALU.logical_shift_right)
                do(dve.tensor_scalar(pos2[:, 1, :], flat, PEER_TOP - 1, None, ALU.bitwise_and))
                do(dve.tensor_copy(pos_f[:], pos2[:]))
                for half in range(2):
                    for h in range(PEER_H):
                        place = wide(pos_f[:, half, h * PEER_TOP:(h + 1) * PEER_TOP], PEER_TOP)
                        view = hit[:, h, :].rearrange("p (k a) -> p k a", a=PEER_TOP)
                        last = dve.tensor_tensor(view, place, spread(count[:], PEER_TOP), ALU.is_equal)
                    do(last)
                    for h in range(PEER_H):
                        view = hit[:, h, :].rearrange("p (k a) -> p k a", a=PEER_TOP)
                        last = dve.tensor_tensor(view, view, spread(top_f[:, 2 * h + half, :], PEER_TOP), ALU.mult)
                    do(last)
                    do(dve.tensor_reduce(part_i[:, half, :],
                                         hit[:].rearrange("p h (k a) -> p (h k) a", a=PEER_TOP), AX.X, ALU.add))
                do(dve.scalar_tensor_tensor(out=part_i[:, 0, :], in0=part_i[:, 0, :], scalar=float(PEER_KEYS),
                                            in1=part_i[:, 1, :], op0=ALU.mult, op1=ALU.add))
                dve.tensor_copy(idx[:, t, :], part_i[:, 0, :])
                g = gates[:, t, :].rearrange("p (h k) -> p h k", h=PEER_H)
                dve.tensor_tensor(g, best[:], wide(best[:, :, 0], PEER_TOP), ALU.subtract).then_inc(shifted.sem, 1)
                dve.wait_ge(raised.sem, raised.at(t + 1))
                do(dve.tensor_reduce(sums[:], g, AX.X, ALU.add))
                do(dve.reciprocal(sums[:], sums[:]))
                do(dve.tensor_tensor(g, g, wide(sums[:], PEER_TOP), ALU.mult))
    consts.passed(32)
    scored.passed(8)
    copied.passed(8)
    shifted.passed(TT)
    raised.passed(TT)


def peer_experts_stage(core, m, idx, gates):
    nc = core.nc
    landed = [core.semaphore_of(f"rows_landed{s}") for s in range(G_SLOTS)]
    asked = core.semaphore_of("rows_asked")
    freed, dots, acts = core.semaphore_of("rows_freed"), core.semaphore_of("dots_ready"), core.semaphore_of("acts_ready")
    batches = PEER_PAIRS // PER_BATCH
    turns = (batches - 1) // G_BATCHES
    steps = core.dve_steps
    with ExitStack() as ctx:
        rows = core.sb(ctx, "expert_rows", [P, G_SLOTS, 2 * D])
        col = core.sb(ctx, "expert_col", [P, G_SLOTS], U32)
        dot = core.sb(ctx, "expert_dot", [P, G_BATCHES, PER_BATCH])
        coef = core.sb(ctx, "expert_coef", [P, G_BATCHES, PER_BATCH])
        junk = core.sb(ctx, "expert_junk", [P, 2, D])
        acc = core.sb(ctx, "expert_sum", [P, TT, D])
        block = ctx.enter_context(nc.Block())

        @block.gpsimd
        def _(pool):
            def gather(t, slot, n, wait):
                if wait is not None:
                    pool.wait_ge(freed.sem, wait)
                core.pool_steps.done(pool, pool.tensor_copy(col[:, slot:slot + 1], idx[:, t, n]))
                pool.sem_inc(asked.sem, 1)
                pool.indirect_dma_start(rows[:, slot, :], None, core.io["experts"],
                                        bass.IndirectOffsetOnAxis(ap=col[:, slot:slot + 1], axis=0)).then_inc(
                                            landed[slot].sem, 16)

            for t in range(TT):
                if t == 0:
                    for slot in range(G_SLOTS):
                        gather(0, slot, slice(slot, slot + 1), None)
                first = 1 if t == 0 else 0
                with core.pool_steps.loop(pool, PEER_PAIRS // G_SLOTS - first, G_SLOTS) as i:
                    for slot in range(G_SLOTS):
                        gather(t, slot, bass.ds(i * G_SLOTS + (first * G_SLOTS + slot), 1),
                               i * G_SLOTS + freed.at(t * PEER_PAIRS + (first - 1) * G_SLOTS + slot + 1))

        @block.scalar
        def _(act):
            with act.Fori(0, TT * batches // G_BATCHES, 1) as i:
                for b in range(G_BATCHES):
                    act.wait_ge(dots.sem, i * G_BATCHES + dots.at(b + 1))
                    act.activation(coef[:, b, :], dot[:, b, :], ACT.Gelu_apprx_tanh).then_inc(acts.sem, 1)

        @block.vector
        def _(dve):
            dve.memset(acc[:], 0.0)

            def products(t, b, i=0):
                for e in range(PER_BATCH):
                    slot = (b * PER_BATCH + e) % G_SLOTS
                    turn = t * PEER_PAIRS // G_SLOTS + (b * PER_BATCH + e) // G_SLOTS + 1
                    dve.wait_ge(landed[slot].sem, (i + turn) * 16 + landed[slot].base)
                    ins = dve.tensor_tensor_reduce(junk[:, e, :], rows[:, slot, 0:D], core.h2[:, t, :], 1.0, 0.0,
                                                   ALU.mult, ALU.add, dot[:, b % G_BATCHES, e:e + 1])
                    if e < PER_BATCH - 1:
                        continue
                    ins.then_inc(dots.sem, 1)
                dve.wait_ge(dots.sem, i * G_BATCHES + dots.at(t * batches + b + 1))

            def sums(t, b, i=0):
                dve.wait_ge(acts.sem, i * G_BATCHES + acts.at(t * batches + b + 1))
                c = coef[:, b % G_BATCHES, :]
                g = gates[:, t, bass.ds(i * G_SLOTS + b * PER_BATCH, PER_BATCH)]
                steps.done(dve, dve.tensor_tensor(c, c, g, ALU.mult))
                for e in range(PER_BATCH):
                    slot = (b * PER_BATCH + e) % G_SLOTS
                    dve.scalar_tensor_tensor(out=acc[:, t, :], in0=rows[:, slot, D:2 * D], scalar=c[:, e:e + 1],
                                             in1=acc[:, t, :], op0=ALU.mult, op1=ALU.add).then_inc(freed.sem, 1)
                    dve.wait_ge(freed.sem, i * G_SLOTS + freed.at(t * PEER_PAIRS + b * PER_BATCH + e + 1))

            for t in range(TT):
                products(t, 0)
                with steps.loop(dve, turns, G_BATCHES) as i:
                    for b in range(G_BATCHES):
                        products(t, b + 1, i)
                        sums(t, b, i)
                for b in range(turns * G_BATCHES, batches):
                    if b + 1 < batches:
                        products(t, b + 1)
                    sums(t, b)
            for t in range(TT):
                steps.done(dve, dve.tensor_tensor(acc[:, t, :], acc[:, t, :], m.rows[:, 3, :], ALU.mult))
                steps.done(dve, dve.tensor_tensor(core.x[:, t, :], core.x[:, t, :], acc[:, t, :], ALU.add))

        @block.sync
        def _(sp):
            core.issue_w(sp, 0)
    for s in landed:
        s.passed(16 * TT * PEER_PAIRS // G_SLOTS)
    freed.passed(TT * PEER_PAIRS)
    dots.passed(TT * batches)
    acts.passed(TT * batches)


def first_block(core, stop=None):
    nc = core.nc
    inputs = core.semaphore_of("inputs")
    with ExitStack() as ctx:
        m = Mod1(core, ctx)
        with ExitStack() as s1:
            a = Projected(core, s1)
            short = s1.enter_context(ExitStack())
            a.allocate_short(core, short)
            cond = core.sb(short, "cond1", [P, 2, KD])
            hcT = core.sb(short, "hcT", [P, KD, T])
            early = short.enter_context(ExitStack())
            xc = core.sb(early, "x_ctx", [P, TT, D])
            core.a_first, core.a_ends = 0, True
            with nc.Block() as block:
                @block.sync
                def _(sp):
                    for dst, name in ((cond, "cond1_in"), (core.cond, "cond2_in"), (core.x, "x_in"),
                                      (xc, "ctx_in"), (core.ident, "ident"), (core.norm_pre, "norm_pre"),
                                      (core.norm_post, "norm_post")):
                        sp.dma_start(dst[:], core.io[name]).then_inc(inputs.sem, 16)
                    core.issue_w(sp, 0)

                @block.scalar
                def _(act):
                    act.wait_ge(inputs.sem, 16 * 7)
                    act.activation(cond[:], cond[:], ACT.Silu)
                    act.activation(core.cond[:], core.cond[:], ACT.Silu)

                @block.vector
                def _(dve):
                    dve.memset(core.ones[:], 1.0)
            inputs.passed(16 * 7)
            core.a_ends = True
            keep, core.cond = core.cond, cond[:, 0, :]
            with ExitStack() as s0:
                core.a_ring = core.sb(s0, "a_ring", [P, A_SLOTS, A_ITEM])
                core.acc = core.sb(s0, "mod_acc", [P, 2 * CTX_COL])
                ada_stage(core, MOD1_FIRST, (cond[:, 1, :], CTX_COL, MOD1_FIRST))
                mod1_columns_stage(core, m)
            norm_stage(core, None, 0, (core.x, core.hT, m.gain, m.shift))
            norm_stage(core, None, 1, (xc, hcT, m.gain, m.shift))
            early.close()
            with ExitStack() as s0:
                rest = MOD1_ITEMS - MOD1_FIRST
                core.a_ends, core.a_first = False, core.a_issued
                core.a_ring = core.sb(s0, "a_ring", [P, A_SLOTS, A_ITEM])
                core.acc = core.sb(s0, "mod_acc", [P, (rest + MOD_ITEMS) * WN])
                a0 = core.a_taken
                side_items = rest + MOD_ITEMS

                def loads(sp, items):
                    total = core.a_taken + side_items
                    for i in range(items):
                        core.issue_w(sp, 1)
                        n = min(-(-side_items // items), total - core.a_taken)
                        core.issue_a(sp, n, 1)

                def work(dve):
                    for lo, n, who in ((0, rest, core.cond), (rest, MOD_ITEMS, keep)):
                        turns = n // A_SLOTS
                        with core.dve_steps.loop(dve, turns, A_SLOTS * KD) as i:
                            for j in range(A_SLOTS):
                                c = (lo + j) * WN
                                acc = core.acc[:, bass.ds(i * (A_SLOTS * WN) + c, WN)]
                                core.mod_unit(dve, a0 + lo + j, [(who, acc)], i)
                        for j in range(turns * A_SLOTS, n):
                            c = (lo + j) * WN
                            core.mod_unit(dve, a0 + lo + j, [(who, core.acc[:, c:c + WN])])

                first_projections(core, a, core.hT, hcT, (loads, work))
                core.cond = keep
                mod1_rest_stage(core, m, core.acc[:, 0:rest * WN], core.acc[:, rest * WN:])
            outT = core.hT
            neighbour_stage(core, a, outT)
            short.close()
            recurrent_mixer(core, a, outT)
        m.rows = core.sb(ctx, "rows1", [P, 4, D])
        rows1_stage(core, m)
        out_projection(core, core.hT)
        core.h2 = core.sb(ctx, "h2", [P, TT, D])
        mixed_stage(core, m)
        idx = core.sb(ctx, "expert_idx", [P, TT, PEER_PAIRS], U32)
        gates = core.sb(ctx, "expert_gates", [P, TT, PEER_PAIRS])
        peer_topk_stage(core, ctx, idx, gates)
        peer_experts_stage(core, m, idx, gates)


def first_layout(a):
    w_in = a["w_in"][0]
    widths = (256, 256, 256, 128, 128, 128, 512, 512, 512, 256, 256, 256)
    r, k, v, zw, za, zg, q, nk, nv, b, c, x = np.split(w_in, np.cumsum(widths)[:-1], 1)
    w = [w_items(y) for y in (r, k, v, np.concatenate([zw, za], 1), padded(zg), q, nk, nv, b, c, x)]
    w += [w_items(a["w_out"][0]), w_items(a["peer_q_w"][0])]
    mods = mod_items(a["ada_w"][0], a["ada_b"][0])
    tok = np.arange(T)
    row, col = tok // GRID, tok % GRID
    dr = row[None, :] - row[:, None] + 7
    dc = np.clip(col[None, :] - col[:, None] + NA_KC - 1, 0, 2 * NA_KC - 2)
    bias = a["na_rpb"][0][:, dr, dc].reshape(NA_HEADS, TT, P, T).transpose(2, 0, 1, 3)
    s, t = np.arange(P)[:, None], np.arange(P)[None, :]
    same = s // CHUNK == t // CHUNK
    masks = np.zeros((P, 2, 4 + LEVELS, P), np.float32)
    for d in range(2):
        before = (s > t) if d else (s < t)
        masks[:, d, 0] = before & same
        masks[:, d, 1] = (before | (s == t)) & same
        masks[:, d, 2] = masks[:, d, 1] * np.float32(LOG_DECAY)
        masks[:, d, 3] = masks[:, d, 0] * np.float32(LOG_DECAY)
        for level in range(LEVELS):
            half = 1 << level
            masks[:, d, 4 + level] = before & (s // (2 * half) == t // (2 * half)) & (s // half != t // half)
    chunk_sum = np.zeros((P, 2), np.float32)
    for c2 in range(2):
        chunk_sum[c2 * CHUNK:(c2 + 1) * CHUNK, c2] = LOG_DECAY
    tiles = lambda y: np.ascontiguousarray(y.reshape(TT, P, D).transpose(1, 0, 2))
    small = {
        "x_in": tiles(a["x"][0]), "ctx_in": tiles(a["ctx"][0]),
        "cond1_in": np.ascontiguousarray(np.stack([columns_of(a["c"][0]), columns_of(a["c_ctx"])], 1)),
        "norm1_g": columns_of(a["norm1_g"][0]), "norm2_g": columns_of(a["norm2_g"][0]),
        "na_bias": np.ascontiguousarray(bias),
        "sc_w": np.ascontiguousarray(a["sc_conv_w"][0].reshape(3, 2, P).transpose(2, 0, 1)),
        "rw_masks": masks, "chunk_sum": chunk_sum,
        "rw_up": np.ascontiguousarray(np.stack([a["rw_w_up"][0].reshape(P, RW_W), a["rw_a_up"][0].reshape(P, RW_W)], 1)),
        "w0a0": np.ascontiguousarray(np.concatenate([a["rw_w0"][0], a["rw_a0"][0]], 1).reshape(1, 4 * RW_W)),
        "rw_rows": np.ascontiguousarray(np.concatenate(
            [a["rw_k_k"][0], a["rw_k_a"][0], a["rw_r_k"][0].reshape(-1), a["rw_lnx_g"][0]]).reshape(1, 4 * RW_W)),
        "rw_g_up": np.ascontiguousarray(a["rw_g_up"][0]),
        "peer_keys": np.ascontiguousarray(a["peer_sub_keys"][0].reshape(2 * PEER_H, PEER_KEYS, P).transpose(2, 0, 1)),
        "count16": np.ascontiguousarray(np.broadcast_to(np.arange(PEER_TOP, dtype=np.float32), (P, PEER_TOP))),
        "experts": np.ascontiguousarray(np.concatenate([a["peer_u"][0], a["peer_v"][0]], 1)),
        "final_g": np.ascontiguousarray(a["final_g"].reshape(1, D)),
    }
    return w, mods, small


def final_norm_stage(core):
    nc = core.nc
    loaded, mean, root = core.semaphore_of("final_g_in"), core.semaphore_of("final_mean"), core.semaphore_of("final_root")
    with ExitStack() as ctx:
        g = core.sb(ctx, "final_g", [P, D])
        junk = core.sb(ctx, "final_junk", [P, TT, D])
        ss = core.sb(ctx, "final_ss", [P, TT])
        block = ctx.enter_context(nc.Block())

        @block.sync
        def _(sp):
            sp.dma_start(g[:], core.io["final_g"].partition_broadcast(P)).then_inc(loaded.sem, 16)
            core.issue_w(sp, 0)

        @block.scalar
        def _(act):
            act.wait_ge(mean.sem, mean.at(1))
            act.activation(ss[:], ss[:], ACT.Sqrt).then_inc(root.sem, 1)

        @block.vector
        def _(dve):
            for t in range(TT):
                core.dve_steps.done(dve, dve.tensor_tensor_reduce(
                    junk[:, t, :], core.x[:, t, :], core.x[:, t, :], 1.0, 0.0, ALU.mult, ALU.add, ss[:, t:t + 1]))
            dve.tensor_scalar(ss[:], ss[:], 1.0 / D, EPS, ALU.mult, ALU.add).then_inc(mean.sem, 1)
            dve.wait_ge(root.sem, root.at(1))
            core.dve_steps.done(dve, dve.reciprocal(ss[:], ss[:]))
            dve.wait_ge(loaded.sem, loaded.at(16))
            for t in range(TT):
                dve.scalar_tensor_tensor(out=core.x[:, t, :], in0=core.x[:, t, :], scalar=ss[:, t:t + 1],
                                         in1=g[:], op0=ALU.mult, op1=ALU.mult)
    loaded.passed(16)
    mean.passed(1)
    root.passed(1)


def store_stage(core, out):
    stored = core.semaphore_of("stored")
    with core.nc.Block() as block:
        @block.sync
        def _(sp):
            sp.dma_start(out.rearrange("a (t p) d -> p (a t) d", p=P), core.x[:]).then_inc(stored.sem, 16)
            sp.wait_ge(stored.sem, 16)


def build_program(nc, io, out):
    with ExitStack() as ctx:
        core = Core(nc, ctx)
        core.io = io
        core.w_stream, core.a_stream = io["w_stream"], io["a_stream"]
        core.ps = ctx.enter_context(nc.psum_tensor("ps", [P, BANKS, BANK], F32))
        core.y = core.ps[:, 4:8, :]
        core.ring = core.sb(ctx, "w_ring", [P, W_SLOTS, ITEM])
        core.x = core.sb(ctx, "x", [P, TT, D])
        core.hT = core.sb(ctx, "hT", [P, KD, T])
        core.cond = core.sb(ctx, "cond2", [P, KD])
        core.ident = core.sb(ctx, "identity", [P, P])
        core.ones = core.sb(ctx, "ones", [P, P])
        core.shift = core.sb(ctx, "shift", [P, 3, KD])
        core.gain = core.sb(ctx, "gain", [P, 3, KD])
        core.gate_cols = core.sb(ctx, "gate_cols", [P, 3, KD])
        core.norm_pre = core.sb(ctx, "norm_pre", [P, DEPTH, 3, KD])
        core.norm_post = core.sb(ctx, "norm_post", [P, DEPTH, 3, KD])
        first_block(core)
        final_norm_stage(core)
        core.gates = core.sb(ctx, "gates", [P, 3, D])
        core.a_ring = core.sb(ctx, "a_ring", [P, A_SLOTS, A_ITEM])
        core.a_first = core.a_issued
        core.a_limit = core.a_stream.shape[0]
        mod_stage(core, 0, None)
        second_block(core)
        store_stage(core, out)


def kernel(**inputs):
    import concourse.bacc as bacc
    from concourse.bass_utils import run_bass_kernel_spmd

    a = {name: np.asarray(v) for name, v in inputs.items()}
    w1, mods1, small1 = first_layout(a)
    w2, mods2, small2 = second_layout(a)
    arrays = {**small1, **small2, **attention_tables(),
              "w_stream": np.concatenate(w1 + w2), "a_stream": np.concatenate([mods1, mods2])}
    nc = bacc.Bacc("TRN2", target_bir_lowering=False, num_devices=1)
    io = {name: nc.dram_tensor(f"in_{name}", v.shape, mybir.dt.from_np(v.dtype), kind="ExternalInput").ap()
          for name, v in arrays.items()}
    out = nc.dram_tensor("out_x", (1, T, D), F32, kind="ExternalOutput").ap()
    build_program(nc, io, out)
    r = run_bass_kernel_spmd(nc, [{f"in_{name}": v for name, v in arrays.items()}], core_ids=[0])
    return r.results[0]["out_x"]
```

```python
from contextlib import ExitStack, contextmanager

import numpy as np

import concourse.bass as bass
from concourse import mybir

F32 = mybir.dt.float32
F32R = mybir.dt.float32r
U32 = mybir.dt.uint32
ALU = mybir.AluOpType
ACT = mybir.ActivationFunctionType
AX = mybir.AxisListType

P = 128
D = 1024
KD = D // P
T = 256
TT = T // P
DH = 64
WN = 256
ITEM = KD * WN
W_SLOTS = 6
A_SLOTS = 4
LAG = 5
S_SLOTS = 3
S_AHEAD = 2
BANK = 512
BANKS = 8
EPS = 1e-6
GN_EPS = 64e-5
NEG = -1e30

DEPTH = 4
D_FF = 2816
FF_STEPS = D_FF // WN
FF_ITEMS = 3 * FF_STEPS
MOD_COLS = 9 * D
MOD_ITEMS = MOD_COLS // WN
UNIT_STEPS = KD + 1
MIXERS = ("nsa", "stick", "diff", "nsa")
NSA_HEADS, NSA_KV = 16, 4
NSA_REP = NSA_HEADS // NSA_KV
CMP_LEN, CMP_STRIDE, CMP_HID = 32, 16, 256
N_CMP = (T - CMP_LEN) // CMP_STRIDE + 1
DIFF_HEADS = 8
SLOPES = [2.0 ** (-8.0 * (h + 1) / NSA_HEADS) for h in range(NSA_HEADS)]


class Signal:

    def __init__(self, sem):
        self.sem = sem
        self.base = 0

    def at(self, n):
        return self.base + n

    def passed(self, n):
        self.base += n


class Steps:

    def __init__(self, sem):
        self.sem = sem
        self.n = 0
        self.turns = 0

    def done(self, eng, ins):
        ins.then_inc(self.sem, 1)
        self.n += 1
        eng.wait_ge(self.sem, self.n + self.turns)

    def passing(self, eng, ins):
        ins.then_inc(self.sem, 1)
        self.n += 1
        eng.wait_ge(self.sem, self.n - 1 + self.turns)

    @contextmanager
    def loop(self, eng, trips, steps):
        start = self.n
        with eng.Fori(0, trips, 1) as i:
            self.turns = i * steps
            yield i
        assert self.n - start == steps, (self.n - start, steps)
        self.turns = 0
        self.n += steps * (trips - 1)


class Core:

    def __init__(self, nc, ctx):
        self.nc = nc
        self.ctx = ctx
        self.signals = {}
        self.serial = 0
        self.pe_steps = Steps(ctx.enter_context(nc.semaphore("pe_steps")))
        self.act_steps = Steps(ctx.enter_context(nc.semaphore("act_steps")))
        self.dve_steps = Steps(ctx.enter_context(nc.semaphore("dve_steps")))
        self.pool_steps = Steps(ctx.enter_context(nc.semaphore("pool_steps")))
        self.w_loaded = [ctx.enter_context(nc.semaphore(f"w_loaded{s}")) for s in range(W_SLOTS)]
        self.w_used = ctx.enter_context(nc.semaphore("w_used"))
        self.a_loaded = [ctx.enter_context(nc.semaphore(f"a_loaded{s}")) for s in range(A_SLOTS)]
        self.a_used = ctx.enter_context(nc.semaphore("a_used"))
        self.hi_made = ctx.enter_context(nc.semaphore("w_hi_made"))
        self.lo_made = ctx.enter_context(nc.semaphore("w_lo_made"))
        self.w_issued = self.w_taken = 0
        self.split_from = self.split_issued = 0
        self.a_issued = self.a_taken = 0
        self.a_limit = MOD1_ITEMS + MOD_ITEMS

    def semaphore_of(self, name):
        if name not in self.signals:
            self.signals[name] = Signal(self.ctx.enter_context(self.nc.semaphore(name)))
        return self.signals[name]

    def sb(self, ctx, name, shape, dtype=F32):
        self.serial += 1
        return ctx.enter_context(self.nc.sbuf_tensor(f"{name}_{self.serial}", shape, dtype))

    def w_item(self, n):
        return self.ring[:, n % W_SLOTS, :].rearrange("p (k n) -> p k n", k=KD)

    def w_wait(self, pe, n, turn=0):
        pe.wait_ge(self.w_loaded[n % W_SLOTS], (turn + (n // W_SLOTS + 1)) * 16)

    def issue_w(self, sp, take):
        total = self.w_stream.shape[0]
        upto = min(self.w_taken + take + W_SLOTS, total)
        n = self.w_issued
        if n < W_SLOTS:
            for n in range(0, W_SLOTS):
                sp.dma_start(self.ring[:, n, :], self.w_stream[n]).then_inc(self.w_loaded[n], 16)
            n = W_SLOTS
        turns = (upto - n) // W_SLOTS
        if turns > 1:
            with sp.Fori(0, turns, 1) as i:
                for s in range(W_SLOTS):
                    sp.wait_ge(self.w_used, i * W_SLOTS + (n + s - W_SLOTS + 1))
                    src = self.w_stream[bass.ds(i * W_SLOTS + (n + s), 1), :, :]
                    sp.dma_start(self.ring[:, (n + s) % W_SLOTS, :],
                                 src.rearrange("a p n -> p (a n)")).then_inc(
                                     self.w_loaded[(n + s) % W_SLOTS], 16)
            n += turns * W_SLOTS
        while n < upto:
            sp.wait_ge(self.w_used, n - W_SLOTS + 1)
            sp.dma_start(self.ring[:, n % W_SLOTS, :], self.w_stream[n]).then_inc(
                self.w_loaded[n % W_SLOTS], 16)
            n += 1
        self.w_issued = n
        self.w_taken += take

    def w_halves(self, n):
        slot = (n - self.split_from) % S_SLOTS
        return [ring[:, slot, :].rearrange("p (k n) -> p k n", k=KD) for ring in (self.w_hi, self.w_lo)]

    def split_hi(self, act, n, turn=0):
        self.w_wait(act, n, turn)
        act.wait_ge(self.w_used, turn * W_SLOTS + (n - S_SLOTS + 1))
        act.activation(self.w_halves(n)[0], self.w_item(n), ACT.Copy).then_inc(self.hi_made, 1)

    def split_lo(self, pool, n, turn=0):
        pool.wait_ge(self.hi_made, turn * W_SLOTS + (n - self.split_from + 1))
        pool.tensor_tensor(self.w_halves(n)[1], self.w_item(n), self.w_halves(n)[0],
                           ALU.subtract).then_inc(self.lo_made, 1)

    def split_wait(self, pe, n, turn=0):
        pe.wait_ge(self.lo_made, turn * W_SLOTS + (n - self.split_from + 1))

    def start_splits(self, ctx):
        self.w_hi, self.w_lo = (self.sb(ctx, name, [P, S_SLOTS, ITEM], F32R) for name in ("w_hi", "w_lo"))
        self.h_split = [self.sb(ctx, name, [P, KD, T], F32R) for name in ("h_hi", "h_lo")]
        self.taken_whole()

    def taken_whole(self):
        self.split_from += self.w_taken - self.split_issued
        self.split_issued = self.w_taken

    def split_to(self, take, ahead=S_AHEAD):
        to = min(self.w_taken + take + ahead, self.w_stream.shape[0])
        return range(self.split_issued, max(to, self.split_issued))

    def issue_a(self, sp, take, ahead):
        upto = min(self.a_taken + take + (A_SLOTS if ahead else 0), self.a_limit)
        n = self.a_issued
        while n < upto and n < self.a_first + A_SLOTS:
            sp.dma_start(self.a_ring[:, n % A_SLOTS, :], self.a_stream[n]).then_inc(
                self.a_loaded[n % A_SLOTS], 16)
            n += 1
        turns = (upto - n) // A_SLOTS
        if turns > 0:
            with sp.Fori(0, turns, 1) as i:
                for s in range(A_SLOTS):
                    sp.wait_ge(self.a_used, i * A_SLOTS + (n + s - A_SLOTS + 1))
                    src = self.a_stream[bass.ds(i * A_SLOTS + (n + s), 1), :, :]
                    sp.dma_start(self.a_ring[:, (n + s) % A_SLOTS, :],
                                 src.rearrange("a p n -> p (a n)")).then_inc(
                                     self.a_loaded[(n + s) % A_SLOTS], 16)
            n += turns * A_SLOTS
        while n < upto:
            sp.wait_ge(self.a_used, n - A_SLOTS + 1)
            sp.dma_start(self.a_ring[:, n % A_SLOTS, :], self.a_stream[n]).then_inc(
                self.a_loaded[n % A_SLOTS], 16)
            n += 1
        self.a_issued = n
        self.a_taken += take

    def load_w(self, sp, n, turn=0):
        sp.wait_ge(self.w_used, turn * W_SLOTS + (n - W_SLOTS + 1))
        src = self.w_stream[bass.ds(turn * W_SLOTS + n, 1), :, :]
        sp.dma_start(self.ring[:, n % W_SLOTS, :], src.rearrange("a p n -> p (a n)")).then_inc(
            self.w_loaded[n % W_SLOTS], 16)

    def load_a(self, sp, n, turn=0):
        sp.wait_ge(self.a_used, turn * A_SLOTS + (n - A_SLOTS + 1))
        src = self.a_stream[bass.ds(turn * A_SLOTS + n, 1), :, :]
        sp.dma_start(self.a_ring[:, n % A_SLOTS, :], src.rearrange("a p n -> p (a n)")).then_inc(
            self.a_loaded[n % A_SLOTS], 16)

    def issue_both(self, sp, w_take, a_take):
        w = self.w_issued
        w_to = min(self.w_taken + w_take + W_SLOTS, self.w_stream.shape[0])
        a, a_to = self.a_issued, self.a_taken + a_take
        if a_take:
            for n in range(a, a + A_SLOTS):
                self.load_a(sp, n)
            a += A_SLOTS
            for n in range(w, w + LAG):
                self.load_w(sp, n)
            w += LAG
            turns = min((w_to - w) // W_SLOTS, (a_to - a) // A_SLOTS)
            with sp.Fori(0, turns, 1) as i:
                for s in range(W_SLOTS):
                    self.load_w(sp, w + s, i)
                    if s % 3 != 2:
                        self.load_a(sp, a + s - s // 3, i)
            w += turns * W_SLOTS
            a += turns * A_SLOTS
            while a < a_to:
                self.load_w(sp, w)
                self.load_w(sp, w + 1)
                self.load_a(sp, a)
                w += 2
                a += 1
        self.w_issued, self.a_issued = w, a
        self.a_taken += a_take
        self.issue_w(sp, w_take)

    def mod_unit(self, dve, n, outs, turn=0):
        dve.wait_ge(self.a_loaded[n % A_SLOTS], (turn + (n // A_SLOTS + 1)) * 16)
        item = self.a_ring[:, n % A_SLOTS, :].rearrange("p (k n) -> p k n", k=KD)
        for k in range(KD):
            for cond, acc, odd in outs:
                dst = odd if k % 2 else acc
                if k < 2:
                    last = dve.tensor_scalar(dst, item[:, k, :], cond[:, k:k + 1], None, ALU.mult)
                else:
                    last = dve.scalar_tensor_tensor(
                        out=dst, in0=item[:, k, :], scalar=cond[:, k:k + 1],
                        in1=dst, op0=ALU.mult, op1=ALU.add)
                if k < KD - 1:
                    self.dve_steps.passing(dve, last)
                else:
                    self.dve_steps.done(dve, last)
        for cond, acc, odd in outs:
            self.dve_steps.passing(dve, dve.tensor_tensor(acc, acc, odd, ALU.add))
        dve.sem_inc(self.a_used, 1)


def put(eng, is_act, out, in_, scale=1.0):
    if is_act:
        return eng.activation(out, in_, ACT.Copy, scale=scale)
    return eng.tensor_scalar(out, in_, scale, None, ALU.mult)


def in_three(pe, out, stationary, moving, start, stop):
    pe.matmul(out, stationary[0], moving[0], start=start, stop=False)
    pe.matmul(out, stationary[0], moving[1], start=False, stop=False)
    return pe.matmul(out, stationary[1], moving[0], start=False, stop=stop)


def wide(ap, n):
    return bass.AP(ap.tensor, ap.offset, [list(x) for x in ap.ap] + [[0, n]])


def norm_stage(core, post, pre, of=None):
    nc = core.nc
    squares, roots = core.semaphore_of("squares_ready"), core.semaphore_of("roots_ready")
    means, rows = core.semaphore_of("means_ready"), core.semaphore_of("rows_ready")
    turned, x_new = core.semaphore_of("turned_ready"), core.semaphore_of("x_new")
    x, hT, gain, shift = of or (core.x, None, core.gain, core.shift)
    whole_made = core.semaphore_of("h_whole_made")
    y = core.y
    n_post = 1 if post is not None else 0
    n_pre = 1 if pre is not None else 0
    with ExitStack() as ctx:
        junk = core.sb(ctx, "junk", [P, 2, D])
        ss = core.sb(ctx, "ss", [P, 2, 2 * TT])
        stat = core.sb(ctx, "stat", [P, 4, TT])
        xn = core.sb(ctx, "xn", [P, TT, D])
        whole = junk[:].rearrange("p t (k n) -> p (t k) n", n=T)
        block = ctx.enter_context(nc.Block())

        @block.sync
        def _(sp):
            core.issue_w(sp, 0)

        @block.scalar
        def _(act):
            if n_post:
                for i in range(2 * TT):
                    act.activation(junk[:, i // 2, (i % 2) * BANK:(i % 2 + 1) * BANK], y[:, i, :], ACT.Square,
                                   accum_out=ss[:, 0, i:i + 1]).then_inc(squares.sem, 1)
                act.wait_ge(means.sem, means.at(1))
                act.activation(stat[:, 0, :], stat[:, 0, :], ACT.Sqrt).then_inc(roots.sem, 1)
                act.wait_ge(x_new.sem, x_new.at(1))
            if n_pre:
                for t in range(TT):
                    act.activation(junk[:, t, :], x[:, t, :], ACT.Square,
                                   accum_out=ss[:, 1, t:t + 1]).then_inc(squares.sem, 1)
                act.wait_ge(means.sem, means.at(n_post + 1))
                act.activation(stat[:, 2, :], stat[:, 2, :], ACT.Sqrt).then_inc(roots.sem, 1)
                for k in range(KD):
                    act.wait_ge(turned.sem, turned.at(k // 2 + 1))
                    last = act.activation((hT or whole)[:, k, :],
                                          core.ps[:, k // 2, (k % 2) * T:(k % 2 + 1) * T],
                                          ACT.Identity, scale=gain[:, pre, k:k + 1],
                                          bias=shift[:, pre, k:k + 1])
                    if k % 2 and not hT:
                        last.then_inc(whole_made.sem, 1)

        @block.vector
        def _(dve):
            if n_post:
                dve.wait_ge(squares.sem, squares.at(2 * TT))
                for t in range(TT):
                    core.dve_steps.done(dve, dve.tensor_tensor(
                        stat[:, 1, t:t + 1], ss[:, 0, 2 * t:2 * t + 1], ss[:, 0, 2 * t + 1:2 * t + 2],
                        ALU.add))
                dve.tensor_scalar(stat[:, 0, :], stat[:, 1, :], 1.0 / D, EPS, ALU.mult,
                                  ALU.add).then_inc(means.sem, 1)
                dve.wait_ge(roots.sem, roots.at(1))
                core.dve_steps.done(dve, dve.reciprocal(stat[:, 1, :], stat[:, 0, :]))
                for i in range(2 * TT):
                    t, half = i // 2, i % 2
                    part = slice(half * BANK, (half + 1) * BANK)
                    core.dve_steps.done(dve, dve.scalar_tensor_tensor(
                        out=xn[:, t, part], in0=y[:, i, :], scalar=stat[:, 1, t:t + 1],
                        in1=core.gates[:, post, part], op0=ALU.mult, op1=ALU.mult))
                last = dve.tensor_tensor(x[:], x[:], xn[:], ALU.add)
                last.then_inc(x_new.sem, 1)
                dve.wait_ge(x_new.sem, x_new.at(1))
            if n_pre:
                dve.wait_ge(squares.sem, squares.at(2 * TT * n_post + TT))
                dve.tensor_scalar(stat[:, 2, :], ss[:, 1, 0:TT], 1.0 / D, EPS, ALU.mult,
                                  ALU.add).then_inc(means.sem, 1)
                dve.wait_ge(roots.sem, roots.at(n_post + 1))
                core.dve_steps.done(dve, dve.reciprocal(stat[:, 3, :], stat[:, 2, :]))
                for t in range(TT):
                    dve.tensor_scalar(xn[:, t, :], x[:, t, :], stat[:, 3, t:t + 1], None,
                                      ALU.mult).then_inc(rows.sem, 1)
                if not hT:
                    for k in range(0, KD, 2):
                        dve.wait_ge(whole_made.sem, whole_made.at(k // 2 + 1))
                        hi, lo = (part[:, k:k + 2, :] for part in core.h_split)
                        core.dve_steps.done(dve, dve.tensor_copy(hi, whole[:, k:k + 2, :]))
                        dve.tensor_tensor(lo, whole[:, k:k + 2, :], hi, ALU.subtract)

        @block.tensor
        def _(pe):
            if n_pre:
                pe.wait_ge(rows.sem, rows.at(TT))
                for k in range(KD):
                    for t in range(TT):
                        last = pe.transpose(core.ps[:, k // 2, (k % 2) * T + t * P:(k % 2) * T + (t + 1) * P],
                                            xn[:, t, k * P:(k + 1) * P], core.ident[:])
                    if k % 2:
                        last.then_inc(turned.sem, 1)

    squares.passed(2 * TT * n_post + TT * n_pre)
    roots.passed(n_post + n_pre)
    means.passed(n_post + n_pre)
    rows.passed(TT * n_pre)
    turned.passed(KD // 2 * n_pre)
    x_new.passed(n_post)
    whole_made.passed(KD // 2 if n_pre and not hT else 0)


def mod_columns(core, pe, acc, chunks, bank):
    for c in range(chunks):
        last = pe.matmul(core.ps[:, bank, c:c + 1], acc[:, c * P:(c + 1) * P], core.ones[:, 0:1],
                         start=True, stop=True)
    return last


def shape_columns(core, dve, layer, columns):
    cols = columns.rearrange("p (s a k) -> p s a k", s=3, a=3)
    dve.tensor_copy(core.shift[:], cols[:, :, 0, :])
    dve.scalar_tensor_tensor(out=core.gain[:], in0=cols[:, :, 1, :], scalar=1.0, in1=core.norm_pre[:, layer],
                             op0=ALU.add, op1=ALU.mult)
    for s in range(3):
        weight = 0.5 if s != 1 else 1.0
        last = dve.scalar_tensor_tensor(out=core.gate_cols[:, s, :], in0=cols[:, s, 2, :], scalar=weight,
                                        in1=core.norm_post[:, layer, s, :], op0=ALU.mult, op1=ALU.mult)
    return last


def mod_stage(core, layer):
    nc = core.nc
    shaped, wide_out = core.semaphore_of("mod_shaped"), core.semaphore_of("mod_wide")
    with nc.Block() as block:
        @block.sync
        def _(sp):
            core.issue_w(sp, 0)

        @block.tensor
        def _(pe):
            if layer:
                pe.wait_ge(shaped.sem, shaped.at(1))
            for s in range(3):
                for half in range(2):
                    for j in range(4):
                        k = 4 * half + j
                        col = core.gate_cols[:, s, k:k + 1]
                        last = pe.matmul(core.ps[:, 1 + 2 * s + half, j * P:(j + 1) * P],
                                         bass.AP(col.tensor, col.offset, [list(col.ap[0]), [0, P]]),
                                         core.ident[:], start=True, stop=True)
                    last.then_inc(wide_out.sem, 1)

        def copies(eng, is_act):
            for i in range(0 if is_act else 1, 6, 2):
                eng.wait_ge(wide_out.sem, wide_out.at(i + 1))
                put(eng, is_act, core.gates[:, i // 2, (i % 2) * BANK:(i % 2 + 1) * BANK], core.ps[:, 1 + i, :])

        @block.scalar
        def _(act):
            copies(act, True)

        @block.vector
        def _(dve):
            if layer:
                shape_columns(core, dve, layer, core.mod_cols[:]).then_inc(shaped.sem, 1)
            copies(dve, False)

    if layer:
        shaped.passed(1)
    wide_out.passed(6)


FF_TURNS = (FF_STEPS - 3) // 2


def ffn_stage(core, mod_part):
    nc = core.nc
    silus, hidden = core.semaphore_of("silu_ready"), core.semaphore_of("hidden_ready")
    w_used = core.w_used
    first, a0 = core.w_taken, core.a_taken
    splits = core.split_to(FF_ITEMS)
    n_mod = MOD_ITEMS // 2 if mod_part is not None else 0
    columns = n_mod * WN // P
    mod_part_cols = core.mod_cols[:, mod_part[1] * columns:(mod_part[1] + 1) * columns] if n_mod else None
    biased = core.semaphore_of("mod_biased")
    mods_made, summed = core.semaphore_of("mods_made"), core.semaphore_of("mod_summed")
    per_turn = 2 * 3

    def gate_item(s):
        return first + (3 * s - 1 if s else 0)

    def up_item(s):
        return first + (3 * s if s else 1)

    def down_item(s):
        return first + (3 * s + 4 if s < FF_STEPS - 1 else FF_ITEMS - 1)

    with ExitStack() as ctx:
        act_g = core.sb(ctx, "act_g", [P, 2, 2 * T])
        if n_mod:
            acc = core.sb(ctx, "mod_acc", [P, n_mod * WN])
            core.a_ring = core.sb(ctx, "a_ring", [P, A_SLOTS, ITEM])
            core.odd_sums = core.sb(ctx, "odd_sums", [P, 2, WN])
        hid = [core.sb(ctx, f"hid_{part}", [P, 2, 2, T], F32R) for part in ("hi", "lo")]
        block = ctx.enter_context(nc.Block())

        @block.sync
        def _(sp):
            if n_mod:
                sp.dma_start(mod_part_cols, core.io["mod_bias2"][
                    :, mod_part[0], 0, mod_part[1] * columns:(mod_part[1] + 1) * columns]).then_inc(biased.sem, 16)
            core.issue_both(sp, FF_ITEMS, n_mod)

        @block.tensor
        def _(pe):
            def up(s, i=0):
                if s >= 2:
                    pe.wait_ge(hidden.sem, i * 2 + hidden.at(s - 1))
                for part, n in enumerate((gate_item(s), up_item(s))):
                    core.split_wait(pe, n, i)
                    halves = core.w_halves(n)
                    for m in range(2):
                        for k in range(KD):
                            last = in_three(pe, core.ps[:, 2 * (s % 2) + part, m * T:(m + 1) * T],
                                            [w[:, k, m * P:(m + 1) * P] for w in halves],
                                            [h[:, k, :] for h in core.h_split], k == 0, k == KD - 1)
                    last.then_inc(w_used, 1)

            def down(s, i=0):
                pe.wait_ge(hidden.sem, i * 2 + hidden.at(s + 1))
                core.split_wait(pe, down_item(s), i)
                halves = [w.rearrange("p (m k) n -> p m (k n)", m=2) for w in core.w_halves(down_item(s))]
                for t in range(TT):
                    for half in range(2):
                        for m in range(2):
                            last = in_three(pe, core.y[:, 2 * t + half, :],
                                            [h[:, s % 2, m, t * P:(t + 1) * P] for h in hid],
                                            [w[:, m, half * BANK:(half + 1) * BANK] for w in halves],
                                            s == 0 and m == 0, s == FF_STEPS - 1 and m == 1)
                last.then_inc(w_used, 1)

            up(0)
            up(1)
            down(0)
            up(2)
            down(1)
            with pe.Fori(0, FF_TURNS, 1) as i:
                up(3, i)
                down(2, i)
                up(4, i)
                down(3, i)
            down(FF_STEPS - 1)
            if n_mod:
                pe.wait_ge(mods_made.sem, mods_made.at(1))
                mod_columns(core, pe, acc, columns, 2).then_inc(summed.sem, 1)

        @block.scalar
        def _(act):
            def silu(s, i=0):
                if s >= 2:
                    act.wait_ge(hidden.sem, i * 2 + hidden.at(s - 1))
                act.wait_ge(w_used, i * per_turn + gate_item(s) + 1)
                act.activation(act_g[:, s % 2, :], core.ps[:, 2 * (s % 2), :], ACT.Silu).then_inc(silus.sem, 1)

            start = gate_item(2) + S_SLOTS
            for n in range(core.split_issued, start):
                if n == gate_item(0) + S_SLOTS:
                    silu(0)
                if n == gate_item(1) + S_SLOTS:
                    silu(1)
                core.split_hi(act, n)
            with act.Fori(0, FF_TURNS, 1) as i:
                for s in (2, 3):
                    silu(s, i)
                    for n in range(3):
                        core.split_hi(act, gate_item(s) + S_SLOTS + n, i)
            silu(FF_STEPS - 1)
            for n in range(start + FF_TURNS * per_turn, splits.stop):
                core.split_hi(act, n)

        @block.gpsimd
        def _(pool):
            turns = len(splits) // per_turn
            with pool.Fori(0, turns, 1) as i:
                for n in splits[:per_turn]:
                    core.split_lo(pool, n, i)
            for n in splits[turns * per_turn:]:
                core.split_lo(pool, n)

        @block.vector
        def _(dve):
            def hide(s, i=0):
                dve.wait_ge(silus.sem, i * 2 + silus.at(s + 1))
                dve.wait_ge(w_used, i * per_turn + up_item(s) + 1)
                if s >= 2:
                    dve.wait_ge(w_used, i * per_turn + down_item(s - 2) + 1)
                whole = act_g[:, s % 2, :]
                hi, lo = (h[:, s % 2, :, :].rearrange("p m n -> p (m n)") for h in hid)
                core.dve_steps.done(dve, dve.tensor_tensor(whole, whole, core.ps[:, 2 * (s % 2) + 1, :], ALU.mult))
                core.dve_steps.done(dve, dve.tensor_copy(hi, whole))
                dve.tensor_tensor(lo, whole, hi, ALU.subtract).then_inc(hidden.sem, 1)

            def mods(i, n, items=2):
                for j in range(items) if n_mod else ():
                    out = acc[:, bass.ds(i * (A_SLOTS * WN) + (n + j) * WN, WN)]
                    core.mod_unit(dve, a0 + n + j, [(core.cond, out, core.odd_sums[:, 0, :])], i)

            hide(0)
            mods(0, 0, 1)
            hide(1)
            mods(0, 1, 1)
            with core.dve_steps.loop(dve, FF_TURNS, 2 * 2 + (A_SLOTS * UNIT_STEPS if n_mod else 0)) as i:
                hide(2, i)
                mods(i, 2)
                hide(3, i)
                mods(i, 4)
            hide(FF_STEPS - 1)
            if n_mod:
                dve.sem_inc(mods_made.sem, 1)
                dve.wait_ge(summed.sem, summed.at(1))
                dve.wait_ge(biased.sem, biased.at(16))
                dve.tensor_tensor(mod_part_cols, mod_part_cols, core.ps[:, 2, 0:columns], ALU.add)

    assert n_mod in (0, 2 + FF_TURNS * A_SLOTS)
    if n_mod:
        biased.passed(16)
        mods_made.passed(1)
        summed.passed(1)
    silus.passed(FF_STEPS)
    hidden.passed(FF_STEPS)
    core.split_issued = splits.stop


def ada_stage(core, take, also=None):
    nc = core.nc
    a0 = core.a_taken
    both = also[2] if also else 0
    with nc.Block() as block:
        @block.sync
        def _(sp):
            core.issue_a(sp, take, 0 if core.a_ends else 1)
            core.issue_w(sp, 0)

        @block.vector
        def _(dve):
            for first, last, two in ((0, both, True), (both, take, False)):
                turns, rest = (last - first) // A_SLOTS, (last - first) % A_SLOTS

                def unit(j, i=0):
                    outs = [(core.cond, core.acc[:, bass.ds(i * (A_SLOTS * WN) + j * WN, WN)],
                             core.odd_sums[:, 0, :])]
                    if two:
                        outs.append((also[0], core.acc[:, bass.ds(i * (A_SLOTS * WN) + j * WN + also[1], WN)],
                                     core.odd_sums[:, 1, :]))
                    core.mod_unit(dve, a0 + j, outs, i)

                if turns:
                    with core.dve_steps.loop(dve, turns, A_SLOTS * UNIT_STEPS * (2 if two else 1)) as i:
                        for j in range(A_SLOTS):
                            unit(first + j, i)
                for j in range(last - rest, last):
                    unit(j)


def projections(core, items, units, side=None, split=True, ahead=S_AHEAD, tables=False):
    nc = core.nc
    ready = core.semaphore_of("proj_ready")
    copied = [core.semaphore_of("proj_copied_act"), core.semaphore_of("proj_copied_dve")]
    first = core.w_taken
    by = 1 if side else 2
    last_of = {item: u for u, (item, _, _, _) in enumerate(units)}
    splits = core.split_to(items, ahead) if split else range(0)
    inner = [u for u, (item, _, _, _) in enumerate(units) if last_of[item] != u]
    with nc.Block() as block:
        @block.sync
        def _(sp):
            if tables:
                sp.dma_start(core.alibi[:], core.io["alibi"]).then_inc(core.semaphore_of("alibi_in").sem, 16)
            if side:
                side[0](sp, items)
            else:
                core.issue_w(sp, items)

        @block.tensor
        def _(pe):
            for u, (item, halves, source, _) in enumerate(units):
                if u >= BANKS:
                    pe.wait_ge(copied[u % by].sem, copied[u % by].at((u - BANKS) // by + 1))
                if split:
                    core.split_wait(pe, first + item)
                    weights = core.w_halves(first + item)
                else:
                    core.w_wait(pe, first + item)
                    weights = [core.w_item(first + item)]
                for m, (rows, stationary, moving) in enumerate(halves):
                    dst = core.ps[0:rows, u % BANKS, m * T:(m + 1) * T]
                    for k in range(KD):
                        a = [stationary(w, h, k) for w, h in zip(weights, source)]
                        b = [moving(w, h, k) for w, h in zip(weights, source)]
                        if split:
                            last = in_three(pe, dst, a, b, k == 0, k == KD - 1)
                        else:
                            last = pe.matmul(dst, a[0], b[0], start=(k == 0), stop=(k == KD - 1))
                last.then_inc(ready.sem if u in inner else core.w_used, 1)

        def copy(eng, parity):
            ahead_of = splits if parity == 0 else range(0)
            for u, (item, _, _, out) in enumerate(units):
                while ahead_of and ahead_of[0] < first + item + S_SLOTS:
                    core.split_hi(eng, ahead_of[0])
                    ahead_of = ahead_of[1:]
                if u % by == parity:
                    if u in inner:
                        eng.wait_ge(ready.sem, ready.at(inner.index(u) + 1))
                    else:
                        eng.wait_ge(core.w_used, first + item + 1)
                    out(eng, parity == 0, core.ps[:, u % BANKS, :]).then_inc(copied[parity].sem, 1)
            for n in ahead_of:
                core.split_hi(eng, n)

        @block.scalar
        def _(act):
            copy(act, 0)

        @block.vector
        def _(dve):
            if side:
                side[1](dve)
            else:
                copy(dve, 1)

        @block.gpsimd
        def _(pool):
            for n in splits:
                core.split_lo(pool, n)

    core.split_issued = splits.stop if split else core.split_issued
    ready.passed(len(inner))
    for parity in range(by):
        copied[parity].passed(len(range(parity, len(units), by)))


def across(core, src, item, out, scale=1.0):
    def half(m):
        return (P, lambda w, h, k: w[:, k, m * P:(m + 1) * P], lambda w, h, k: h[:, k, :])
    return (item, [half(0), half(1)], src,
            lambda eng, is_act, bank: put(eng, is_act, out, bank.rearrange("p (m n) -> p m n", m=2), scale))


def along(core, src, item, out, cols=WN):
    def half(t):
        return (P, lambda w, h, k: h[:, k, t * P:(t + 1) * P], lambda w, h, k: w[:, k, :])
    return (item, [half(0), half(1)], src,
            lambda eng, is_act, bank: put(eng, is_act, out,
                                          bank.rearrange("p (t n) -> p t n", t=TT)[:, :, 0:cols]))


def across_twice(core, src, item, out):
    item, halves, _, _ = across(core, src, item, None)

    def copies(eng, is_act, bank):
        pairs = bank.rearrange("p (m n) -> p m n", m=2)
        for odd in range(2):
            for half in range(2):
                last = put(eng, is_act, out[half * DH:(half + 1) * DH, odd::2, :],
                           pairs[odd * DH:(odd + 1) * DH, :, :])
        return last

    return (item, halves, src, copies)


def out_projection(core, src, ahead=S_AHEAD):
    nc = core.nc
    hi_made, lo_made = core.semaphore_of("o_hi_made"), core.semaphore_of("o_lo_made")
    hi, lo = core.h_split
    splits = core.split_to(D // WN, ahead)
    first = core.w_taken
    items = D // WN
    with nc.Block() as block:
        @block.sync
        def _(sp):
            core.issue_w(sp, items)

        @block.tensor
        def _(pe):
            for n in range(items):
                core.split_wait(pe, first + n)
                halves = core.w_halves(first + n)
                for t in range(TT):
                    for k in range(KD):
                        if n == 0 and t == 0 and k % 2 == 0:
                            pe.wait_ge(lo_made.sem, lo_made.at(k // 2 + 1))
                        last = in_three(pe, core.y[:, 2 * t + n // 2, (n % 2) * WN:(n % 2 + 1) * WN],
                                        [h[:, k, t * P:(t + 1) * P] for h in core.h_split],
                                        [w[:, k, :] for w in halves], k == 0, k == KD - 1)
                last.then_inc(core.w_used, 1)

        @block.scalar
        def _(act):
            for k in range(0, KD, 2):
                act.activation(hi[:, k:k + 2, :], src[:, k:k + 2, :], ACT.Copy).then_inc(hi_made.sem, 1)
            for n in splits:
                core.split_hi(act, n)

        @block.vector
        def _(dve):
            for k in range(0, KD, 2):
                dve.wait_ge(hi_made.sem, hi_made.at(k // 2 + 1))
                dve.tensor_tensor(lo[:, k:k + 2, :], src[:, k:k + 2, :], hi[:, k:k + 2, :],
                                  ALU.subtract).then_inc(lo_made.sem, 1)

        @block.gpsimd
        def _(pool):
            for n in splits:
                core.split_lo(pool, n)

    hi_made.passed(KD // 2)
    lo_made.passed(KD // 2)
    core.split_issued = splits.stop


LOGITS = 2 * BANK
LBUF = 528
L_BUFS = 3


def attention(core, ctx, mixer, n_units, split=True):
    nc = core.nc
    scored, logits = core.semaphore_of("at_scored"), core.semaphore_of("at_logits")
    raised, weighed = core.semaphore_of("at_raised"), core.semaphore_of("at_weighed")
    turned, copied = core.semaphore_of("at_turned"), core.semaphore_of("at_copied")
    valued, out = core.semaphore_of("at_valued"), core.semaphore_of("at_out")
    primed = core.semaphore_of("at_primed")
    tables = core.semaphore_of("alibi_in")
    splits = core.split_to(0) if split else range(0)
    with ExitStack() as inner:
        L = core.sb(inner, "logits", [P, L_BUFS, LBUF])
        pT = core.sb(inner, "probs_T", [P, 2, 5 * P])
        mx = core.sb(inner, "maxima", [P, L_BUFS, 4])
        sums = core.sb(inner, "sums", [P, L_BUFS, 4])
        block = inner.enter_context(nc.Block())

        def S(u):
            return core.ps[:, 2 * (u % 2):2 * (u % 2) + 2, :].rearrange("p b n -> p (b n)")

        turn_out = core.ps[:, 4:6, :].rearrange("p b n -> p (b n)")

        def O(u):
            return core.ps[:, 6 + u % 2, :]

        @block.sync
        def _(sp):
            core.issue_w(sp, 0)

        @block.tensor
        def _(pe):
            def score(u):
                if u >= 2:
                    pe.wait_ge(logits.sem, logits.at(u - 1))
                for c, n, stationary, moving in mixer.scores(u):
                    last = pe.matmul(S(u)[:, c:c + n], stationary, moving, start=True, stop=True)
                last.then_inc(scored.sem, 1)

            def turn(u):
                pe.wait_ge(weighed.sem, weighed.at(u + 1))
                if u >= 1:
                    pe.wait_ge(copied.sem, copied.at(u))
                for i, (c, n) in enumerate(mixer.tiles(u)):
                    last = pe.transpose(turn_out[0:n, i * P:(i + 1) * P], L[:, u % L_BUFS, c:c + n], core.ident[:])
                last.then_inc(turned.sem, 1)

            def value(u):
                pe.wait_ge(copied.sem, copied.at(u + 1))
                if u >= 2:
                    pe.wait_ge(out.sem, out.at(u - 1))
                mixer.values(pe, u, pT[:, u % 2, :], O(u)).then_inc(valued.sem, 1)

            score(0)
            score(1)
            for u in range(n_units):
                if u + 2 < n_units:
                    score(u + 2)
                turn(u)
                if u >= 1:
                    value(u - 1)
            value(n_units - 1)

        @block.gpsimd
        def _(pool):
            for n in splits:
                core.split_lo(pool, n)

        @block.scalar
        def _(act):
            for n in splits:
                core.split_hi(act, n)

            def prime(u):
                act.wait_ge(scored.sem, scored.at(u + 1))
                mixer.first(act, u, S(u)).then_inc(primed.sem, 1)

            def exps(u):
                act.wait_ge(logits.sem, logits.at(u + 1))
                for g, (c, n) in enumerate(mixer.groups(u)):
                    part = L[:, u % L_BUFS, c:c + n]
                    if mixer.first is not None:
                        last = act.activation(part, part, ACT.Exp)
                    else:
                        last = act.activation(part, part, ACT.Exp, bias=mx[:, u % L_BUFS, g:g + 1],
                                              accum_out=sums[:, u % L_BUFS, g:g + 1])
                last.then_inc(raised.sem, 1)

            def copy(u):
                act.wait_ge(turned.sem, turned.at(u + 1))
                if u >= 2:
                    act.wait_ge(valued.sem, valued.at(u - 1))
                tiles = mixer.tiles(u)
                full = sum(n == P for _, n in tiles)
                last = act.activation(pT[:, u % 2, 0:full * P], turn_out[:, 0:full * P], ACT.Copy)
                if full < len(tiles):
                    n = tiles[-1][1]
                    last = act.activation(pT[0:n, u % 2, full * P:(full + 1) * P],
                                          turn_out[0:n, full * P:(full + 1) * P], ACT.Copy)
                last.then_inc(copied.sem, 1)

            def copy_out(u):
                act.wait_ge(valued.sem, valued.at(u + 1))
                mixer.out(act, u, O(u)).then_inc(out.sem, 1)

            if mixer.first is not None:
                act.preload_act_table_set("natural_log_exp_and_others")
                prime(0)
            for u in range(n_units + 2):
                if mixer.first is not None and u + 1 < n_units:
                    if u >= 1:
                        act.wait_ge(logits.sem, logits.at(u))
                    prime(u + 1)
                if u < n_units:
                    exps(u)
                if 1 <= u <= n_units:
                    copy(u - 1)
                if u >= 2:
                    copy_out(u - 2)

        @block.vector
        def _(dve):
            def logit(u):
                dve.wait_ge(scored.sem, scored.at(u + 1))
                if u >= L_BUFS:
                    dve.wait_ge(turned.sem, turned.at(u - L_BUFS + 1))
                if mixer.first is not None:
                    dve.wait_ge(primed.sem, primed.at(u + 1))
                mixer.logits(dve, u, S(u), L[:, u % L_BUFS, :], mx[:, u % L_BUFS, :]).then_inc(logits.sem, 1)

            def weigh(u):
                dve.wait_ge(raised.sem, raised.at(u + 1))
                mixer.weigh(dve, u, L[:, u % L_BUFS, :], sums[:, u % L_BUFS, :]).then_inc(weighed.sem, 1)

            if mixer.biased:
                dve.wait_ge(tables.sem, tables.at(16))
            logit(0)
            for u in range(n_units):
                if u + 1 < n_units:
                    logit(u + 1)
                weigh(u)

    core.split_issued = splits.stop if split else core.split_issued
    for s in (scored, logits, raised, weighed, turned, copied, valued, out):
        s.passed(n_units)
    if mixer.first is not None:
        primed.passed(n_units)
    if mixer.biased:
        tables.passed(16)


def causal(t):
    return (t + 1) * P


def alibi(core, h, t):
    return core.alibi[:, h, t * P:t * P + causal(t)]


class Softmax:

    first = None
    biased = False

    def finish_maxima(self, dve, mx, n):
        return dve.tensor_scalar(mx[:, 0:n], mx[:, 0:n], -1.0, None, ALU.mult)


class NSA(Softmax):

    biased = True

    def __init__(self, core, ctx):
        self.core = core
        self.qT = core.sb(ctx, "qT", [P, KD, T])
        self.ksT = core.sb(ctx, "ksT", [P, NSA_KV, T])
        self.kwT = core.sb(ctx, "kwT", [P, NSA_KV, T])
        self.vs = core.sb(ctx, "vs", [P, TT, NSA_KV * DH])
        self.vw = core.sb(ctx, "vw", [P, TT, NSA_KV * DH])
        self.gate = core.sb(ctx, "gate", [P, TT, 3 * NSA_HEADS])
        self.kcmpT = core.sb(ctx, "kcmpT", [P, NSA_KV, N_CMP])
        self.vcmp = core.sb(ctx, "vcmp", [N_CMP, NSA_KV, DH])
        self.oT = core.sb(ctx, "oT", [P, KD, T])

    def at(self, u):
        h, t = u // TT, u % TT
        return h, t, slice((h % 2) * DH, (h % 2) * DH + DH), h // NSA_REP

    def scores(self, u):
        h, t, part, g = self.at(u)
        q = self.qT[part, h // 2, t * P:(t + 1) * P]
        n = causal(t)
        return [(0, n, q, self.ksT[part, g, 0:n]), (T, n, q, self.kwT[part, g, 0:n]),
                (2 * T, N_CMP, q, self.kcmpT[part, g, :])]

    def groups(self, u):
        n = causal(u % TT)
        return [(0, n), (T, n), (2 * T, N_CMP)]

    def tiles(self, u):
        n = u % TT + 1
        return [(j * P, P) for j in range(n)] + [(T + j * P, P) for j in range(n)] + [(2 * T, N_CMP)]

    def logits(self, dve, u, S, L, mx):
        core = self.core
        h, t, _, _ = self.at(u)
        for g, (c, n) in enumerate(self.groups(u)):
            bias = alibi(core, h, t) if g < 2 else core.cmp_bias[:, h, t, :]
            last = dve.tensor_tensor_reduce(L[:, c:c + n], S[:, c:c + n], bias, 1.0, -3e38, ALU.add, ALU.max,
                                            mx[:, g:g + 1])
        core.dve_steps.done(dve, last)
        return self.finish_maxima(dve, mx, 3)

    def weigh(self, dve, u, L, sums):
        core = self.core
        h, t, _, _ = self.at(u)
        core.dve_steps.done(dve, dve.reciprocal(sums[:, 0:3], sums[:, 0:3]))
        core.dve_steps.done(dve, dve.tensor_tensor(sums[:, 0:3], sums[:, 0:3],
                                                   self.gate[:, t, 3 * h:3 * h + 3], ALU.mult))
        for g, (c, n) in enumerate(self.groups(u)):
            if g < 2:
                dve.tensor_scalar(L[:, c:c + n], L[:, c:c + n], sums[:, g:g + 1], None, ALU.mult)
            else:
                last = dve.scalar_tensor_tensor(out=L[:, c:c + n], in0=L[:, c:c + n], scalar=sums[:, g:g + 1],
                                                in1=core.cmp_valid[:, t, :], op0=ALU.mult, op1=ALU.mult)
        return last

    def values(self, pe, u, pT, O):
        h, t, part, g = self.at(u)
        vals = [(self.vs, j) for j in range(t + 1)] + [(self.vw, j) for j in range(t + 1)]
        for i, (v, j) in enumerate(vals):
            pe.matmul(O[part, 0:P], v[:, j, g * DH:(g + 1) * DH], pT[:, i * P:(i + 1) * P],
                      start=(i == 0), stop=False)
        i = len(vals)
        return pe.matmul(O[part, 0:P], self.vcmp[:, g, :], pT[0:N_CMP, i * P:(i + 1) * P], start=False, stop=True)

    def out(self, act, u, O):
        h, t, part, _ = self.at(u)
        return act.activation(self.oT[part, h // 2, t * P:(t + 1) * P], O[part, 0:P], ACT.Copy)


class Diff(Softmax):

    biased = True

    def __init__(self, core, ctx, lam_init):
        self.core = core
        self.keep = 1.0 - lam_init
        self.qT = core.sb(ctx, "qT", [P, DIFF_HEADS, T])
        self.kT = core.sb(ctx, "kT", [P, DIFF_HEADS, T])
        self.v = core.sb(ctx, "v", [P, TT, D])
        self.lam = core.sb(ctx, "lam", [P, 1])
        self.o = core.sb(ctx, "o", [P, TT, D])

    def scores(self, u):
        h, t = u // TT, u % TT
        n = causal(t)
        return [(m * BANK, n, self.qT[m * DH:(m + 1) * DH, h, t * P:(t + 1) * P],
                 self.kT[m * DH:(m + 1) * DH, h, 0:n]) for m in range(2)]

    def groups(self, u):
        n = causal(u % TT)
        return [(0, n), (T, n)]

    def tiles(self, u):
        return [(j * P, P) for j in range(u % TT + 1)]

    def logits(self, dve, u, S, L, mx):
        core = self.core
        h, t = u // TT, u % TT
        for g, (c, n) in enumerate(self.groups(u)):
            last = dve.tensor_tensor_reduce(L[:, c:c + n], S[:, g * BANK:g * BANK + n], alibi(core, 2 * h + 1, t), 1.0, -3e38,
                                            ALU.add, ALU.max, mx[:, g:g + 1])
        core.dve_steps.done(dve, last)
        return self.finish_maxima(dve, mx, 2)

    def weigh(self, dve, u, L, sums):
        core = self.core
        n = causal(u % TT)
        core.dve_steps.done(dve, dve.reciprocal(sums[:, 0:2], sums[:, 0:2]))
        core.dve_steps.done(dve, dve.tensor_tensor(sums[:, 1:2], sums[:, 1:2], self.lam[:], ALU.mult))
        core.dve_steps.done(dve, dve.tensor_scalar(L[:, T:T + n], L[:, T:T + n], sums[:, 1:2], None, ALU.mult))
        return dve.scalar_tensor_tensor(out=L[:, 0:n], in0=L[:, 0:n], scalar=sums[:, 0:1], in1=L[:, T:T + n],
                                        op0=ALU.mult, op1=ALU.subtract)

    def values(self, pe, u, pT, O):
        h, t = u // TT, u % TT
        for j in range(t + 1):
            last = pe.matmul(O[:, 0:P], pT[:, j * P:(j + 1) * P], self.v[:, j, h * P:(h + 1) * P],
                             start=(j == 0), stop=(j == t))
        return last

    def out(self, act, u, O):
        h, t = u // TT, u % TT
        return act.activation(self.o[:, t, h * P:(h + 1) * P], O[:, 0:P], ACT.Copy)


class Stick:

    biased = False

    def __init__(self, core, ctx):
        self.core = core
        self.qT = core.sb(ctx, "qT", [P, KD, T])
        self.kT = core.sb(ctx, "kT", [P, KD, T])
        self.v = core.sb(ctx, "v", [P, TT, D])
        self.oT = core.sb(ctx, "oT", [P, KD, T])
        self.soft = core.sb(ctx, "soft", [P, 2, T])
        self.scan = core.sb(ctx, "scan", [P, 2, T])

    def at(self, u):
        h, t = u // TT, u % TT
        return h, t, slice((h % 2) * DH, (h % 2) * DH + DH)

    def scores(self, u):
        h, t, part = self.at(u)
        n = causal(t)
        return [(0, n, self.qT[part, h // 2, t * P:(t + 1) * P], self.kT[part, h // 2, 0:n])]

    def groups(self, u):
        return [(0, causal(u % TT))]

    def tiles(self, u):
        return [(j * P, P) for j in range(u % TT + 1)]

    def first(self, act, u, S):
        n = causal(u % TT)
        soft = self.soft[:, u % 2, 0:n]
        steps = self.core.act_steps
        steps.done(act, act.activation(soft, S[:, 0:n], ACT.Abs))
        steps.done(act, act.activation(soft, soft, ACT.Exp, scale=-1.0))
        return act.activation(soft, soft, ACT.Ln, bias=1.0)

    def logits(self, dve, u, S, L, mx):
        core = self.core
        t = u % TT
        n = causal(t)
        soft, scan = self.soft[:, u % 2, 0:n], self.scan[:, u % 2, 0:n]
        steps = core.dve_steps
        steps.done(dve, dve.scalar_tensor_tensor(out=soft, in0=S[:, 0:n], scalar=0.0, in1=soft,
                                                 op0=ALU.max, op1=ALU.add))
        steps.done(dve, dve.tensor_tensor(soft[:, t * P:n], soft[:, t * P:n], core.before[:], ALU.mult))
        steps.done(dve, dve.tensor_tensor_scan(scan, soft, soft, 0.0, ALU.add, ALU.bypass))
        steps.done(dve, dve.tensor_tensor(L[:, 0:n], S[:, 0:n], soft, ALU.subtract))
        steps.done(dve, dve.tensor_tensor(L[:, 0:n], L[:, 0:n], scan, ALU.add))
        return dve.tensor_scalar(L[:, 0:n], L[:, 0:n], scan[:, n - 1:n], 0.0, ALU.subtract, ALU.min)

    def weigh(self, dve, u, L, sums):
        t = u % TT
        part = L[:, t * P:causal(t)]
        return dve.tensor_tensor(part, part, self.core.before[:], ALU.mult)

    def values(self, pe, u, pT, O):
        h, t, part = self.at(u)
        for j in range(t + 1):
            last = pe.matmul(O[part, 0:P], self.v[:, j, h * DH:(h + 1) * DH], pT[:, j * P:(j + 1) * P],
                             start=(j == 0), stop=(j == t))
        return last

    def out(self, act, u, O):
        h, t, part = self.at(u)
        return act.activation(self.oT[part, h // 2, t * P:(t + 1) * P], O[part, 0:P], ACT.Copy)


NSA_PROJ = 11


def nsa_stage(core, j):
    nc = core.nc
    hT = core.h_split
    with ExitStack() as ctx:
        n = NSA(core, ctx)
        core.alibi = core.sb(ctx, "alibi", [P, NSA_HEADS, P + T])
        with ExitStack() as early:
            srcT = [core.sb(early, f"cmp_src{i}", [P, NSA_KV, T]) for i in range(2)]
            units = [across(core, hT, i, n.qT[:, 2 * i:2 * i + 2, :], DH ** -0.5) for i in range(4)]
            for i in range(2):
                units += [across_twice(core, hT, 4 + i, srcT[i][:])]
            for i, dst in enumerate((n.ksT, n.kwT)):
                units += [across_twice(core, hT, 6 + i, dst[:])]
            units += [along(core, hT, 8, n.vs[:]), along(core, hT, 9, n.vw[:]),
                      along(core, hT, 10, n.gate[:], 3 * NSA_HEADS)]
            projections(core, NSA_PROJ, units, ahead=0, tables=True)
            compress(core, n, j, srcT)
            core.taken_whole()
        attention(core, ctx, n, NSA_HEADS * TT)
        out_projection(core, n.oT)


def compress(core, n, j, srcT):
    nc = core.nc
    consts, blocks = core.semaphore_of("cmp_consts"), core.semaphore_of("cmp_blocks")
    hid, act_h, outs = core.semaphore_of("cmp_hid"), core.semaphore_of("cmp_act"), core.semaphore_of("cmp_outs")
    first = core.w_taken
    nb = NSA_KV * N_CMP
    chunks = CMP_LEN // 2
    with ExitStack() as ctx:
        pe_col = core.sb(ctx, "cmp_pe", [P, 2, chunks])
        w2 = core.sb(ctx, "cmp_w2", [P, 2, 2, DH])
        blk = core.sb(ctx, "cmp_blk", [P, 2, chunks, nb])
        hT = core.sb(ctx, "cmp_hT", [P, 2, 2, nb])
        block = ctx.enter_context(nc.Block())

        @block.sync
        def _(sp):
            sp.dma_start(pe_col[:], core.io["cmp_pe"][j]).then_inc(consts.sem, 16)
            sp.dma_start(w2[:], core.io["cmp_w2"][j]).then_inc(consts.sem, 16)
            core.issue_w(sp, 4)

        @block.vector
        def _(dve):
            dve.wait_ge(consts.sem, consts.at(32))
            for i in range(2):
                for c in range(chunks):
                    for up in range(2):
                        part = slice(up * DH, (up + 1) * DH)
                        t0 = 2 * c + up
                        src = srcT[i][part, :, t0:t0 + (N_CMP - 1) * CMP_STRIDE + 1:CMP_STRIDE]
                        dst = blk[part, i, c, :].rearrange("p (g n) -> p g n", g=NSA_KV)
                        last = dve.tensor_scalar(dst, src, pe_col[part, i, c:c + 1], None, ALU.add)
                last.then_inc(blocks.sem, 1)
            for i in range(2):
                dve.wait_ge(outs.sem, outs.at(i + 1))
                if i == 0:
                    dve.tensor_copy(n.kcmpT[:].rearrange("p g n -> p (g n)"), core.ps[:, 4, 0:nb])
                else:
                    for g in range(NSA_KV):
                        dve.tensor_copy(n.vcmp[:, g, :], core.ps[0:N_CMP, 5, g * DH:(g + 1) * DH])

        @block.scalar
        def _(act):
            gate = n.gate[:]
            core.act_steps.done(act, act.activation(gate, gate, ACT.Sigmoid))
            for i in range(2):
                act.wait_ge(hid.sem, hid.at(i + 1))
                for m in range(2):
                    last = act.activation(hT[:, i, m, :], core.ps[:, 2 * i + m, 0:nb], ACT.Gelu_apprx_tanh)
                last.then_inc(act_h.sem, 1)

        @block.tensor
        def _(pe):
            for i in range(2):
                pe.wait_ge(blocks.sem, blocks.at(i + 1))
                for part in range(2):
                    item = first + 2 * i + part
                    core.w_wait(pe, item)
                    w = core.w_item(item)
                    for k in range(KD):
                        for m in range(2):
                            last = pe.matmul(core.ps[:, 2 * i + m, 0:nb], w[:, k, m * P:(m + 1) * P],
                                             blk[:, i, part * KD + k, :],
                                             start=(part == 0 and k == 0), stop=(part == 1 and k == KD - 1))
                    last.then_inc(core.w_used, 1)
                pe.wait_ge(core.w_used, item + 1)
                pe.sem_inc(hid.sem, 1)
            for i in range(2):
                pe.wait_ge(act_h.sem, act_h.at(i + 1))
                if i == 0:
                    for half in range(2):
                        for m in range(2):
                            last = pe.matmul(core.ps[half * DH:(half + 1) * DH, 4, 0:nb], w2[:, 0, m, :],
                                             hT[:, 0, m, :], start=(m == 0), stop=(m == 1))
                else:
                    for g in range(NSA_KV):
                        for m in range(2):
                            last = pe.matmul(core.ps[0:N_CMP, 5, g * DH:(g + 1) * DH],
                                             hT[:, 1, m, g * N_CMP:(g + 1) * N_CMP], w2[:, 1, m, :],
                                             start=(m == 0), stop=(m == 1))
                last.then_inc(outs.sem, 1)

    consts.passed(32)
    for s in (blocks, hid, act_h, outs):
        s.passed(2)


def stick_stage(core):
    with ExitStack() as ctx:
        n = Stick(core, ctx)
        units = [across(core, core.h_split, i, n.qT[:, 2 * i:2 * i + 2, :], DH ** -0.5) for i in range(4)]
        units += [across(core, core.h_split, 4 + i, n.kT[:, 2 * i:2 * i + 2, :]) for i in range(4)]
        units += [along(core, core.h_split, 8 + i, n.v[:, :, i * WN:(i + 1) * WN]) for i in range(4)]
        projections(core, 12, units)
        attention(core, ctx, n, (D // DH) * TT)
        out_projection(core, n.oT)


def diff_stage(core, layer):
    nc = core.nc
    lam_init = 0.8 - 0.6 * float(np.exp(-0.3 * layer))
    consts, lam_sums, lam_exps = core.semaphore_of("diff_consts"), core.semaphore_of("diff_sums"), core.semaphore_of("diff_exps")
    ss, roots = core.semaphore_of("diff_squares"), core.semaphore_of("diff_roots")
    normed, turned = core.semaphore_of("diff_normed"), core.semaphore_of("diff_turned")
    with ExitStack() as ctx:
        n = Diff(core, ctx, lam_init)
        core.alibi = core.sb(ctx, "alibi", [P, NSA_HEADS, P + T])
        lam_in = core.sb(ctx, "lam_in", [P, 4, DH])
        lam_s = core.sb(ctx, "lam_s", [P, 2])
        junk = core.sb(ctx, "lam_junk", [P, 2, DH])
        g = core.sb(ctx, "subln_g", [P, P])
        units = [across(core, core.h_split, i, n.qT[:, 2 * i:2 * i + 2, :], DH ** -0.5) for i in range(4)]
        units += [across(core, core.h_split, 4 + i, n.kT[:, 2 * i:2 * i + 2, :]) for i in range(4)]
        units += [along(core, core.h_split, 8 + i, n.v[:, :, i * WN:(i + 1) * WN]) for i in range(4)]
        projections(core, 12, units, tables=True)
        with nc.Block() as block:
            @block.sync
            def _(sp):
                lam_dram = core.io["diff_lam"].rearrange("a n d -> a (n d)")
                sp.dma_start(lam_in[:].rearrange("p n d -> p (n d)"),
                             lam_dram.partition_broadcast(P)).then_inc(consts.sem, 16)
                sp.dma_start(g[:], core.io["subln_g"].partition_broadcast(P)).then_inc(consts.sem, 16)

            @block.vector
            def _(dve):
                dve.wait_ge(consts.sem, consts.at(32))
                for i in range(2):
                    last = dve.tensor_tensor_reduce(junk[:, i, :], lam_in[:, 2 * i, :], lam_in[:, 2 * i + 1, :],
                                                    1.0, 0.0, ALU.mult, ALU.add, lam_s[:, i:i + 1])
                last.then_inc(lam_sums.sem, 1)
                dve.wait_ge(lam_exps.sem, lam_exps.at(1))
                core.dve_steps.done(dve, dve.tensor_tensor(n.lam[:], lam_s[:, 0:1], lam_s[:, 1:2], ALU.subtract))
                dve.tensor_scalar(n.lam[:], n.lam[:], lam_init, None, ALU.add)

            @block.scalar
            def _(act):
                act.wait_ge(lam_sums.sem, lam_sums.at(1))
                act.activation(lam_s[:], lam_s[:], ACT.Exp).then_inc(lam_exps.sem, 1)
        attention(core, ctx, n, DIFF_HEADS * TT)
        oT = n.qT
        with ExitStack() as inner:
            sq = core.sb(inner, "sq", [P, TT, D])
            st = core.sb(inner, "st", [P, 2, TT, DIFF_HEADS])
            block = inner.enter_context(nc.Block())

            @block.vector
            def _(dve):
                o4 = n.o[:].rearrange("p t (h e) -> p t h e", h=DIFF_HEADS)
                sq4 = sq[:].rearrange("p t (h e) -> p t h e", h=DIFF_HEADS)
                core.dve_steps.done(dve, dve.tensor_tensor(sq[:], n.o[:], n.o[:], ALU.mult))
                core.dve_steps.done(dve, dve.tensor_reduce(st[:, 0], sq4, AX.X, ALU.add))
                dve.tensor_scalar(st[:, 0], st[:, 0], 1.0 / P, EPS, ALU.mult, ALU.add).then_inc(ss.sem, 1)
                dve.wait_ge(roots.sem, roots.at(1))
                core.dve_steps.done(dve, dve.reciprocal(st[:, 1], st[:, 0]))
                for t in range(TT):
                    core.dve_steps.done(dve, dve.tensor_tensor(sq4[:, t], o4[:, t], wide(st[:, 1, t, :], P), ALU.mult))
                    gb = bass.AP(g[:].tensor, g[:].offset, [list(g[:].ap[0]), [0, DIFF_HEADS], list(g[:].ap[1])])
                    core.dve_steps.done(dve, dve.scalar_tensor_tensor(
                        out=sq4[:, t], in0=sq4[:, t], scalar=n.keep, in1=gb, op0=ALU.mult, op1=ALU.mult))
                    dve.sem_inc(normed.sem, 1)

            @block.scalar
            def _(act):
                act.wait_ge(ss.sem, ss.at(1))
                act.activation(st[:, 0], st[:, 0], ACT.Sqrt).then_inc(roots.sem, 1)
                for k in range(0, KD, 2):
                    act.wait_ge(turned.sem, turned.at(k // 2 + 1))
                    act.activation(oT[:, k:k + 2, :], core.ps[:, k // 2, :].rearrange("p (k n) -> p k n", k=2),
                                   ACT.Copy)

            @block.tensor
            def _(pe):
                pe.wait_ge(normed.sem, normed.at(TT))
                for k in range(KD):
                    for t in range(TT):
                        last = pe.transpose(core.ps[:, k // 2, (k % 2) * T + t * P:(k % 2) * T + (t + 1) * P],
                                            sq[:, t, k * P:(k + 1) * P], core.ident[:])
                    if k % 2:
                        last.then_inc(turned.sem, 1)
        out_projection(core, oT)
    consts.passed(32)
    for s in (lam_sums, lam_exps, ss, roots):
        s.passed(1)
    normed.passed(TT)
    turned.passed(KD // 2)


def second_block(core):
    taken = {"nsa": 0}
    with ExitStack() as ctx:
        core.start_splits(ctx)
        core.mod_cols = core.sb(ctx, "mod_cols", [P, MOD_COLS // P])
        core.cmp_bias = core.sb(ctx, "cmp_bias", [P, NSA_HEADS, TT, N_CMP])
        core.cmp_valid = core.sb(ctx, "cmp_valid", [P, TT, N_CMP])
        core.before = core.sb(ctx, "before", [P, P])
        tables = core.semaphore_of("attention_tables")
        with core.nc.Block() as block:
            @block.scalar
            def _(act):
                act.dma_start(core.cmp_bias[:], core.io["cmp_bias"]).then_inc(tables.sem, 16)
                act.dma_start(core.cmp_valid[:], core.io["cmp_valid"]).then_inc(tables.sem, 16)
                act.dma_start(core.before[:], core.io["before"]).then_inc(tables.sem, 16)
                act.wait_ge(tables.sem, tables.at(48))
        tables.passed(48)
        norm_stage(core, None, 0)
        for layer, kind in enumerate(MIXERS):
            last = layer == DEPTH - 1
            ffn_stage(core, None if last else (layer + 1, 0))
            norm_stage(core, 0, 1)
            if kind == "nsa":
                nsa_stage(core, taken["nsa"])
                taken["nsa"] += 1
            elif kind == "stick":
                stick_stage(core)
            else:
                diff_stage(core, layer)
            norm_stage(core, 1, 2)
            ffn_stage(core, None if last else (layer + 1, 1))
            norm_stage(core, 2, None)
            if not last:
                mod_stage(core, layer + 1)
                norm_stage(core, None, 0)


def w_items(w):
    n = w.shape[1] // WN
    return w.reshape(KD, P, n, WN).transpose(2, 1, 0, 3).reshape(n, P, ITEM)


def padded(w):
    n = -w.shape[1] % WN
    return np.concatenate([w, np.zeros((w.shape[0], n), w.dtype)], 1) if n else w


def ffn_items(w1, w2):
    gate, up = w_items(w1[:, :D_FF]), w_items(w1[:, D_FF:])
    down = w2.reshape(FF_STEPS, 2, P, D).transpose(0, 2, 1, 3).reshape(FF_STEPS, P, ITEM)
    order = [gate[:1], up[:1]]
    for s in range(FF_STEPS - 1):
        order += [gate[s + 1:s + 2], up[s + 1:s + 2], down[s:s + 1]]
    return order + [down[FF_STEPS - 1:]]


def columns_of(v):
    return np.ascontiguousarray(np.swapaxes(v.reshape(*v.shape[:-1], v.shape[-1] // P, P), -1, -2))


def attention_tables():
    q = np.arange(P)[:, None]
    alibi = np.zeros((P, NSA_HEADS, P + T), np.float32)
    cmp_bias = np.zeros((P, NSA_HEADS, TT, N_CMP), np.float32)
    cmp_valid = np.zeros((P, TT, N_CMP), np.float32)
    ends = np.arange(N_CMP)[None, :] * CMP_STRIDE + CMP_LEN - 1
    for t in range(TT):
        dist = (q + t * P - np.arange(causal(t))[None, :]).astype(np.float32)
        near = (q + t * P - ends).astype(np.float32)
        cmp_valid[:, t] = near >= 0
        for h in range(NSA_HEADS):
            slope = np.float32(SLOPES[h])
            alibi[:, h, t * P:t * P + causal(t)] = np.where(dist >= 0, -slope * dist, np.float32(NEG))
            cmp_bias[:, h, t] = np.where(near >= 0, -slope * near, np.float32(NEG))
    before = (np.arange(P)[None, :] < q).astype(np.float32)
    return {"alibi": alibi, "cmp_bias": cmp_bias, "cmp_valid": cmp_valid, "before": before,
            "ident": np.eye(P, dtype=np.float32)}


def second_layout(a):
    w = []
    nsa = 0
    for layer, kind in enumerate(MIXERS):
        w += ffn_items(a["ffn_w1_2"][layer, 0], a["ffn_w2_2"][layer, 0])
        if kind == "nsa":
            cols = a["nsa_w_in_2"][nsa]
            main = NSA_HEADS * DH + 6 * NSA_KV * DH
            q, kc, vc, ks, vs, kw, vw = np.split(cols[:, :main], [1024 + 256 * i for i in range(6)], 1)
            gates = cols[:, main:].reshape(D, NSA_HEADS, 3)[:, :, [1, 2, 0]].reshape(D, 3 * NSA_HEADS)
            w += [w_items(x) for x in (q, kc, vc, ks, kw, vs, vw, padded(gates))]
            w += [a["nsa_cmp_w1_2"][nsa].reshape(2, 2, KD, P, CMP_HID).transpose(0, 1, 3, 2, 4).reshape(4, P, ITEM)]
            w += [w_items(a["nsa_w_out_2"][nsa])]
            nsa += 1
        else:
            name = "sb" if kind == "stick" else "diff"
            w += [w_items(a[name + "_w_in_2"][0]), w_items(a[name + "_w_out_2"][0])]
        w += ffn_items(a["ffn_w1_2"][layer, 1], a["ffn_w2_2"][layer, 1])
    norm = a["norm_g_2"]
    mods = np.concatenate([w_items(a["ada_w_2"][i]) for i in range(DEPTH)])
    small = {
        "norm_pre": np.ascontiguousarray(columns_of(norm[:, 0::2]).transpose(2, 0, 1, 3)),
        "norm_post": np.ascontiguousarray(columns_of(norm[:, 1::2]).transpose(2, 0, 1, 3)),
        "mod_bias2": np.ascontiguousarray(a["ada_b_2"].reshape(DEPTH, 1, MOD_COLS // P, P).transpose(3, 0, 1, 2)),
        "cond2_in": columns_of(a["c_2"][0]),
        "cmp_pe": np.ascontiguousarray(
            a["nsa_cmp_pe_2"].reshape(-1, 2, CMP_LEN // 2, 2, DH).transpose(0, 3, 4, 1, 2).reshape(-1, P, 2, CMP_LEN // 2)),
        "cmp_w2": np.ascontiguousarray(a["nsa_cmp_w2_2"].reshape(-1, 2, 2, P, DH).transpose(0, 3, 1, 2, 4)),
        "diff_lam": np.ascontiguousarray(a["diff_lam_2"]),
        "subln_g": np.ascontiguousarray(a["diff_subln_g_2"]),
    }
    return w, mods, small


RW_W = 256
RW_H = RW_W // DH
CHUNK = 64
NCH = 2 * T // CHUNK
LEVELS = 6
LOG_DECAY = -float(np.exp(-0.5))
ROOT_EPS = 1e-12


def heads(ap):
    return ap.rearrange("p (h n) -> p h n", h=RW_H)


def spread(ap, n):
    return bass.AP(ap.tensor, ap.offset, [list(ap.ap[0]), [0, n]] + [list(x) for x in ap.ap[1:]])


def place_of(t, c, d):
    n = 2 * (t % TT) + c
    return NCH // 2 * (t // TT) + (NCH // 2 - 1 - n if d else n)


class Recurrence:

    def __init__(self, core, ctx):
        sb = lambda name, shape: core.sb(ctx, name, shape)
        self.psi = sb("psi", [P, NCH, RW_H, DH])
        self.gamma = sb("gamma", [P, NCH, RW_H, DH])
        self.p_end = sb("p_end", [P, NCH, RW_H])
        self.state = sb("state", [P, NCH + 1, RW_H, DH])
        self.qT = sb("rw_qT", [P, TT, RW_H, P])
        self.y = sb("rw_y", [P, TT, RW_W])
        self.masks = sb("rw_masks", [P, 2, 4 + LEVELS, P])
        self.chunk_sum = sb("chunk_sum", [P, 2])
        self.w0a0 = sb("w0a0", [P, 2, 2 * RW_W])
        self.rows = sb("rw_rows", [P, 4, RW_W])
        self.up = sb("rw_up", [P, 2, RW_W])


def rw_tile_stage(core, rw, a, t):
    nc = core.nc
    is_x = t >= TT
    names = ("kk_root", "kk_done", "wa_up", "wa_in", "wa_out", "cums", "p_ready", "ends", "nats", "turn1", "turn1_out",
             "tri", "tri_out", "lvl_in", "lvl_z", "lvl_z_out", "lvl_x", "lvl_x_out", "cv", "cv_out",
             "mg", "mg_out", "maps", "maps_out", "kk_sum")
    s = {n: core.semaphore_of("rw_" + n) for n in names}
    with ExitStack() as ctx:
        early = core.sb(ctx, "early", [P, 2, 6 * RW_W])
        late = early
        kk = core.sb(ctx, "kk", [P, 2, RW_W])
        st = core.sb(ctx, "kk_st", [P, RW_H])
        bx = core.sb(ctx, "bx", [P, 2, 2, RW_W])
        kc = core.sb(ctx, "kc", [P, 2, RW_H, P])
        mg = core.sb(ctx, "mg", [P, 2, RW_H, P])
        chT = core.sb(ctx, "chT", [P, 4, RW_H, P])
        tri = core.sb(ctx, "tri", [P, 2, 4, RW_H, P])
        block = ctx.enter_context(nc.Block())
        n_ch = 4 if is_x else 3

        def wa(d):
            return early[:, d, 0:2 * RW_W]

        def decay(d, which):
            return early[:, d, (2 + which) * RW_W:(3 + which) * RW_W]

        def tmp(d):
            return early[:, d, 5 * RW_W:6 * RW_W]

        def lvl(d, which):
            return late[:, d, which * BANK:(which + 1) * BANK].rearrange("p (h n) -> p h n", h=RW_H)

        def bank(i):
            return core.ps[:, i, :].rearrange("p (h n) -> p h n", h=RW_H)

        def part(d):
            return slice(d * DH, (d + 1) * DH)

        tok = slice(t * P, (t + 1) * P)

        @block.sync
        def _(sp):
            core.issue_w(sp, 0)

        @block.scalar
        def _(act):
            act.wait_ge(s["kk_sum"].sem, s["kk_sum"].at(1))
            act.activation(st[:], st[:], ACT.Sqrt).then_inc(s["kk_root"].sem, 1)
            for d in range(2):
                act.wait_ge(s["wa_in"].sem, s["wa_in"].at(d + 1))
                act.activation(wa(d), wa(d), ACT.Sigmoid).then_inc(s["wa_out"].sem, 1)
            for d in range(2):
                act.wait_ge(s["cums"].sem, s["cums"].at(d + 1))
                act.activation(early[:, d, 2 * RW_W:4 * RW_W], core.ps[:, 2 + d, :], ACT.Exp)
                act.activation(decay(d, 2), core.ps[:, 2 + d, 0:RW_W], ACT.Exp, scale=-1.0)
                for c in range(2):
                    last = act.activation(rw.p_end[part(d), place_of(t, c, d), :],
                                          core.ps[part(d), 4 + d, c:c + 2 * RW_H - 1:2], ACT.Exp)
                last.then_inc(s["p_ready"].sem, 1)
            for d in range(2):
                for i in range(n_ch):
                    n = n_ch * d + i
                    act.wait_ge(s["turn1"].sem, s["turn1"].at(n + 1))
                    act.activation(chT[part(d), i, :, :], bank(4 + i)[0:DH], ACT.Copy).then_inc(
                        s["turn1_out"].sem, 1)
            for level in range(LEVELS):
                for d in range(2):
                    n = 2 * level + d
                    act.wait_ge(s["lvl_z"].sem, s["lvl_z"].at(n + 1))
                    act.activation(lvl(d, 2), bank(4 * d), ACT.Copy).then_inc(s["lvl_z_out"].sem, 1)
            for d in range(2):
                act.wait_ge(s["cv"].sem, s["cv"].at(d + 1))
                act.activation(kc[:, d, :, DH:P], heads(core.ps[:, 4 * d, 0:RW_W]), ACT.Copy).then_inc(
                    s["cv_out"].sem, 1)
            for d in range(2):
                act.wait_ge(s["mg"].sem, s["mg"].at(d + 1))
                act.activation(mg[:, d, :, :], bank(4 * d + 1), ACT.Copy, scale=-1.0).then_inc(
                    s["mg_out"].sem, 1)

        @block.vector
        def _(dve):
            steps = core.dve_steps
            k, v = a.k[:, t, :], a.v[:, t, :]
            kk_raw, kk_n = kk[:, 0, :], kk[:, 1, :]
            steps.done(dve, dve.tensor_tensor(kk_raw, k, rw.rows[:, 0, :], ALU.mult))
            steps.done(dve, dve.tensor_tensor(kk_n, kk_raw, kk_raw, ALU.mult))
            steps.done(dve, dve.tensor_reduce(st[:], heads(kk_n), AX.X, ALU.add))
            dve.tensor_scalar(st[:], st[:], ROOT_EPS, None, ALU.add).then_inc(s["kk_sum"].sem, 1)
            for d in range(2):
                dve.wait_ge(s["wa_up"].sem, s["wa_up"].at(d + 1))
                dve.tensor_tensor(wa(d), core.ps[:, d, :], rw.w0a0[:, d, :], ALU.add).then_inc(s["wa_in"].sem, 1)
            dve.wait_ge(s["kk_root"].sem, s["kk_root"].at(1))
            steps.done(dve, dve.reciprocal(st[:], st[:]))
            steps.done(dve, dve.tensor_tensor(heads(kk_n), heads(kk_raw), wide(st[:], DH), ALU.mult))
            for d in range(2):
                dve.wait_ge(s["p_ready"].sem, s["p_ready"].at(d + 1))
                a_in = wa(d)[:, RW_W:]
                dve.tensor_tensor(kc[:, d, :, 0:DH], heads(decay(d, 1)), heads(kk_n), ALU.mult)
                steps.done(dve, dve.tensor_tensor(tmp(d), kk_n, a_in, ALU.mult))
                steps.done(dve, dve.tensor_tensor(bx[:, d, 0, :], tmp(d), decay(d, 2), ALU.mult))
                steps.done(dve, dve.scalar_tensor_tensor(out=tmp(d), in0=a_in, scalar=-1.0, in1=rw.rows[:, 1, :],
                                                         op0=ALU.add, op1=ALU.mult))
                steps.done(dve, dve.scalar_tensor_tensor(out=tmp(d), in0=tmp(d), scalar=1.0, in1=k,
                                                         op0=ALU.add, op1=ALU.mult))
                last = dve.tensor_tensor(bx[:, d, 1, :], tmp(d), decay(d, 2), ALU.mult)
                if is_x:
                    steps.done(dve, last)
                    last = dve.tensor_tensor(decay(d, 0), decay(d, 0), a.r[:, t - TT, :], ALU.mult)
                last.then_inc(s["nats"].sem, 1)
            for d in range(2):
                for i in range(4 if is_x else 2):
                    n = (4 if is_x else 2) * d + i
                    dve.wait_ge(s["tri"].sem, s["tri"].at(n + 1))
                    dve.tensor_tensor(tri[:, d, i, :, :], bank(4 * d + i), spread(rw.masks[:, d, i // 2, :], RW_H),
                                      ALU.mult).then_inc(s["tri_out"].sem, 1)
            dve.wait_ge(s["turn1"].sem, s["turn1"].at(2 * n_ch))
            for d in range(2):
                for i in range(2):
                    last = dve.tensor_copy(lvl(d, i), spread(core.ident[:], RW_H))
            steps.done(dve, last)
            for level in range(LEVELS):
                for d in range(2):
                    n = 2 * level + d
                    if level == 0:
                        dve.wait_ge(s["tri_out"].sem, s["tri_out"].at((4 if is_x else 2) * d + 1))
                    else:
                        dve.wait_ge(s["lvl_x"].sem, s["lvl_x"].at(n - 1))
                        for i in range(2):
                            dve.tensor_tensor(lvl(d, i), lvl(d, i), bank(4 * d + 1 + i), ALU.subtract)
                    dve.tensor_tensor(lvl(d, 2), tri[:, d, 0, :, :], spread(rw.masks[:, d, 4 + level, :], RW_H),
                                      ALU.mult).then_inc(s["lvl_in"].sem, 1)
            for d in range(2):
                dve.wait_ge(s["lvl_x"].sem, s["lvl_x"].at(2 * LEVELS - 1 + d))
                dve.tensor_tensor(lvl(d, 1), lvl(d, 1), bank(4 * d + 2), ALU.subtract).then_inc(
                    s["lvl_x_out"].sem, 1)
            for d in range(2):
                dve.wait_ge(s["maps"].sem, s["maps"].at(d + 1))
                for c in range(2):
                    n = place_of(t, c, d)
                    eye = core.ident[part(d), d * DH:(d + 1) * DH]
                    src = core.ps[part(d), 4 * d + c, :]
                    dve.tensor_tensor(rw.psi[part(d), n, :, :], heads(src[:, 0:RW_W]), spread(eye, RW_H), ALU.add)
                    last = dve.tensor_copy(rw.gamma[part(d), n, :, :], heads(src[:, RW_W:]))
                if is_x:
                    x = t - TT
                    dve.tensor_tensor(rw.qT[part(d), x, :, :], bank(4 * d + 2)[part(d)], chT[part(d), 3, :, :], ALU.add)
                    y = core.ps[:, 4 * d + 3, 0:RW_W]
                    if d == 0:
                        last = dve.tensor_copy(rw.y[:, x, :], y)
                        steps.done(dve, last)
                    else:
                        dve.tensor_tensor(rw.y[:, x, :], rw.y[:, x, :], y, ALU.add)

        @block.tensor
        def _(pe):
            for d in range(2):
                for i in range(2):
                    last = pe.matmul(core.ps[:, d, i * RW_W:(i + 1) * RW_W], a.waT[part(d), i, tok],
                                     rw.up[part(d), i, :], start=True, stop=True)
                last.then_inc(s["wa_up"].sem, 1)
            for d in range(2):
                pe.wait_ge(s["wa_out"].sem, s["wa_out"].at(d + 1))
                for h in range(RW_H):
                    pe.matmul(core.ps[part(d), 4 + d, 2 * h:2 * h + 2], early[:, d, h * DH:(h + 1) * DH],
                              rw.chunk_sum[:], start=True, stop=True)
                for i in range(2):
                    last = pe.matmul(core.ps[:, 2 + d, i * RW_W:(i + 1) * RW_W], rw.masks[:, d, 2 + i, :],
                                     early[:, d, 0:RW_W], start=True, stop=True)
                last.then_inc(s["cums"].sem, 1)
            pe.wait_ge(s["p_ready"].sem, s["p_ready"].at(2))
            for d in range(2):
                pe.wait_ge(s["nats"].sem, s["nats"].at(d + 1))
                for i in range(n_ch):
                    if d:
                        pe.wait_ge(s["turn1_out"].sem, s["turn1_out"].at(i + 1))
                    for h in range(RW_H):
                        src = (kc[:, d, h, 0:DH], bx[:, d, 0, h * DH:(h + 1) * DH],
                               bx[:, d, 1, h * DH:(h + 1) * DH], decay(d, 0)[:, h * DH:(h + 1) * DH])[i]
                        last = pe.transpose(core.ps[0:DH, 4 + i, h * P:(h + 1) * P], src, core.ident[:])
                    last.then_inc(s["turn1"].sem, 1)
            for d in range(2):
                pe.wait_ge(s["turn1_out"].sem, s["turn1_out"].at(n_ch * (d + 1)))
                for i in range(4 if is_x else 2):
                    src, dst = ((1, 0), (2, 0), (1, 3), (2, 3))[i]
                    for h in range(RW_H):
                        last = pe.matmul(core.ps[:, 4 * d + i, h * P:(h + 1) * P], chT[part(d), src, h, :],
                                         chT[part(d), dst, h, :], start=True, stop=True)
                    last.then_inc(s["tri"].sem, 1)
            for level in range(LEVELS):
                for d in range(2):
                    n = 2 * level + d
                    if level == 0:
                        pe.wait_ge(s["tri_out"].sem, s["tri_out"].at((4 if is_x else 2) * (d + 1)))
                    pe.wait_ge(s["lvl_in"].sem, s["lvl_in"].at(n + 1))
                    for h in range(RW_H):
                        last = pe.matmul(bank(4 * d)[:, h, :], lvl(d, 2)[:, h, :], lvl(d, 0)[:, h, :],
                                         start=True, stop=True)
                    last.then_inc(s["lvl_z"].sem, 1)
                for d in range(2):
                    n = 2 * level + d
                    pe.wait_ge(s["lvl_z_out"].sem, s["lvl_z_out"].at(n + 1))
                    for h in range(RW_H):
                        pe.matmul(bank(4 * d + 1)[:, h, :], lvl(d, 1)[:, h, :], lvl(d, 2)[:, h, :],
                                  start=True, stop=True)
                        last = pe.matmul(bank(4 * d + 2)[:, h, :], lvl(d, 2)[:, h, :], lvl(d, 1)[:, h, :],
                                         start=True, stop=True)
                    last.then_inc(s["lvl_x"].sem, 1)
            for d in range(2):
                for h in range(RW_H):
                    last = pe.matmul(core.ps[:, 4 * d, h * DH:(h + 1) * DH], tri[:, d, 1, h, :],
                                     a.v[:, t, h * DH:(h + 1) * DH], start=True, stop=True)
                last.then_inc(s["cv"].sem, 1)
            for d in range(2):
                pe.wait_ge(s["cv_out"].sem, s["cv_out"].at(d + 1))
                pe.wait_ge(s["lvl_x_out"].sem, s["lvl_x_out"].at(d + 1))
                for h in range(RW_H):
                    last = pe.matmul(bank(4 * d + 1)[:, h, :], lvl(d, 1)[:, h, :], kc[:, d, h, :],
                                     start=True, stop=True)
                last.then_inc(s["mg"].sem, 1)
            for d in range(2):
                pe.wait_ge(s["mg_out"].sem, s["mg_out"].at(d + 1))
                if is_x:
                    for h in range(RW_H):
                        pe.matmul(core.ps[part(d), 4 * d + 2, h * P:(h + 1) * P], mg[:, d, h, 0:DH],
                                  tri[:, d, 2, h, :], start=True, stop=True)
                    for h in range(RW_H):
                        y = core.ps[:, 4 * d + 3, h * DH:(h + 1) * DH]
                        pe.matmul(y, tri[:, d, 3, h, :], a.v[:, t, h * DH:(h + 1) * DH], start=True, stop=False)
                        pe.matmul(y, tri[:, d, 2, h, :], mg[:, d, h, DH:P], start=False, stop=True)
                for c in range(2):
                    ch = slice(c * CHUNK, (c + 1) * CHUNK)
                    for h in range(RW_H):
                        hd = slice(h * DH, (h + 1) * DH)
                        pe.matmul(core.ps[part(d), 4 * d + c, hd], mg[ch, d, h, 0:DH], bx[ch, d, 0, hd],
                                  start=True, stop=True)
                    for h in range(RW_H):
                        hd = slice(h * DH, (h + 1) * DH)
                        dst = core.ps[part(d), 4 * d + c, RW_W + h * DH:RW_W + (h + 1) * DH]
                        pe.matmul(dst, bx[ch, d, 1, hd], a.v[ch, t, hd], start=True, stop=False)
                        last = pe.matmul(dst, bx[ch, d, 0, hd], mg[ch, d, h, DH:P], start=False, stop=True)
                    core.pe_steps.done(pe, last)
                pe.sem_inc(s["maps"].sem, 1)

    for n in ("kk_root", "kk_sum"):
        s[n].passed(1)
    for n in ("wa_up", "wa_in", "wa_out", "cums", "p_ready", "nats", "cv", "cv_out", "mg", "mg_out", "maps",
              "lvl_x_out"):
        s[n].passed(2)
    for n in ("turn1", "turn1_out"):
        s[n].passed(2 * n_ch)
    for n in ("tri", "tri_out"):
        s[n].passed(8 if is_x else 4)
    for n in ("lvl_in", "lvl_z", "lvl_z_out", "lvl_x"):
        s[n].passed(2 * LEVELS)


def rw_chain_stage(core, rw):
    nc = core.nc
    moved = [core.semaphore_of(f"state_moved{d}") for d in range(2)]
    kept = [core.semaphore_of(f"state_kept{d}") for d in range(2)]
    y_done = core.semaphore_of("rw_y_done")

    def part(d):
        return slice(d * DH, (d + 1) * DH)

    with nc.Block() as block:
        @block.sync
        def _(sp):
            core.issue_w(sp, 0)

        @block.tensor
        def _(pe):
            for n in range(1, NCH):
                for d in range(2):
                    pe.wait_ge(kept[d].sem, kept[d].at(n))
                    for h in range(RW_H):
                        last = pe.matmul(core.ps[part(d), d, h * DH:(h + 1) * DH], rw.psi[part(d), n, h, :],
                                         rw.state[part(d), n, h, :], start=True, stop=True)
                    last.then_inc(moved[d].sem, 1)
            for d in range(2):
                for x in range(TT):
                    for c in range(2):
                        n = place_of(TT + x, c, d)
                        for h in range(RW_H):
                            last = pe.matmul(
                                core.ps[c * CHUNK:(c + 1) * CHUNK, 2 + d, x * RW_W + h * DH:x * RW_W + (h + 1) * DH],
                                rw.qT[part(d), x, h, c * CHUNK:(c + 1) * CHUNK], rw.state[part(d), n, h, :],
                                start=True, stop=True)
                last.then_inc(y_done.sem, 1)

        @block.vector
        def _(dve):
            for n in range(NCH):
                for d in range(2):
                    new = rw.state[part(d), n + 1, :, :]
                    end = wide(rw.p_end[part(d), n, :], DH)
                    src = rw.gamma[part(d), n, :, :]
                    if n:
                        dve.wait_ge(moved[d].sem, moved[d].at(n))
                        core.dve_steps.done(dve, dve.tensor_tensor(
                            new, heads(core.ps[part(d), d, 0:RW_W]), src, ALU.add))
                        src = new
                    dve.tensor_tensor(new, src, end, ALU.mult).then_inc(kept[d].sem, 1)
            for d in range(2):
                dve.wait_ge(y_done.sem, y_done.at(d + 1))
                core.dve_steps.done(dve, dve.tensor_tensor(
                    rw.y[:], rw.y[:], core.ps[:, 2 + d, :].rearrange("p (t n) -> p t n", t=TT), ALU.add))

    for d in range(2):
        moved[d].passed(NCH - 1)
        kept[d].passed(NCH)
    y_done.passed(2)


def rw_output_stage(core, rw, a, outT):
    nc = core.nc
    gate, gates = core.semaphore_of("rw_gate"), core.semaphore_of("rw_gates")
    var, root = core.semaphore_of("rw_var"), core.semaphore_of("rw_root")
    done, turned = core.semaphore_of("rw_done"), core.semaphore_of("rw_turned")
    consts = core.semaphore_of("rw_g_up")
    with ExitStack() as ctx:
        g_up = core.sb(ctx, "g_up", [P, RW_W])
        sq = core.sb(ctx, "rw_sq", [P, TT, RW_W])
        bonus = core.sb(ctx, "rw_bonus", [P, TT, RW_W])
        st = core.sb(ctx, "rw_st", [P, 3, TT * RW_H])
        block = ctx.enter_context(nc.Block())

        def by_head(ap):
            return ap.rearrange("p t (h n) -> p (t h) n", h=RW_H)

        def rows(i):
            return spread(rw.rows[:, i, :], TT)

        @block.sync
        def _(sp):
            sp.dma_start(g_up[:], core.io["rw_g_up"]).then_inc(consts.sem, 16)

        @block.scalar
        def _(act):
            act.activation(a.gT[:], a.gT[:], ACT.Sigmoid).then_inc(gate.sem, 1)
            act.wait_ge(var.sem, var.at(1))
            act.activation(st[:, 1, :], st[:, 1, :], ACT.Sqrt).then_inc(root.sem, 1)
            act.wait_ge(turned.sem, turned.at(1))
            act.activation(outT[:, 0:2, :], core.ps[:, 1, :].rearrange("p (k n) -> p k n", k=2), ACT.Copy)

        @block.tensor
        def _(pe):
            pe.wait_ge(gate.sem, gate.at(1))
            pe.wait_ge(consts.sem, consts.at(16))
            for x in range(TT):
                last = pe.matmul(core.ps[:, 0, x * RW_W:(x + 1) * RW_W], a.gT[:, x * P:(x + 1) * P], g_up[:],
                                 start=True, stop=True)
            last.then_inc(gates.sem, 1)
            pe.wait_ge(done.sem, done.at(1))
            for k in range(2):
                for x in range(TT):
                    last = pe.transpose(core.ps[:, 1, k * T + x * P:k * T + (x + 1) * P],
                                        rw.y[:, x, k * P:(k + 1) * P], core.ident[:])
            last.then_inc(turned.sem, 1)

        @block.vector
        def _(dve):
            do = lambda ins: core.dve_steps.done(dve, ins)
            y = by_head(rw.y[:])
            do(dve.tensor_reduce(st[:, 0, :], y, AX.X, ALU.add))
            do(dve.tensor_scalar(st[:, 0, :], st[:, 0, :], 1.0 / DH, None, ALU.mult))
            do(dve.tensor_tensor(y, y, wide(st[:, 0, :], DH), ALU.subtract))
            do(dve.tensor_tensor(sq[:], rw.y[:], rw.y[:], ALU.mult))
            do(dve.tensor_reduce(st[:, 1, :], by_head(sq[:]), AX.X, ALU.add))
            dve.tensor_scalar(st[:, 1, :], st[:, 1, :], 1.0 / DH, GN_EPS, ALU.mult, ALU.add).then_inc(var.sem, 1)
            do(dve.tensor_tensor(bonus[:], a.r[:], a.k[:, TT:2 * TT, :], ALU.mult))
            do(dve.tensor_tensor(bonus[:], bonus[:], rows(2), ALU.mult))
            do(dve.tensor_reduce(st[:, 2, :], by_head(bonus[:]), AX.X, ALU.add))
            do(dve.tensor_tensor(by_head(bonus[:]), by_head(a.v[:, TT:2 * TT, :]), wide(st[:, 2, :], DH), ALU.mult))
            dve.wait_ge(root.sem, root.at(1))
            do(dve.reciprocal(st[:, 1, :], st[:, 1, :]))
            do(dve.tensor_tensor(y, y, wide(st[:, 1, :], DH), ALU.mult))
            do(dve.tensor_tensor(rw.y[:], rw.y[:], rows(3), ALU.mult))
            do(dve.tensor_tensor(rw.y[:], rw.y[:], bonus[:], ALU.add))
            dve.wait_ge(gates.sem, gates.at(1))
            dve.tensor_tensor(rw.y[:], rw.y[:], core.ps[:, 0, :].rearrange("p (t n) -> p t n", t=TT),
                              ALU.mult).then_inc(done.sem, 1)
    consts.passed(16)
    for x in (gate, gates, var, root, done, turned):
        x.passed(1)


MOD1_ITEMS = 6 * D // WN
NA_HEADS = 8
NA_W = NA_HEADS * DH
GRID = 64
NA_KC = 16
PROJ1 = 14
MOD1_FIRST = 2 * D // WN
CTX_COL = 2 * D


class Mod1:

    def __init__(self, core, ctx):
        self.gain = core.sb(ctx, "gain1", [P, 2, KD])
        self.shift = core.sb(ctx, "shift1", [P, 2, KD])
        self.cols = core.sb(ctx, "cols1", [P, 4, KD])


def mod1_columns_stage(core, m):
    nc = core.nc
    consts, summed = core.semaphore_of("mod1_consts"), core.semaphore_of("mod1_summed")
    with ExitStack() as ctx:
        g = core.sb(ctx, "norm1_g", [P, KD])
        bias = core.sb(ctx, "mod_bias", [P, 2 * KD])
        sums = core.sb(ctx, "mod_sums", [P, 2, 2 * KD])
        block = ctx.enter_context(nc.Block())

        @block.sync
        def _(sp):
            sp.dma_start(g[:], core.io["norm1_g"]).then_inc(consts.sem, 16)
            sp.dma_start(bias[:], core.io["mod_bias1"][:, 0:2 * KD]).then_inc(consts.sem, 16)

        @block.tensor
        def _(pe):
            mod_columns(core, pe, core.acc, 4 * KD, 0).then_inc(summed.sem, 1)

        @block.vector
        def _(dve):
            dve.wait_ge(consts.sem, consts.at(32))
            dve.wait_ge(summed.sem, summed.at(1))
            core.dve_steps.done(dve, dve.tensor_tensor(
                sums[:], core.ps[:, 0, 0:4 * KD].rearrange("p (w n) -> p w n", w=2), spread(bias[:], 2), ALU.add))
            cols = sums[:].rearrange("p w (j k) -> p w j k", j=2)
            dve.tensor_copy(m.shift[:], cols[:, :, 0])
            dve.scalar_tensor_tensor(out=m.gain[:], in0=cols[:, :, 1], scalar=1.0, in1=spread(g[:], 2),
                                     op0=ALU.add, op1=ALU.mult)
    consts.passed(32)
    summed.passed(1)


def mod1_rest_stage(core, m, rest_acc, layer_acc):
    nc = core.nc
    consts, summed = core.semaphore_of("mod1_consts"), core.semaphore_of("mod1_summed")
    with ExitStack() as ctx:
        g = core.sb(ctx, "norm2_g", [P, KD])
        bias = core.sb(ctx, "mod_bias", [P, 13 * KD])
        sums = core.sb(ctx, "mod_sums", [P, 13 * KD])
        block = ctx.enter_context(nc.Block())

        @block.sync
        def _(sp):
            sp.dma_start(g[:], core.io["norm2_g"]).then_inc(consts.sem, 16)
            sp.dma_start(bias[:, 0:9 * KD], core.io["mod_bias2"][:, 0, 0, :]).then_inc(consts.sem, 16)
            sp.dma_start(bias[:, 9 * KD:], core.io["mod_bias1"][:, 2 * KD:]).then_inc(consts.sem, 16)

        @block.tensor
        def _(pe):
            mod_columns(core, pe, layer_acc, 9 * KD, 0).then_inc(summed.sem, 1)
            mod_columns(core, pe, rest_acc, 4 * KD, 1).then_inc(summed.sem, 1)

        @block.vector
        def _(dve):
            dve.wait_ge(consts.sem, consts.at(48))
            for i, (c, n) in enumerate(((0, 9 * KD), (9 * KD, 4 * KD))):
                dve.wait_ge(summed.sem, summed.at(i + 1))
                core.dve_steps.done(dve, dve.tensor_tensor(sums[:, c:c + n], core.ps[:, i, 0:n], bias[:, c:c + n],
                                                           ALU.add))
            shape_columns(core, dve, 0, sums[:, 0:9 * KD])
            cols = sums[:, 9 * KD:].rearrange("p (v k) -> p v k", v=4)
            core.dve_steps.done(dve, dve.tensor_copy(m.cols[:], cols))
            dve.scalar_tensor_tensor(out=m.cols[:, 2, :], in0=cols[:, 2, :], scalar=1.0, in1=g[:],
                                     op0=ALU.add, op1=ALU.mult)
    consts.passed(48)
    summed.passed(2)


def rows1_stage(core, m):
    wide_out = core.semaphore_of("mod_wide")
    with core.nc.Block() as block:
        @block.sync
        def _(sp):
            core.issue_w(sp, 0)

        @block.tensor
        def _(pe):
            for i in range(8):
                for j in range(4):
                    col = m.cols[:, i // 2, 4 * (i % 2) + j:4 * (i % 2) + j + 1]
                    last = pe.matmul(core.ps[:, i, j * P:(j + 1) * P],
                                     bass.AP(col.tensor, col.offset, [list(col.ap[0]), [0, P]]),
                                     core.ident[:], start=True, stop=True)
                last.then_inc(wide_out.sem, 1)

        def copies(eng, is_act):
            for i in range(0 if is_act else 1, 8, 2):
                eng.wait_ge(wide_out.sem, wide_out.at(i + 1))
                put(eng, is_act, m.rows[:, i // 2, (i % 2) * BANK:(i % 2 + 1) * BANK], core.ps[:, i, :])

        @block.scalar
        def _(act):
            copies(act, True)

        @block.vector
        def _(dve):
            copies(dve, False)
    wide_out.passed(8)


class Projected:

    def __init__(self, core, ctx):
        self.r = core.sb(ctx, "r", [P, TT, RW_W])
        self.k = core.sb(ctx, "k", [P, 2 * TT, RW_W])
        self.v = core.sb(ctx, "v", [P, 2 * TT, RW_W])
        self.waT = core.sb(ctx, "waT", [P, 2, 2 * T])
        self.gT = core.sb(ctx, "gT", [P, T])

    def allocate_short(self, core, short):
        self.qT = core.sb(short, "na_qT", [P, NA_W // P, T])
        self.kT = core.sb(short, "na_kT", [P, NA_W // P, 2 * T])
        self.nv = core.sb(short, "na_v", [P, 2 * TT, NA_W])
        self.sc = core.sb(short, "sc", [P, 3, 2, T])


def first_projections(core, a, hT, hcT, side):
    def unit_g(item):
        return (item, [(P, lambda w, h, k: w[:, k, 0:P], lambda w, h, k: h[:, k, :])], [hT],
                lambda eng, is_act, bank: put(eng, is_act, a.gT[:], bank[:, 0:T]))

    units = [along(core, [hT], 0, a.r[:])]
    for i, dst in ((1, a.k), (2, a.v)):
        units += [along(core, [hcT], i, dst[:, 0:TT, :]), along(core, [hT], i, dst[:, TT:2 * TT, :])]
    units += [across(core, [hcT], 3, a.waT[:, :, 0:T]), across(core, [hT], 3, a.waT[:, :, T:2 * T])]
    units += [unit_g(4)]
    units += [across(core, [hT], 5 + i, a.qT[:, 2 * i:2 * i + 2, :], DH ** -0.5) for i in range(2)]
    for i in range(2):
        units += [across(core, [hT], 7 + i, a.kT[:, 2 * i:2 * i + 2, 0:T]),
                  across(core, [hcT], 7 + i, a.kT[:, 2 * i:2 * i + 2, T:2 * T])]
    for i in range(2):
        units += [along(core, [hT], 9 + i, a.nv[:, 0:TT, i * WN:(i + 1) * WN]),
                  along(core, [hcT], 9 + i, a.nv[:, TT:2 * TT, i * WN:(i + 1) * WN])]
    units += [across(core, [hT], 11 + i, a.sc[:, i, :, :]) for i in range(3)]
    projections(core, PROJ1, units, side, split=False)


class Neighbours(Softmax):

    def __init__(self, core, ctx, a, outT):
        self.core, self.a, self.outT = core, a, outT
        self.bias = core.sb(ctx, "na_bias", [P, NA_HEADS, TT, T])

    def at(self, u):
        h, t = u // TT, u % TT
        return h, t, slice((h % 2) * DH, (h % 2) * DH + DH)

    def scores(self, u):
        h, t, part = self.at(u)
        return [(0, 2 * T, self.a.qT[part, h // 2, t * P:(t + 1) * P], self.a.kT[part, h // 2, :])]

    def groups(self, u):
        return [(0, 2 * T)]

    def tiles(self, u):
        return [(j * P, P) for j in range(2 * TT)]

    def logits(self, dve, u, S, L, mx):
        core = self.core
        h, t, _ = self.at(u)
        dve.tensor_tensor_reduce(L[:, 0:T], S[:, 0:T], self.bias[:, h, t, :], 1.0, -3e38, ALU.add, ALU.max,
                                 mx[:, 0:1])
        core.dve_steps.done(dve, dve.tensor_scalar(L[:, T:2 * T], S[:, T:2 * T], 1.0, -3e38, ALU.mult, ALU.max,
                                                   accum_out=mx[:, 1:2]))
        core.dve_steps.done(dve, dve.tensor_tensor(mx[:, 0:1], mx[:, 0:1], mx[:, 1:2], ALU.max))
        return self.finish_maxima(dve, mx, 1)

    def weigh(self, dve, u, L, sums):
        self.core.dve_steps.done(dve, dve.reciprocal(sums[:, 0:1], sums[:, 0:1]))
        return dve.tensor_scalar(L[:, 0:2 * T], L[:, 0:2 * T], sums[:, 0:1], None, ALU.mult)

    def values(self, pe, u, pT, O):
        h, t, part = self.at(u)
        for j in range(2 * TT):
            last = pe.matmul(O[part, 0:P], self.a.nv[:, j, h * DH:(h + 1) * DH], pT[:, j * P:(j + 1) * P],
                             start=(j == 0), stop=(j == 2 * TT - 1))
        return last

    def out(self, act, u, O):
        h, t, part = self.at(u)
        return act.activation(self.outT[part, 2 + h // 2, t * P:(t + 1) * P], O[part, 0:P], ACT.Copy)


def neighbour_stage(core, a, outT):
    nc = core.nc
    loaded, ready = core.semaphore_of("na_loaded"), core.semaphore_of("na_ready")
    with ExitStack() as ctx:
        n = Neighbours(core, ctx, a, outT)
        with ExitStack() as inner:
            w = core.sb(inner, "sc_w", [P, 3, 2])
            u = core.sb(inner, "sc_u", [P, 2, T + 2])
            o = core.sb(inner, "sc_o", [P, 2, T])
            block = inner.enter_context(nc.Block())

            @block.sync
            def _(sp):
                sp.dma_start(n.bias[:], core.io["na_bias"]).then_inc(loaded.sem, 16)
                sp.dma_start(w[:], core.io["sc_w"]).then_inc(ready.sem, 16)
                core.issue_w(sp, 0)

            @block.gpsimd
            def _(pool):
                pool.wait_ge(loaded.sem, loaded.at(16))
                for half in range(P // GRID):
                    part = slice(half * GRID, (half + 1) * GRID)
                    view = n.bias[part].rearrange("p h t (r c) -> p (h t) r c", c=GRID)
                    low, high = view[:, :, :, 0:GRID - NA_KC], view[:, :, :, NA_KC:GRID]
                    groups = NA_HEADS * TT
                    core.pool_steps.done(pool, pool.affine_select(
                        out=low, in_=low, compare_op=ALU.is_ge, fill=NEG, base=NA_KC // 2,
                        pattern=[[0, groups], [0, T // GRID], [1, GRID - NA_KC]], channel_multiplier=-1))
                    core.pool_steps.done(pool, pool.affine_select(
                        out=high, in_=high, compare_op=ALU.is_gt, fill=NEG, base=NA_KC // 2 - NA_KC,
                        pattern=[[0, groups], [0, T // GRID], [-1, GRID - NA_KC]], channel_multiplier=1))

            @block.vector
            def _(dve):
                dve.wait_ge(ready.sem, ready.at(16))
                dve.memset(u[:], 0.0)
                core.dve_steps.done(dve, dve.memset(o[:], 0.0))
                core.dve_steps.done(dve, dve.tensor_tensor(u[:, :, 1:T + 1], a.sc[:, 1], a.sc[:, 2], ALU.mult))
                for tap in range(3):
                    for m in range(2):
                        last = dve.scalar_tensor_tensor(out=o[:, m, :], in0=u[:, m, tap:tap + T],
                                                        scalar=w[:, tap, m:m + 1], in1=o[:, m, :],
                                                        op0=ALU.mult, op1=ALU.add)
                    core.dve_steps.done(dve, last)
                dve.tensor_tensor(outT[:, 6:8, :], o[:], a.sc[:, 0], ALU.mult)
        attention(core, ctx, n, NA_HEADS * TT, split=False)
    loaded.passed(16)
    ready.passed(16)


def recurrent_mixer(core, a, outT):
    nc = core.nc
    consts = core.semaphore_of("rw_consts")
    with ExitStack() as ctx:
        rw = Recurrence(core, ctx)
        with nc.Block() as block:
            @block.sync
            def _(sp):
                io = core.io
                sp.dma_start(rw.masks[:], io["rw_masks"]).then_inc(consts.sem, 16)
                sp.dma_start(rw.chunk_sum[:], io["chunk_sum"]).then_inc(consts.sem, 16)
                sp.dma_start(rw.up[:], io["rw_up"]).then_inc(consts.sem, 16)
                sp.dma_start(rw.w0a0[:].rearrange("p d n -> p (d n)"),
                             io["w0a0"].partition_broadcast(P)).then_inc(consts.sem, 16)
                sp.dma_start(rw.rows[:].rearrange("p d n -> p (d n)"),
                             io["rw_rows"].partition_broadcast(P)).then_inc(consts.sem, 16)
                sp.wait_ge(consts.sem, consts.at(80))

            @block.scalar
            def _(act):
                act.activation(a.waT[:, 0, :], a.waT[:, 0, :], ACT.Tanh)

            @block.vector
            def _(dve):
                dve.memset(rw.state[:, 0, :, :], 0.0)
        consts.passed(80)
        for t in range(2 * TT):
            rw_tile_stage(core, rw, a, t)
        rw_chain_stage(core, rw)
        rw_output_stage(core, rw, a, outT)


def mixed_stage(core, m):
    nc = core.nc
    squares, mean = core.semaphore_of("mix_squares"), core.semaphore_of("mix_mean")
    root, rows, turned = core.semaphore_of("mix_root"), core.semaphore_of("mix_rows"), core.semaphore_of("mix_turned")
    with ExitStack() as ctx:
        t_sb = core.sb(ctx, "gated", [P, TT, D])
        ss = core.sb(ctx, "ss1", [P, TT])
        block = ctx.enter_context(nc.Block())
        x = core.x

        @block.vector
        def _(dve):
            do = lambda ins: core.dve_steps.done(dve, ins)
            for i in range(2 * TT):
                t, part = i // 2, slice((i % 2) * BANK, (i % 2 + 1) * BANK)
                do(dve.tensor_tensor(t_sb[:, t, part], core.y[:, i, :], m.rows[:, 0, part], ALU.mult))
            do(dve.tensor_tensor(x[:], x[:], t_sb[:], ALU.add))
            for t in range(TT):
                do(dve.tensor_tensor_reduce(t_sb[:, t, :], x[:, t, :], x[:, t, :], 1.0, 0.0, ALU.mult, ALU.add,
                                            ss[:, t:t + 1]))
            dve.tensor_scalar(ss[:], ss[:], 1.0 / D, EPS, ALU.mult, ALU.add).then_inc(mean.sem, 1)
            dve.wait_ge(root.sem, root.at(1))
            do(dve.reciprocal(ss[:], ss[:]))
            for t in range(TT):
                do(dve.scalar_tensor_tensor(out=core.h2[:, t, :], in0=x[:, t, :], scalar=ss[:, t:t + 1],
                                            in1=m.rows[:, 2, :], op0=ALU.mult, op1=ALU.mult))
                dve.tensor_tensor(core.h2[:, t, :], core.h2[:, t, :], m.rows[:, 1, :],
                                  ALU.add).then_inc(rows.sem, 1)

        @block.scalar
        def _(act):
            act.wait_ge(mean.sem, mean.at(1))
            act.activation(ss[:], ss[:], ACT.Sqrt).then_inc(root.sem, 1)
            for k in range(0, KD, 2):
                act.wait_ge(turned.sem, turned.at(k // 2 + 1))
                act.activation(core.hT[:, k:k + 2, :], core.ps[:, k // 2, :].rearrange("p (k n) -> p k n", k=2),
                               ACT.Copy)

        @block.tensor
        def _(pe):
            pe.wait_ge(rows.sem, rows.at(TT))
            for k in range(KD):
                for t in range(TT):
                    last = pe.transpose(core.ps[:, k // 2, (k % 2) * T + t * P:(k % 2) * T + (t + 1) * P],
                                        core.h2[:, t, k * P:(k + 1) * P], core.ident[:])
                if k % 2:
                    last.then_inc(turned.sem, 1)
    mean.passed(1)
    root.passed(1)
    rows.passed(TT)
    turned.passed(KD // 2)


PEER_H, PEER_KEYS, PEER_TOP = 8, 128, 16
PEER_PAIRS = PEER_H * PEER_TOP
PEER_N = PEER_KEYS * PEER_KEYS
PER_BATCH = 2
G_SLOTS = 8
G_BATCHES = G_SLOTS // PER_BATCH


def peer_topk_stage(core, ctx, idx, gates):
    nc = core.nc
    consts, scored = core.semaphore_of("peer_keys_in"), core.semaphore_of("peer_scored")
    copied = core.semaphore_of("peer_copied")
    shifted, raised = core.semaphore_of("peer_shifted"), core.semaphore_of("peer_raised")
    steps = core.dve_steps
    with ExitStack() as inner:
        qT = core.sb(inner, "peer_qT", [P, 2 * PEER_H, T])
        keys = core.sb(inner, "peer_keys", [P, 2 * PEER_H, PEER_KEYS])
        units = [across(core, [core.hT], i, qT[:, 2 * i:2 * i + 2, :]) for i in range(PEER_H)]
        projections(core, PEER_H, units, split=False)
        sc = core.sb(inner, "peer_s", [P, 2 * PEER_H, PEER_KEYS])
        top = core.sb(inner, "peer_top", [P, 2 * PEER_H, PEER_TOP])
        top_i = core.sb(inner, "peer_top_i", [P, 2 * PEER_H, PEER_TOP], U32)
        top_f = core.sb(inner, "peer_top_f", [P, 2 * PEER_H, PEER_TOP])
        cand = core.sb(inner, "peer_cand", [P, PEER_H, PEER_TOP * PEER_TOP])
        best = core.sb(inner, "peer_best", [P, PEER_H, PEER_TOP])
        pos = core.sb(inner, "peer_pos", [P, PEER_H, PEER_TOP], U32)
        pos2 = core.sb(inner, "peer_pos2", [P, 2, PEER_PAIRS], U32)
        pos_f = core.sb(inner, "peer_pos_f", [P, 2, PEER_PAIRS])
        hit = core.sb(inner, "peer_hit", [P, PEER_H, PEER_TOP * PEER_TOP])
        count = core.sb(inner, "peer_count", [P, PEER_TOP])
        part_i = core.sb(inner, "peer_part", [P, 2, PEER_PAIRS])
        sums = core.sb(inner, "peer_sums", [P, PEER_H])
        block = inner.enter_context(nc.Block())

        @block.sync
        def _(sp):
            sp.dma_start(keys[:], core.io["peer_keys"]).then_inc(consts.sem, 16)
            sp.dma_start(count[:], core.io["count16"]).then_inc(consts.sem, 16)
            core.issue_w(sp, 0)

        @block.tensor
        def _(pe):
            pe.wait_ge(consts.sem, consts.at(32))
            for t in range(TT):
                for b in range(4):
                    if t:
                        pe.wait_ge(copied.sem, copied.at(b + 1))
                    for i in range(4):
                        last = pe.matmul(core.ps[:, b, i * P:(i + 1) * P], qT[:, 4 * b + i, t * P:(t + 1) * P],
                                         keys[:, 4 * b + i, :], start=True, stop=True)
                    last.then_inc(scored.sem, 1)

        @block.scalar
        def _(act):
            for t in range(TT):
                act.wait_ge(shifted.sem, shifted.at(t + 1))
                act.activation(gates[:, t, :], gates[:, t, :], ACT.Exp).then_inc(raised.sem, 1)

        @block.vector
        def _(dve):
            def do(ins):
                steps.done(dve, ins)

            def top16(values, out, out_i, n):
                for half in range(2):
                    cols = slice(8 * half, 8 * half + 8)
                    for r in range(n):
                        last = dve.max(out[:, r, cols], values[:, r, :])
                    do(last)
                    for r in range(n):
                        last = dve.max_index(out_i[:, r, cols], out[:, r, cols], values[:, r, :])
                    do(last)
                    if half == 0:
                        for r in range(n):
                            last = dve.match_replace(values[:, r, :], out[:, r, cols], values[:, r, :], -3e38)
                        do(last)

            for t in range(TT):
                for b in range(4):
                    dve.wait_ge(scored.sem, scored.at(4 * t + b + 1))
                    last = dve.tensor_copy(sc[:, 4 * b:4 * b + 4, :],
                                           core.ps[:, b, :].rearrange("p (i n) -> p i n", i=4))
                    last.then_inc(copied.sem, 1)
                dve.wait_ge(copied.sem, copied.at(4 * t + 4))
                top16(sc, top, top_i, 2 * PEER_H)
                do(dve.tensor_copy(top_f[:], top_i[:]))
                for h in range(PEER_H):
                    last = dve.tensor_tensor(cand[:, h, :].rearrange("p (a b) -> p a b", a=PEER_TOP),
                                             wide(top[:, 2 * h, :], PEER_TOP),
                                             spread(top[:, 2 * h + 1, :], PEER_TOP), ALU.add)
                do(last)
                top16(cand, best, pos, PEER_H)
                flat = pos[:].rearrange("p h k -> p (h k)")
                dve.tensor_scalar(pos2[:, 0, :], flat, 4, None, ALU.logical_shift_right)
                do(dve.tensor_scalar(pos2[:, 1, :], flat, PEER_TOP - 1, None, ALU.bitwise_and))
                do(dve.tensor_copy(pos_f[:], pos2[:]))
                for half in range(2):
                    for h in range(PEER_H):
                        place = wide(pos_f[:, half, h * PEER_TOP:(h + 1) * PEER_TOP], PEER_TOP)
                        view = hit[:, h, :].rearrange("p (k a) -> p k a", a=PEER_TOP)
                        last = dve.tensor_tensor(view, place, spread(count[:], PEER_TOP), ALU.is_equal)
                    do(last)
                    for h in range(PEER_H):
                        view = hit[:, h, :].rearrange("p (k a) -> p k a", a=PEER_TOP)
                        last = dve.tensor_tensor(view, view, spread(top_f[:, 2 * h + half, :], PEER_TOP), ALU.mult)
                    do(last)
                    do(dve.tensor_reduce(part_i[:, half, :],
                                         hit[:].rearrange("p h (k a) -> p (h k) a", a=PEER_TOP), AX.X, ALU.add))
                do(dve.scalar_tensor_tensor(out=part_i[:, 0, :], in0=part_i[:, 0, :], scalar=float(PEER_KEYS),
                                            in1=part_i[:, 1, :], op0=ALU.mult, op1=ALU.add))
                dve.tensor_copy(idx[:, t, :], part_i[:, 0, :])
                g = gates[:, t, :].rearrange("p (h k) -> p h k", h=PEER_H)
                dve.tensor_tensor(g, best[:], wide(best[:, :, 0], PEER_TOP), ALU.subtract).then_inc(shifted.sem, 1)
                dve.wait_ge(raised.sem, raised.at(t + 1))
                do(dve.tensor_reduce(sums[:], g, AX.X, ALU.add))
                do(dve.reciprocal(sums[:], sums[:]))
                do(dve.tensor_tensor(g, g, wide(sums[:], PEER_TOP), ALU.mult))
    consts.passed(32)
    scored.passed(8)
    copied.passed(8)
    shifted.passed(TT)
    raised.passed(TT)


def peer_experts_stage(core, m, idx, gates):
    nc = core.nc
    landed = [core.semaphore_of(f"rows_landed{s}") for s in range(G_SLOTS)]
    asked = core.semaphore_of("rows_asked")
    freed, dots, acts = core.semaphore_of("rows_freed"), core.semaphore_of("dots_ready"), core.semaphore_of("acts_ready")
    batches = PEER_PAIRS // PER_BATCH
    turns = (batches - 1) // G_BATCHES
    steps = core.dve_steps
    with ExitStack() as ctx:
        rows = core.sb(ctx, "expert_rows", [P, G_SLOTS, 2 * D])
        col = core.sb(ctx, "expert_col", [P, G_SLOTS], U32)
        dot = core.sb(ctx, "expert_dot", [P, G_BATCHES, PER_BATCH])
        coef = core.sb(ctx, "expert_coef", [P, G_BATCHES, PER_BATCH])
        junk = core.sb(ctx, "expert_junk", [P, 2, D])
        acc = core.sb(ctx, "expert_sum", [P, TT, D])
        block = ctx.enter_context(nc.Block())

        @block.gpsimd
        def _(pool):
            def gather(t, slot, n, wait):
                if wait is not None:
                    pool.wait_ge(freed.sem, wait)
                core.pool_steps.done(pool, pool.tensor_copy(col[:, slot:slot + 1], idx[:, t, n]))
                pool.sem_inc(asked.sem, 1)
                pool.indirect_dma_start(rows[:, slot, :], None, core.io["experts"],
                                        bass.IndirectOffsetOnAxis(ap=col[:, slot:slot + 1], axis=0)).then_inc(
                                            landed[slot].sem, 16)

            for t in range(TT):
                if t == 0:
                    for slot in range(G_SLOTS):
                        gather(0, slot, slice(slot, slot + 1), None)
                first = 1 if t == 0 else 0
                with core.pool_steps.loop(pool, PEER_PAIRS // G_SLOTS - first, G_SLOTS) as i:
                    for slot in range(G_SLOTS):
                        gather(t, slot, bass.ds(i * G_SLOTS + (first * G_SLOTS + slot), 1),
                               i * G_SLOTS + freed.at(t * PEER_PAIRS + (first - 1) * G_SLOTS + slot + 1))

        @block.scalar
        def _(act):
            with act.Fori(0, TT * batches // G_BATCHES, 1) as i:
                for b in range(G_BATCHES):
                    act.wait_ge(dots.sem, i * G_BATCHES + dots.at(b + 1))
                    act.activation(coef[:, b, :], dot[:, b, :], ACT.Gelu_apprx_tanh).then_inc(acts.sem, 1)

        @block.vector
        def _(dve):
            dve.memset(acc[:], 0.0)

            def products(t, b, i=0):
                for e in range(PER_BATCH):
                    slot = (b * PER_BATCH + e) % G_SLOTS
                    turn = t * PEER_PAIRS // G_SLOTS + (b * PER_BATCH + e) // G_SLOTS + 1
                    dve.wait_ge(landed[slot].sem, (i + turn) * 16 + landed[slot].base)
                    ins = dve.tensor_tensor_reduce(junk[:, e, :], rows[:, slot, 0:D], core.h2[:, t, :], 1.0, 0.0,
                                                   ALU.mult, ALU.add, dot[:, b % G_BATCHES, e:e + 1])
                    if e < PER_BATCH - 1:
                        continue
                    ins.then_inc(dots.sem, 1)
                dve.wait_ge(dots.sem, i * G_BATCHES + dots.at(t * batches + b + 1))

            def sums(t, b, i=0):
                dve.wait_ge(acts.sem, i * G_BATCHES + acts.at(t * batches + b + 1))
                c = coef[:, b % G_BATCHES, :]
                g = gates[:, t, bass.ds(i * G_SLOTS + b * PER_BATCH, PER_BATCH)]
                steps.done(dve, dve.tensor_tensor(c, c, g, ALU.mult))
                for e in range(PER_BATCH):
                    slot = (b * PER_BATCH + e) % G_SLOTS
                    dve.scalar_tensor_tensor(out=acc[:, t, :], in0=rows[:, slot, D:2 * D], scalar=c[:, e:e + 1],
                                             in1=acc[:, t, :], op0=ALU.mult, op1=ALU.add).then_inc(freed.sem, 1)
                    dve.wait_ge(freed.sem, i * G_SLOTS + freed.at(t * PEER_PAIRS + b * PER_BATCH + e + 1))

            for t in range(TT):
                products(t, 0)
                with steps.loop(dve, turns, G_BATCHES) as i:
                    for b in range(G_BATCHES):
                        products(t, b + 1, i)
                        sums(t, b, i)
                for b in range(turns * G_BATCHES, batches):
                    if b + 1 < batches:
                        products(t, b + 1)
                    sums(t, b)
            for t in range(TT):
                steps.done(dve, dve.tensor_tensor(acc[:, t, :], acc[:, t, :], m.rows[:, 3, :], ALU.mult))
                steps.done(dve, dve.tensor_tensor(core.x[:, t, :], core.x[:, t, :], acc[:, t, :], ALU.add))

        @block.sync
        def _(sp):
            core.issue_w(sp, 0)
    for s in landed:
        s.passed(16 * TT * PEER_PAIRS // G_SLOTS)
    freed.passed(TT * PEER_PAIRS)
    dots.passed(TT * batches)
    acts.passed(TT * batches)


def first_block(core):
    nc = core.nc
    inputs = core.semaphore_of("inputs")
    with ExitStack() as ctx:
        m = Mod1(core, ctx)
        core.hT = core.sb(ctx, "hT", [P, KD, T])
        with ExitStack() as s1:
            a = Projected(core, s1)
            short = s1.enter_context(ExitStack())
            a.allocate_short(core, short)
            cond = core.sb(short, "cond1", [P, 2, KD])
            hcT = core.sb(short, "hcT", [P, KD, T])
            early = short.enter_context(ExitStack())
            xc = core.sb(early, "x_ctx", [P, TT, D])
            core.a_first, core.a_ends = 0, True
            with nc.Block() as block:
                @block.sync
                def _(sp):
                    for dst, name in ((cond, "cond1_in"), (core.cond, "cond2_in"), (core.x, "x_in"),
                                      (xc, "ctx_in"), (core.ident, "ident"), (core.norm_pre, "norm_pre"),
                                      (core.norm_post, "norm_post")):
                        sp.dma_start(dst[:], core.io[name]).then_inc(inputs.sem, 16)

                @block.scalar
                def _(act):
                    act.wait_ge(inputs.sem, 16 * 7)
                    act.activation(cond[:], cond[:], ACT.Silu)
                    act.activation(core.cond[:], core.cond[:], ACT.Silu)

                @block.vector
                def _(dve):
                    core.dve_steps.done(dve, dve.memset(core.ones[:], 1.0))
            inputs.passed(16 * 7)
            core.a_ends = True
            keep, core.cond = core.cond, cond[:, 0, :]
            with ExitStack() as s0:
                core.a_ring = core.sb(s0, "a_ring", [P, A_SLOTS, ITEM])
                core.odd_sums = core.sb(s0, "odd_sums", [P, 2, WN])
                core.acc = core.sb(s0, "mod_acc", [P, 2 * CTX_COL])
                ada_stage(core, MOD1_FIRST, (cond[:, 1, :], CTX_COL, MOD1_FIRST))
                mod1_columns_stage(core, m)
            norm_stage(core, None, 0, (core.x, core.hT, m.gain, m.shift))
            norm_stage(core, None, 1, (xc, hcT, m.gain, m.shift))
            early.close()
            with ExitStack() as s0:
                rest = MOD1_ITEMS - MOD1_FIRST
                core.a_ends, core.a_first = False, core.a_issued
                core.a_ring = core.sb(s0, "a_ring", [P, A_SLOTS, ITEM])
                core.odd_sums = core.sb(s0, "odd_sums", [P, 2, WN])
                core.acc = core.sb(s0, "mod_acc", [P, (rest + MOD_ITEMS) * WN])
                a0 = core.a_taken
                side_items = rest + MOD_ITEMS

                def loads(sp, items):
                    total = core.a_taken + side_items
                    for i in range(items):
                        core.issue_w(sp, 1)
                        n = min(-(-side_items // items), total - core.a_taken)
                        core.issue_a(sp, n, 1)

                def work(dve):
                    for lo, n, who in ((0, rest, core.cond), (rest, MOD_ITEMS, keep)):
                        turns = n // A_SLOTS
                        with core.dve_steps.loop(dve, turns, A_SLOTS * UNIT_STEPS) as i:
                            for j in range(A_SLOTS):
                                c = (lo + j) * WN
                                acc = core.acc[:, bass.ds(i * (A_SLOTS * WN) + c, WN)]
                                core.mod_unit(dve, a0 + lo + j, [(who, acc, core.odd_sums[:, 0, :])], i)
                        for j in range(turns * A_SLOTS, n):
                            c = (lo + j) * WN
                            core.mod_unit(dve, a0 + lo + j, [(who, core.acc[:, c:c + WN], core.odd_sums[:, 0, :])])

                first_projections(core, a, core.hT, hcT, (loads, work))
                core.cond = keep
                mod1_rest_stage(core, m, core.acc[:, 0:rest * WN], core.acc[:, rest * WN:])
            outT = core.hT
            neighbour_stage(core, a, outT)
            short.close()
            recurrent_mixer(core, a, outT)
        m.rows = core.sb(ctx, "rows1", [P, 4, D])
        rows1_stage(core, m)
        with ExitStack() as s0:
            core.start_splits(s0)
            out_projection(core, core.hT, ahead=0)
        core.h2 = core.sb(ctx, "h2", [P, TT, D])
        mixed_stage(core, m)
        idx = core.sb(ctx, "expert_idx", [P, TT, PEER_PAIRS], U32)
        gates = core.sb(ctx, "expert_gates", [P, TT, PEER_PAIRS])
        peer_topk_stage(core, ctx, idx, gates)
        peer_experts_stage(core, m, idx, gates)


def first_layout(a):
    w_in = a["w_in"][0]
    widths = (256, 256, 256, 128, 128, 128, 512, 512, 512, 256, 256, 256)
    r, k, v, zw, za, zg, q, nk, nv, b, c, x = np.split(w_in, np.cumsum(widths)[:-1], 1)
    w = [w_items(y) for y in (r, k, v, np.concatenate([zw, za], 1), padded(zg), q, nk, nv, b, c, x)]
    w += [w_items(a["w_out"][0]), w_items(a["peer_q_w"][0])]
    mods = w_items(a["ada_w"][0])
    tok = np.arange(T)
    row, col = tok // GRID, tok % GRID
    dr = row[None, :] - row[:, None] + 7
    dc = np.clip(col[None, :] - col[:, None] + NA_KC - 1, 0, 2 * NA_KC - 2)
    bias = a["na_rpb"][0][:, dr, dc].reshape(NA_HEADS, TT, P, T).transpose(2, 0, 1, 3)
    s, t = np.arange(P)[:, None], np.arange(P)[None, :]
    same = s // CHUNK == t // CHUNK
    masks = np.zeros((P, 2, 4 + LEVELS, P), np.float32)
    for d in range(2):
        before = (s > t) if d else (s < t)
        masks[:, d, 0] = before & same
        masks[:, d, 1] = (before | (s == t)) & same
        masks[:, d, 2] = masks[:, d, 1] * np.float32(LOG_DECAY)
        masks[:, d, 3] = masks[:, d, 0] * np.float32(LOG_DECAY)
        for level in range(LEVELS):
            half = 1 << level
            masks[:, d, 4 + level] = before & (s // (2 * half) == t // (2 * half)) & (s // half != t // half)
    chunk_sum = np.zeros((P, 2), np.float32)
    for c2 in range(2):
        chunk_sum[c2 * CHUNK:(c2 + 1) * CHUNK, c2] = LOG_DECAY
    tiles = lambda y: np.ascontiguousarray(y.reshape(TT, P, D).transpose(1, 0, 2))
    small = {
        "x_in": tiles(a["x"][0]), "ctx_in": tiles(a["ctx"][0]),
        "cond1_in": np.ascontiguousarray(np.stack([columns_of(a["c"][0]), columns_of(a["c_ctx"])], 1)),
        "mod_bias1": np.ascontiguousarray(a["ada_b"][0].reshape(-1, P).T),
        "norm1_g": columns_of(a["norm1_g"][0]), "norm2_g": columns_of(a["norm2_g"][0]),
        "na_bias": np.ascontiguousarray(bias),
        "sc_w": np.ascontiguousarray(a["sc_conv_w"][0].reshape(3, 2, P).transpose(2, 0, 1)),
        "rw_masks": masks, "chunk_sum": chunk_sum,
        "rw_up": np.ascontiguousarray(np.stack([a["rw_w_up"][0].reshape(P, RW_W), a["rw_a_up"][0].reshape(P, RW_W)], 1)),
        "w0a0": np.ascontiguousarray(np.concatenate([a["rw_w0"][0], a["rw_a0"][0]], 1).reshape(1, 4 * RW_W)),
        "rw_rows": np.ascontiguousarray(np.concatenate(
            [a["rw_k_k"][0], a["rw_k_a"][0], a["rw_r_k"][0].reshape(-1), a["rw_lnx_g"][0]]).reshape(1, 4 * RW_W)),
        "rw_g_up": np.ascontiguousarray(a["rw_g_up"][0]),
        "peer_keys": np.ascontiguousarray(a["peer_sub_keys"][0].reshape(2 * PEER_H, PEER_KEYS, P).transpose(2, 0, 1)),
        "count16": np.ascontiguousarray(np.broadcast_to(np.arange(PEER_TOP, dtype=np.float32), (P, PEER_TOP))),
        "experts": np.ascontiguousarray(np.concatenate([a["peer_u"][0], a["peer_v"][0]], 1)),
        "final_g": np.ascontiguousarray(a["final_g"].reshape(1, D)),
    }
    return w, mods, small


def final_norm_stage(core):
    nc = core.nc
    loaded, mean, root = core.semaphore_of("final_g_in"), core.semaphore_of("final_mean"), core.semaphore_of("final_root")
    with ExitStack() as ctx:
        g = core.sb(ctx, "final_g", [P, D])
        junk = core.sb(ctx, "final_junk", [P, TT, D])
        ss = core.sb(ctx, "final_ss", [P, TT])
        block = ctx.enter_context(nc.Block())

        @block.sync
        def _(sp):
            sp.dma_start(g[:], core.io["final_g"].partition_broadcast(P)).then_inc(loaded.sem, 16)
            core.issue_w(sp, 0)

        @block.scalar
        def _(act):
            act.wait_ge(mean.sem, mean.at(1))
            act.activation(ss[:], ss[:], ACT.Sqrt).then_inc(root.sem, 1)

        @block.vector
        def _(dve):
            for t in range(TT):
                core.dve_steps.done(dve, dve.tensor_tensor_reduce(
                    junk[:, t, :], core.x[:, t, :], core.x[:, t, :], 1.0, 0.0, ALU.mult, ALU.add, ss[:, t:t + 1]))
            dve.tensor_scalar(ss[:], ss[:], 1.0 / D, EPS, ALU.mult, ALU.add).then_inc(mean.sem, 1)
            dve.wait_ge(root.sem, root.at(1))
            core.dve_steps.done(dve, dve.reciprocal(ss[:], ss[:]))
            dve.wait_ge(loaded.sem, loaded.at(16))
            for t in range(TT):
                dve.scalar_tensor_tensor(out=core.x[:, t, :], in0=core.x[:, t, :], scalar=ss[:, t:t + 1],
                                         in1=g[:], op0=ALU.mult, op1=ALU.mult)
    loaded.passed(16)
    mean.passed(1)
    root.passed(1)


def store_stage(core, out):
    stored = core.semaphore_of("stored")
    with core.nc.Block() as block:
        @block.sync
        def _(sp):
            sp.dma_start(out.rearrange("a (t p) d -> p (a t) d", p=P), core.x[:]).then_inc(stored.sem, 16)
            sp.wait_ge(stored.sem, 16)


def build_program(nc, io, out):
    with ExitStack() as ctx:
        core = Core(nc, ctx)
        core.io = io
        core.w_stream, core.a_stream = io["w_stream"], io["a_stream"]
        core.ps = ctx.enter_context(nc.psum_tensor("ps", [P, BANKS, BANK], F32))
        core.y = core.ps[:, 4:8, :]
        core.ring = core.sb(ctx, "w_ring", [P, W_SLOTS, ITEM])
        core.x = core.sb(ctx, "x", [P, TT, D])
        core.cond = core.sb(ctx, "cond2", [P, KD])
        core.ident = core.sb(ctx, "identity", [P, P])
        core.ones = core.sb(ctx, "ones", [P, 1])
        core.shift = core.sb(ctx, "shift", [P, 3, KD])
        core.gain = core.sb(ctx, "gain", [P, 3, KD])
        core.gate_cols = core.sb(ctx, "gate_cols", [P, 3, KD])
        core.norm_pre = core.sb(ctx, "norm_pre", [P, DEPTH, 3, KD])
        core.norm_post = core.sb(ctx, "norm_post", [P, DEPTH, 3, KD])
        first_block(core)
        final_norm_stage(core)
        core.gates = core.sb(ctx, "gates", [P, 3, D])
        core.a_limit = core.a_stream.shape[0]
        mod_stage(core, 0)
        second_block(core)
        store_stage(core, out)


def kernel(**inputs):
    import concourse.bacc as bacc
    from concourse.bass_utils import run_bass_kernel_spmd

    a = {name: np.asarray(v) for name, v in inputs.items()}
    w1, mods1, small1 = first_layout(a)
    w2, mods2, small2 = second_layout(a)
    arrays = {**small1, **small2, **attention_tables(),
              "w_stream": np.concatenate(w1 + w2), "a_stream": np.concatenate([mods1, mods2])}
    nc = bacc.Bacc("TRN2", target_bir_lowering=False, num_devices=1)
    io = {name: nc.dram_tensor(f"in_{name}", v.shape, mybir.dt.from_np(v.dtype), kind="ExternalInput").ap()
          for name, v in arrays.items()}
    out = nc.dram_tensor("out_x", (1, T, D), F32, kind="ExternalOutput").ap()
    build_program(nc, io, out)
    r = run_bass_kernel_spmd(nc, [{f"in_{name}": v for name, v in arrays.items()}], core_ids=[0])
    return r.results[0]["out_x"]
```
